# Optimizing a Trainium2 kernel written in Bass

```python
import jax, jax.numpy as jnp
from jax import lax
import numpy as np

D_MODEL = 1024
BATCH = 1
SEQ = 512
DEPTH = 1

MEM_LEN = 256
D_MIX = D_MODEL
DN_HEAD_DIM = 128
DN_HEADS = (D_MIX // 2) // DN_HEAD_DIM
D_DN = DN_HEADS * DN_HEAD_DIM
D_RG = D_MIX - D_DN
RG_BLOCKS = 4
RG_BLOCK_W = D_RG // RG_BLOCKS
RG_C = 8.0
CONV_WIDTH = 4
CHUNK = 64
XA_HEADS = 4
XA_HEAD_DIM = D_MODEL // XA_HEADS
N_EXPERTS = 32
TOP_K = 4
D_FF = D_MODEL
SWIGLU_LIMIT = 7.0
SWIGLU_ALPHA = 1.702
MOE_BLOCK = 128
EPS = 1e-6

kernel_name = "hybrid_deltanet_rglru_memxattn_moe"

def rmsnorm(x, g):
    xf = x.astype(jnp.float32)
    y = xf * lax.rsqrt(jnp.mean(xf * xf, axis=-1, keepdims=True) + EPS)
    return (y * g.astype(jnp.float32)).astype(x.dtype)

def l2norm(x):
    return x * lax.rsqrt(jnp.sum(x * x, axis=-1, keepdims=True) + EPS)

def causal_dwconv(x, w):
    K, C = w.shape
    return lax.conv_general_dilated(
        x, w[:, None, :].astype(x.dtype), window_strides=(1,), padding=[(K - 1, 0)],
        dimension_numbers=('NWC', 'WIO', 'NWC'), feature_group_count=C)

def gated_delta_rule(q, k, v, g, beta):
    B, T, H, DK = q.shape
    DV = v.shape[-1]
    C = CHUNK
    N = T // C
    q = q * (DK ** -0.5)

    def chunk(t):
        return t.reshape(B, N, C, H, -1).transpose(0, 3, 1, 2, 4)

    qc, kc, vc = chunk(q), chunk(k), chunk(v)
    gc = g.reshape(B, N, C, H).transpose(0, 3, 1, 2)
    bc = beta.reshape(B, N, C, H).transpose(0, 3, 1, 2)
    gcum = jnp.cumsum(gc, axis=-1)
    causal = jnp.tril(jnp.ones((C, C), bool))
    strict = jnp.tril(jnp.ones((C, C), bool), k=-1)
    diff = gcum[..., :, None] - gcum[..., None, :]
    decay = jnp.where(causal, jnp.exp(jnp.where(causal, diff, 0.0)), 0.0)
    k_beta = kc * bc[..., None]
    A = jnp.where(strict, jnp.einsum('bhncd,bhnsd->bhncs', k_beta, kc) * decay, 0.0)
    lower = A + jnp.eye(C, dtype=A.dtype)
    rhs = jnp.concatenate([vc * bc[..., None], k_beta * jnp.exp(gcum)[..., None]], axis=-1)
    sol = lax.linalg.triangular_solve(lower, rhs, left_side=True, lower=True, unit_diagonal=True)
    u, w = sol[..., :DV], sol[..., DV:]
    qk = jnp.einsum('bhncd,bhnsd->bhncs', qc, kc) * decay

    def step(S, inp):
        q_i, k_i, u_i, w_i, qk_i, g_i = inp
        v_new = u_i - jnp.matmul(w_i, S)
        o = jnp.matmul(q_i * jnp.exp(g_i)[..., None], S) + jnp.matmul(qk_i, v_new)
        g_last = g_i[..., -1]
        k_dec = k_i * jnp.exp(g_last[..., None] - g_i)[..., None]
        S = S * jnp.exp(g_last)[..., None, None] + jnp.einsum('bhcd,bhce->bhde', k_dec, v_new)
        return S, o

    mv = lambda t: jnp.moveaxis(t, 2, 0)
    S0 = jnp.zeros((B, H, DK, DV), jnp.float32)
    _, o = lax.scan(step, S0, (mv(qc), mv(kc), mv(u), mv(w), mv(qk), mv(gcum)))
    return o.transpose(1, 0, 3, 2, 4).reshape(B, T, H, DV)

def rg_lru(xr, w_a, b_a, w_x, b_x, lam):
    B, T, _ = xr.shape
    xf = xr.astype(jnp.float32)
    xb = xf.reshape(B, T, RG_BLOCKS, RG_BLOCK_W)
    r = jax.nn.sigmoid(jnp.einsum('btni,nio->btno', xb, w_a.astype(jnp.float32)) + b_a.astype(jnp.float32))
    i = jax.nn.sigmoid(jnp.einsum('btni,nio->btno', xb, w_x.astype(jnp.float32)) + b_x.astype(jnp.float32))
    r = r.reshape(B, T, D_RG)
    i = i.reshape(B, T, D_RG)
    log_a = RG_C * r * jax.nn.log_sigmoid(lam.astype(jnp.float32))
    a = jnp.exp(log_a)
    mult = jnp.sqrt(-jnp.expm1(2.0 * log_a))
    mult = jnp.where(jnp.arange(T)[None, :, None] == 0, 1.0, mult)
    bx = mult * (i * xf)

    def combine(c1, c2):
        a1, b1 = c1
        a2, b2 = c2
        return a1 * a2, a2 * b1 + b2

    _, h = lax.associative_scan(combine, (a, bx), axis=1)
    return h

def hybrid_mixer(u, w_in, dn_conv, dn_a_log, dn_dt_bias, dn_norm, rg_conv, rg_conv_b,
                 rg_w_a, rg_b_a, rg_w_x, rg_b_x, rg_lambda, w_out):
    B, T, _ = u.shape
    proj = u @ w_in
    sizes = (D_DN, D_DN, D_DN, D_DN, DN_HEADS, DN_HEADS, D_RG, D_RG)
    cuts = [int(c) for c in np.cumsum(sizes)[:-1]]
    q, k, v, z, b, a, rx, ry = jnp.split(proj, cuts, axis=-1)

    qkv = jax.nn.silu(causal_dwconv(jnp.concatenate([q, k, v], axis=-1), dn_conv)).astype(jnp.float32)
    q, k, v = jnp.split(qkv, 3, axis=-1)
    heads = lambda t: t.reshape(B, T, DN_HEADS, DN_HEAD_DIM)
    q, k, v = l2norm(heads(q)), l2norm(heads(k)), heads(v)
    beta = jax.nn.sigmoid(b.astype(jnp.float32))
    g = -jnp.exp(dn_a_log.astype(jnp.float32)) * jax.nn.softplus(
        a.astype(jnp.float32) + dn_dt_bias.astype(jnp.float32))
    o = gated_delta_rule(q, k, v, g, beta)
    o = rmsnorm(o, dn_norm) * jax.nn.silu(heads(z.astype(jnp.float32)))
    dn_out = o.reshape(B, T, D_DN).astype(u.dtype)

    xr = causal_dwconv(rx, rg_conv) + rg_conv_b.astype(rx.dtype)
    h = rg_lru(xr, rg_w_a, rg_b_a, rg_w_x, rg_b_x, rg_lambda)
    rg_out = (h * jax.nn.gelu(ry.astype(jnp.float32))).astype(u.dtype)

    return jnp.concatenate([dn_out, rg_out], axis=-1) @ w_out

def memory_cross_attention(hn, mem_n, w_cq, w_ckv, w_co):
    B, T, D = hn.shape
    M = mem_n.shape[1]
    q = (hn @ w_cq).reshape(B, T, XA_HEADS, XA_HEAD_DIM)
    k, v = jnp.split(mem_n @ w_ckv, 2, axis=-1)
    k = k.reshape(B, M, XA_HEADS, XA_HEAD_DIM)
    v = v.reshape(B, M, XA_HEADS, XA_HEAD_DIM)
    s = jnp.einsum('bthd,bmhd->bhtm', q, k).astype(jnp.float32) * (XA_HEAD_DIM ** -0.5)
    p = jax.nn.softmax(s, axis=-1).astype(hn.dtype)
    o = jnp.einsum('bhtm,bmhd->bthd', p, v).reshape(B, T, D)
    return o @ w_co

def moe_ffn(hn, w_router, b_router, w_gate, b_gate, w_up, b_up, w_down, b_down):
    B, T, D = hn.shape
    n_tok = B * T
    xt = hn.reshape(n_tok, D)
    logits = xt.astype(jnp.float32) @ w_router.astype(jnp.float32) + b_router.astype(jnp.float32)
    top_logit, top_e = lax.top_k(logits, TOP_K)
    gate = jax.nn.softmax(top_logit, axis=-1)
    n_assign = n_tok * TOP_K
    flat_e = top_e.reshape(-1)
    order = jnp.argsort(flat_e)
    sorted_e = flat_e[order]
    sorted_tok = order // TOP_K
    sorted_gate = gate.reshape(-1)[order]
    counts = jnp.bincount(flat_e, length=N_EXPERTS)
    padded = (counts + MOE_BLOCK - 1) // MOE_BLOCK * MOE_BLOCK
    pad_end = jnp.cumsum(padded)
    pad_start = pad_end - padded
    start = jnp.cumsum(counts) - counts
    dest = pad_start[sorted_e] + jnp.arange(n_assign) - start[sorted_e]
    n_blocks = -(-n_assign // MOE_BLOCK) + N_EXPERTS
    n_rows = n_blocks * MOE_BLOCK
    row_tok = jnp.full((n_rows,), n_tok, jnp.int32).at[dest].set(sorted_tok.astype(jnp.int32))
    row_gate = jnp.zeros((n_rows,), xt.dtype).at[dest].set(sorted_gate.astype(xt.dtype))
    block_e = jnp.minimum(jnp.searchsorted(pad_end, jnp.arange(n_blocks) * MOE_BLOCK, side='right'),
                          N_EXPERTS - 1)
    x_pad = jnp.concatenate([xt, jnp.zeros((1, D), xt.dtype)], axis=0)
    xb = x_pad[row_tok].reshape(n_blocks, MOE_BLOCK, D)

    def expert_block(args):
        xblk, e = args
        gt = jnp.minimum(xblk @ w_gate[e] + b_gate[e], SWIGLU_LIMIT)
        up = jnp.clip(xblk @ w_up[e] + b_up[e], -SWIGLU_LIMIT, SWIGLU_LIMIT)
        hid = (up + 1.0) * (gt * jax.nn.sigmoid(SWIGLU_ALPHA * gt))
        return hid @ w_down[e] + b_down[e]

    yb = lax.map(expert_block, (xb, block_e))
    y = yb.reshape(n_rows, D) * row_gate[:, None]
    out = jax.ops.segment_sum(y, row_tok, num_segments=n_tok + 1)[:n_tok]
    return out.reshape(B, T, D)

def setup_inputs(seed: int = 0) -> dict:
    key = jax.random.key(seed)
    ks = jax.random.split(key, 32)
    L = DEPTH
    f32 = jnp.float32
    nrm = lambda kk, shape, scale: jax.random.normal(kk, shape, f32) * scale
    gain = lambda kk, shape: 1.0 + 0.02 * jax.random.normal(kk, shape, f32)
    d_in = 4 * D_DN + 2 * DN_HEADS + 2 * D_RG
    dt = jnp.exp(jax.random.uniform(ks[6], (L, DN_HEADS), f32, np.log(1e-3), np.log(1e-1)))
    a8 = jax.random.uniform(ks[14], (L, D_RG), f32, 0.9, 0.999)
    s = a8 ** (1.0 / RG_C)
    return {
        'x': nrm(ks[0], (BATCH, SEQ, D_MODEL), 1.0),
        'mem': nrm(ks[1], (BATCH, MEM_LEN, D_MODEL), 1.0),
        'norm_mix': gain(ks[2], (L, D_MODEL)),
        'w_in': nrm(ks[3], (L, D_MODEL, d_in), D_MODEL ** -0.5),
        'dn_conv': nrm(ks[4], (L, CONV_WIDTH, 3 * D_DN), CONV_WIDTH ** -0.5),
        'dn_a_log': jnp.log(jax.random.uniform(ks[5], (L, DN_HEADS), f32, 1.0, 16.0)),
        'dn_dt_bias': dt + jnp.log(-jnp.expm1(-dt)),
        'dn_norm': gain(ks[7], (L, DN_HEAD_DIM)),
        'rg_conv': nrm(ks[8], (L, CONV_WIDTH, D_RG), CONV_WIDTH ** -0.5),
        'rg_conv_b': nrm(ks[9], (L, D_RG), 0.01),
        'rg_w_a': nrm(ks[10], (L, RG_BLOCKS, RG_BLOCK_W, RG_BLOCK_W), RG_BLOCK_W ** -0.5),
        'rg_b_a': nrm(ks[11], (L, RG_BLOCKS, RG_BLOCK_W), 0.01),
        'rg_w_x': nrm(ks[12], (L, RG_BLOCKS, RG_BLOCK_W, RG_BLOCK_W), RG_BLOCK_W ** -0.5),
        'rg_b_x': nrm(ks[13], (L, RG_BLOCKS, RG_BLOCK_W), 0.01),
        'rg_lambda': jnp.log(s) - jnp.log1p(-s),
        'w_out': nrm(ks[15], (L, D_MIX, D_MODEL), D_MIX ** -0.5),
        'norm_cross': gain(ks[16], (L, D_MODEL)),
        'norm_mem': gain(ks[17], (L, D_MODEL)),
        'w_cq': nrm(ks[18], (L, D_MODEL, D_MODEL), D_MODEL ** -0.5),
        'w_ckv': nrm(ks[19], (L, D_MODEL, 2 * D_MODEL), D_MODEL ** -0.5),
        'w_co': nrm(ks[20], (L, D_MODEL, D_MODEL), D_MODEL ** -0.5),
        'norm_moe': gain(ks[21], (L, D_MODEL)),
        'w_router': nrm(ks[22], (L, D_MODEL, N_EXPERTS), D_MODEL ** -0.5),
        'b_router': nrm(ks[23], (L, N_EXPERTS), 0.01),
        'w_gate': nrm(ks[24], (L, N_EXPERTS, D_MODEL, D_FF), D_MODEL ** -0.5),
        'b_gate': nrm(ks[25], (L, N_EXPERTS, D_FF), 0.01),
        'w_up': nrm(ks[26], (L, N_EXPERTS, D_MODEL, D_FF), D_MODEL ** -0.5),
        'b_up': nrm(ks[27], (L, N_EXPERTS, D_FF), 0.01),
        'w_down': nrm(ks[28], (L, N_EXPERTS, D_FF, D_MODEL), D_FF ** -0.5),
        'b_down': nrm(ks[29], (L, N_EXPERTS, D_MODEL), 0.01),
        'norm_final': gain(ks[30], (D_MODEL,)),
    }

def reference(x, mem, norm_mix, w_in, dn_conv, dn_a_log, dn_dt_bias, dn_norm, rg_conv, rg_conv_b,
              rg_w_a, rg_b_a, rg_w_x, rg_b_x, rg_lambda, w_out, norm_cross, norm_mem, w_cq, w_ckv,
              w_co, norm_moe, w_router, b_router, w_gate, b_gate, w_up, b_up, w_down, b_down,
              norm_final):
    h = x
    for l in range(DEPTH):
        h = h + hybrid_mixer(rmsnorm(h, norm_mix[l]), w_in[l], dn_conv[l], dn_a_log[l], dn_dt_bias[l],
                             dn_norm[l], rg_conv[l], rg_conv_b[l], rg_w_a[l], rg_b_a[l], rg_w_x[l],
                             rg_b_x[l], rg_lambda[l], w_out[l])
        h = h + memory_cross_attention(rmsnorm(h, norm_cross[l]), rmsnorm(mem, norm_mem[l]),
                                       w_cq[l], w_ckv[l], w_co[l])
        h = h + moe_ffn(rmsnorm(h, norm_moe[l]), w_router[l], b_router[l], w_gate[l], b_gate[l],
                        w_up[l], b_up[l], w_down[l], b_down[l])
    return rmsnorm(h, norm_final)


_drawn_inputs = setup_inputs


def setup_inputs(seed=0):
    import zlib

    import numpy as np

    out = dict(_drawn_inputs(seed))
    spreads = {}
    factors = {'rg_b_a': 8.0,
     'rg_b_x': 8.0,
     'norm_cross': 5.01,
     'norm_mem': 5.355,
     'b_router': 16.064,
     'b_gate': 57.665,
     'b_up': 64.0,
     'b_down': 54.666,
     'norm_final': 7.681,
     'norm_moe': 5.551}
    for name, (base, spread) in spreads.items():
        noise = np.random.default_rng([zlib.crc32(name.encode()), seed]).standard_normal(out[name].shape)
        drawn = base * np.exp(spread * noise) if base else spread * noise
        out[name] = __import__('jax').numpy.asarray(drawn.astype(out[name].dtype))
    for name, factor in factors.items():
        out[name] = (out[name] * factor).astype(out[name].dtype)
    return out
```

```python
from contextlib import ExitStack

import concourse.bass as bass
from concourse import mybir

ALU = mybir.AluOpType
ACT = mybir.ActivationFunctionType
AX_X = mybir.AxisListType.X
F32 = mybir.dt.float32
BF16 = mybir.dt.bfloat16
I32 = mybir.dt.int32
U32 = mybir.dt.uint32

P = 128
EPS = 1e-6
GELU_C = 0.7978845608028654


def build_layer(nc, x, mem, norm_mix, w_in, dn_conv, dn_a_log, dn_dt_bias, dn_norm, rg_conv, rg_conv_b,
                rg_w_a, rg_b_a, rg_w_x, rg_b_x, rg_lambda, w_out, norm_cross, norm_mem, w_cq, w_ckv,
                w_co, norm_moe, w_router, b_router, w_gate, b_gate, w_up, b_up, w_down, b_down,
                norm_final, out):
    T, D = x.shape[1], x.shape[2]
    NT = T // P
    KT = D // P
    HALF = KT // 2
    H = dn_a_log.shape[1]
    M = mem.shape[1]
    MT = M // P
    XH = 4
    XD = D // XH
    E = w_router.shape[2]
    TOPK = 4
    N_ROW = T * TOPK
    CAP = NT
    MAXB = 48
    NOBODY = 1 << 20
    LEVELS = [1, 2, 4, 8, 16, 32, 64]
    assert D == 1024 and T == 512 and H == 4 and M == 256 and E == 32

    hn_rows = nc.dram_tensor("hn_rows", [T, D], F32, kind="Internal").ap()
    y_rows = nc.dram_tensor("y_rows", [N_ROW, D], F32, kind="Internal").ap()
    places = nc.dram_tensor("places", [(E * CAP + 1) * P, 1], I32, kind="Internal").ap()
    bias_parts = nc.dram_tensor("bias_parts", [E, 3, 3 * D], BF16, kind="Internal").ap()
    places_by_block = places.rearrange("(c p) o -> c p o", p=P)

    with ExitStack() as ctx:
        def sb(name, shape, dt=F32):
            return ctx.enter_context(nc.sbuf_tensor(name, shape, dt))

        def sem(name):
            return ctx.enter_context(nc.semaphore(name))

        ps = ctx.enter_context(nc.psum_tensor("ps", [P, 8, 512], F32))

        def quarters(bank):
            return ps[:, bank, :].rearrange("p (c f) -> p c f", c=4)

        resid = sb("resid", [P, NT, D])
        ring = sb("ring", [P, 3, KT, D])
        act_t = sb("act_t", [P, KT, T])
        xn = sb("xn", [P, 2, D])
        chan = sb("chan", [P, 24, T])
        extra = sb("extra", [P, 8, T])
        ident = sb("ident", [P, P])
        ones = sb("ones", [P, P])
        tri = sb("tri", [P, P])
        par_rows = sb("par_rows", [P, P])
        par = sb("par", [P, P])
        w_ba = sb("w_ba", [P, KT, 2 * H])
        w_rt = sb("w_rt", [P, KT, E])
        brt = sb("brt", [P, E])
        small = sb("small", [P, 320])
        ones3 = sb("ones3", [3, P], BF16)
        codes = sb("codes", [1, MAXB], I32)
        experts = sb("experts", [1, MAXB], I32)
        nblocks = sb("nblocks", [1, 1], I32)
        gates = sb("gates", [P, NT, TOPK])
        guard = sb("guard", [1, 8])
        gain_moe = sb("gain_moe", [P, KT])

        at = [0]

        def cols(n):
            at[0] += n
            assert at[0] <= 320
            return small[:, at[0] - n:at[0]]

        eps_t = cols(1)
        ss = cols(14)
        rms = cols(14)
        rstd = cols(14)
        dtb = cols(H)
        alog = cols(H)
        sp_in = cols(20)
        sp_e = cols(20)
        sp_s = cols(20)
        sp_s2 = cols(20)
        g_t = cols(16)
        beta = cols(16)
        gp = cols(16)
        egp = cols(16)
        kdf = cols(16)
        beg = cols(16)
        elast = cols(16)
        rate = cols(4)
        nrate = cols(4)
        mx = cols(8)
        nmx = cols(8)
        rsum = cols(8)
        rinv = cols(8)

        R_DCONV, R_RCONV, R_RCB, R_BA, R_BX, R_LAM, R_DN = 0, 48, 64, 68, 72, 76, 80
        R_MIX, R_CROSS, R_MEM, R_MOE, R_END = 81, 89, 97, 105, 113

        xn_flat = xn[:, :, :].rearrange("p a d -> p (a d)")
        rgw = xn_flat[:, 0:1024].rearrange("p (g n o) -> p g n o", g=2, n=4)
        lmask = xn_flat[:, 1024:1024 + 7 * P].rearrange("p (l s) -> p l s", l=7)

        tmp = ring[:, 2, :, :].rearrange("p k d -> p (k d)").rearrange("p (a f) -> p a f", f=T)
        a_m, x_m, kdec = tmp[:, 0:4], tmp[:, 4:8], tmp[:, 8:12]
        as_m, q_m = tmp[:, 12:14], tmp[:, 14:16]
        vnew, state = tmp[:, 12, :], tmp[:, 13, :]
        y_m, qkt = extra[:, 0:4], extra[:, 4:8]

        def quart(ap):
            return ap.rearrange("p (c f) -> p c f", c=4)

        cf = chan[:, :, :].rearrange("p a t -> p (a t)")
        xg, xt, hid, hid_t = cf[:, 0:D], cf[:, D:2 * D], cf[:, 2 * D:3 * D], cf[:, 3 * D:4 * D]
        gt, up, y_sb = cf[:, 4 * D:5 * D], cf[:, 5 * D:6 * D], cf[:, 6 * D:7 * D]
        sig_e = cf[:, 7 * D:8 * D]
        bias3 = cf[:, 8 * D:8 * D + 3 * D // 2].bitcast(BF16)
        nf_b = cf[:, 10 * D:11 * D]
        idx = sb("idx", [P, 4], I32)

        x_in = [sem(f"x_in{t}") for t in range(NT)]
        w_in_slot = [sem(f"w_in_slot{i}") for i in range(6)]
        par_in, ba_in, rgw_in, small_in, bias_in = (sem(n) for n in ("par_in", "ba_in", "rgw_in", "small_in", "bias_in"))
        consts_ready, par_clear = sem("consts_ready"), sem("par_clear")
        par_t, par_ready = sem("par_t"), sem("par_ready")
        xn_ready, tr_done, tr_evac = sem("xn_ready"), sem("tr_done"), sem("tr_evac")
        stat_ready, rstd_ready = sem("stat_ready"), sem("rstd_ready")
        dve_c, act_c, pool_c = sem("dve_chain"), sem("act_chain"), sem("pool_chain")
        ba_done, g_ready, gp_done, gp_ready = sem("ba_done"), sem("g_ready"), sem("gp_done"), sem("gp_ready")
        exp_small, beta_ready, sp_ready = sem("exp_small"), sem("beta_ready"), sem("sp_ready")
        proj_done, tap_ready, tile_done, sig_ready, silu_done = (sem(n) for n in ("proj_done", "tap_ready", "tile_done", "sig_ready", "silu_done"))
        sq_ready, l2_done, l2_evac, norm_ready, qk_ready = (sem(n) for n in ("sq_ready", "l2_done", "l2_evac", "norm_ready", "qk_ready"))
        y2_ready, yt_ready, tanh_ready = sem("y2_ready"), sem("yt_ready"), sem("tanh_ready")
        gate_mm, ri_ready, bx_ready, rt_ready, mult_in, mult_ready, rg_done = (sem(n) for n in ("gate_mm", "ri_ready", "bx_ready", "rt_ready", "mult_in", "mult_ready", "rg_done"))
        masks_ready = sem("masks_ready")
        gu_ready, gb_done, d_ready, split_ready, decay_ready, masked_ready = (sem(n) for n in ("gu_ready", "gb_done", "d_ready", "split_ready", "decay_ready", "masked_ready"))
        kk_done, kk_evac, qexp_ready, kd_in, kdf_ready = (sem(n) for n in ("kk_done", "kk_evac", "qexp_ready", "kd_in", "kdf_ready"))
        x1_ready, x1t_done, y1_ready = sem("x1_ready"), sem("x1t_done"), sem("y1_ready")
        as_ready, qm_done, qm_ready, p_done, y_lev, x_lev = (sem(n) for n in ("as_ready", "qm_done", "qm_ready", "p_done", "y_lev", "x_lev"))
        wt_done, wt_ready = sem("wt_done"), sem("wt_ready")
        vn_done, vn_ready, s_done, s_ready, o_done = (sem(n) for n in ("vn_done", "vn_ready", "s_done", "s_ready", "o_done"))
        osq_ready, oss_done, orms_ready, onorm_ready, dn_done = (sem(n) for n in ("osq_ready", "oss_done", "orms_ready", "onorm_ready", "dn_done"))
        out_mm, h1_ready = sem("out_mm"), sem("h1_ready")
        mem_in, mk_mm, mk_evac = sem("mem_in"), sem("mk_mm"), sem("mk_evac")
        q_mm, q_evac = sem("q_mm"), sem("q_evac")
        sc_mm, mx_ready, ex_ready, p_ready, pt_mm, pt_evac = (sem(n) for n in ("sc_mm", "mx_ready", "ex_ready", "p_ready", "pt_mm", "pt_evac"))
        o_mm, o_evac, co_mm, h2_ready = sem("o_mm"), sem("o_evac"), sem("co_mm"), sem("h2_ready")
        hn_out = [sem(f"hn_out{i}") for i in range(2)]
        lg_mm, lg_ready, top_ready, gexp_ready, oh_ready, pos_mm, slot_ready = (sem(n) for n in ("lg_mm", "lg_ready", "top_ready", "gexp_ready", "oh_ready", "pos_mm", "slot_ready"))
        codes_ready, places_init, placed, iota_ready = (sem(n) for n in ("codes_ready", "places_init", "placed", "iota_ready"))
        bias_split, bias_out = sem("bias_split"), sem("bias_out")
        xg_clear, idx_in, tok_ready, xg_in, xgt_done, xt_ready = (sem(n) for n in ("xg_clear", "idx_in", "tok_ready", "xg_in", "xgt_done", "xt_ready"))
        bias3_in = sem("bias3_in")
        gate_done, up_done, gt_ready, sg_ready, hid_ready, hidt_done, hidt_ready = (sem(n) for n in ("gate_done", "up_done", "gt_ready", "sg_ready", "hid_ready", "hidt_done", "hidt_ready"))
        down_done, y_ready, y_out = sem("down_done"), sem("y_ready"), sem("y_out")
        y_in = [sem(f"y_in{t}") for t in range(NT)]
        comb_ready, nf_in, fin_ready, out_sent = sem("comb_ready"), sem("nf_in"), sem("fin_ready"), sem("out_sent")
        stood, gate_half, down_half, gs_ready, up_ready, row_in, tail_c = (sem(n) for n in ("stood", "gate_half", "down_half", "gs_ready", "up_ready", "row_in", "tail_c"))

        block = ctx.enter_context(nc.Block())

        def front(w, c0):
            v = w[0].rearrange("(h k p) n -> h p k n", h=2, p=P)
            return [v[h, :, :, c0:c0 + D] for h in range(2)]

        C_BA = 4 * H * P
        FRONT = [front(w_in, 0), front(w_in, D), front(w_in, C_BA + 2 * H),
                 front(w_out, 0), front(w_ckv, 0), front(w_ckv, D), front(w_cq, 0), front(w_co, 0)]
        NF = len(FRONT)
        W_QK, W_VZ, W_RXY, W_OUT, W_CK, W_CV, W_CQ, W_CO = range(NF)
        USED = [(proj_done, 8), (proj_done, 16), (proj_done, 24), (out_mm, 8), (mk_mm, 8), (mk_mm, 12), (q_mm, 8), (co_mm, 8)]

        def slot_w(m, k):
            return ring[:, m % 3, k, :]

        expert_w = [w[0].rearrange("e (h p k) n -> e h p k n", h=2, p=P) for w in (w_gate, w_up, w_down)]

        GM = NF % 3

        @block.sync
        def _(sp):
            for t in range(NT):
                sp.dma_start(resid[:, t, :], x[0, t * P:(t + 1) * P, :]).then_inc(x_in[t], 16)
            for m in range(NF):
                if m == W_CV:
                    sp.wait_ge(dn_done, H)
                    sp.dma_start(chan[:, 0:4, :].rearrange("p a t -> p (a t)").rearrange("p (m d) -> p m d", m=MT),
                                 mem[0].rearrange("(m p) d -> p m d", p=P)).then_inc(mem_in, 16)
                if m >= 3:
                    sp.wait_ge(*USED[m - 3])
                for h in range(2):
                    s = 2 * (m % 3) + h
                    sp.dma_start(ring[:, m % 3, HALF * h:HALF * (h + 1), :], FRONT[m][h]).then_inc(w_in_slot[s], 16)
                if m == W_RXY:
                    sp.wait_ge(tr_evac, 2 * NT)
                    sp.dma_start(rgw[:, 0], rg_w_a[0].rearrange("n i o -> i n o")).then_inc(rgw_in, 16)
                    sp.dma_start(rgw[:, 1], rg_w_x[0].rearrange("n i o -> i n o")).then_inc(rgw_in, 16)

            for j in range(3):
                sp.wait_ge(*USED[NF + j - 3])
                for h in range(2):
                    sp.dma_start(ring[:, (GM + j) % 3, HALF * h:HALF * (h + 1), :],
                                 expert_w[j][0, h]).then_inc(w_in_slot[2 * ((GM + j) % 3) + h], 16)
            sp.wait_ge(bias_out, 16)
            sp.wait_ge(h2_ready, 8)
            sp.dma_start(bias3[0:3, :], bias_parts[0]).then_inc(bias3_in, 16)
            sp.dma_start(nf_b, norm_final.rearrange("(o d) -> o d", o=1).to_broadcast([P, D])).then_inc(nf_in, 16)
            sp.wait_ge(codes_ready, 1)
            n_blocks = sp.value_load(nblocks[0:1, 0:1], min_val=E, max_val=MAXB - 1)
            freed = [[(gate_half, 1), (gate_done, 1)], [(up_done, 2), (up_done, 2)], [(down_half, 1), (down_done, 2)]]
            with sp.Fori(1, n_blocks) as n:
                e = sp.value_load(experts[0:1, bass.ds(n, 1)], min_val=0, max_val=E - 1)
                for j in range(3):
                    for h in range(2):
                        done, per = freed[j][h]
                        sp.wait_ge(done, n * per)
                        sp.dma_start(ring[:, (GM + j) % 3, HALF * h:HALF * (h + 1), :],
                                     expert_w[j][bass.ds(e, 1), h].rearrange("o p k n -> (o p) k n"))\
                            .then_inc(w_in_slot[2 * ((GM + j) % 3) + h], 16)
                sp.dma_start(bias3[0:3, :], bias_parts[bass.ds(e, 1)].rearrange("o a b -> (o a) b")).then_inc(bias3_in, 16)
            sp.wait_ge(y_out, n_blocks * 16)
            y_tok = y_rows.rearrange("(t p k) d -> t p k d", p=P, k=TOPK)
            for t in range(NT):
                sp.dma_start(ring[:, :, :, :].rearrange("p a k d -> p (a k) d")[:, 4 * t:4 * t + 4, :], y_tok[t]).then_inc(y_in[t], 16)
            for t in range(NT):
                sp.wait_ge(fin_ready, t + 1)
                sp.dma_start(out[0, t * P:(t + 1) * P, :], resid[:, t, :]).then_inc(out_sent, 16)
            sp.wait_ge(out_sent, 16 * NT)

        @block.gpsimd
        def _(pool):
            chain = [0]

            def link(ins):
                chain[0] += 1
                ins.then_inc(pool_c, 1)
                pool.wait_ge(pool_c, chain[0])

            link(pool.memset(ones[:], 1.0))
            link(pool.memset(ident[:], 0.0))
            pool.affine_select(out=ident[:], in_=ident[:], compare_op=ALU.not_equal, fill=1.0, base=0,
                               pattern=[[-1, P]], channel_multiplier=1).then_inc(consts_ready, 1)
            pool.affine_select(out=tri[:], in_=ones[:], compare_op=ALU.is_ge, fill=0.0, base=0,
                               pattern=[[1, P]], channel_multiplier=-1).then_inc(consts_ready, 1)
            pool.memset(ones3[:], 1.0).then_inc(consts_ready, 1)
            pool.memset(guard[:], 0.0).then_inc(stood, 1)
            nobody = act_t[:, 0, 0:E * CAP + 1].bitcast(I32)
            link(pool.memset(nobody, NOBODY))
            pool.dma_start(places.rearrange("(p c) o -> p (c o)", p=P), nobody).then_inc(places_init, 16)

            b_f = extra[0:E, 0:6, :].rearrange("p a t -> p (a t)")
            parts = chan[0:E, 15:24, :].rearrange("p a t -> p (a t)").bitcast(BF16).rearrange("p (s f) -> p s f", s=3)
            pool.wait_ge(bias_in, 48)
            link(pool.tensor_copy(parts[:, 0], b_f))
            link(pool.tensor_tensor(b_f, b_f, parts[:, 0], ALU.subtract))
            link(pool.tensor_copy(parts[:, 1], b_f))
            link(pool.tensor_tensor(b_f, b_f, parts[:, 1], ALU.subtract))
            link(pool.tensor_copy(parts[:, 2], b_f))
            pool.dma_start(bias_parts, parts).then_inc(bias_out, 16)

            pool.wait_ge(tr_evac, 2 * NT)
            for l, w in enumerate(LEVELS):
                nb = P // (2 * w)
                v = lmask[:, l, :].rearrange("p (b j) -> p b j", b=nb)
                src = ones[:, :].rearrange("p (b j) -> p b j", b=nb)
                link(pool.affine_select(out=v, in_=src, compare_op=ALU.is_ge, fill=0.0, base=-w,
                                        pattern=[[-2 * w, nb], [0, 2 * w]], channel_multiplier=1))
                link(pool.affine_select(out=v, in_=v, compare_op=ALU.is_ge, fill=0.0, base=2 * w - 1,
                                        pattern=[[2 * w, nb], [0, 2 * w]], channel_multiplier=-1))
                link(pool.affine_select(out=v, in_=v, compare_op=ALU.is_ge, fill=0.0, base=w - 1,
                                        pattern=[[0, nb], [-1, 2 * w]], channel_multiplier=0))

            for j in range(12):
                pool.wait_ge(sig_ready, j + 1)
                pool.tensor_tensor(chan[:, j], chan[:, j], extra[:, 4 + j % 2], ALU.mult).then_inc(silu_done, 1)

            for n in range(4):
                pool.wait_ge(ri_ready, 2 * n + 2)
                pool.tensor_tensor(chan[:, 16 + n], chan[:, 16 + n], act_t[:, 4 + n], ALU.mult).then_inc(bx_ready, 1)

            for h in range(H):
                pool.wait_ge(d_ready, h + 1)
                link(pool.tensor_scalar(qkt[:, h], a_m[:, h], 0.0, None, ALU.min))
                pool.tensor_scalar(a_m[:, h], a_m[:, h], 0.0, None, ALU.max).then_inc(split_ready, 1)
            for h in range(H):
                pool.wait_ge(decay_ready, 3 * h + 2)
                link(pool.affine_select(out=quart(a_m[:, h]), in_=quart(a_m[:, h]), compare_op=ALU.is_ge, fill=0.0,
                                        base=-1, pattern=[[0, 4], [-1, P]], channel_multiplier=1))
                link(pool.tensor_tensor(quart(a_m[:, h]), quart(a_m[:, h]),
                                        beta[:, 4 * h:4 * h + 4].unsqueeze(2).to_broadcast([P, 4, P]), ALU.mult))
                pool.affine_select(out=quart(qkt[:, h]), in_=quart(qkt[:, h]), compare_op=ALU.is_ge, fill=0.0,
                                   base=0, pattern=[[0, 4], [1, P]], channel_multiplier=-1).then_inc(masked_ready, 1)
                pool.wait_ge(decay_ready, 3 * h + 3)
                pool.wait_ge(kk_done, 4 * h + 2)
                link(pool.tensor_tensor(chan[:, h], chan[:, h], q_m[:, h % 2], ALU.mult))
                pool.tensor_copy(elast[:, 4 * h:4 * h + 4].unsqueeze(2), quart(q_m[:, h % 2])[:, :, P - 1:P]).then_inc(qexp_ready, 1)

            pool.wait_ge(kk_evac, 4 * H)
            for l in range(7):
                for h in range(H):
                    i = 4 * l + h
                    if l == 0 and h >= 2:
                        pool.wait_ge(x1_ready, h - 1)
                    if l > 0:
                        if i - 4 >= 2:
                            pool.wait_ge(qm_done, i - 5)
                        else:
                            pool.wait_ge(x1_ready, H)
                    pool.tensor_tensor(quart(as_m[:, i % 2]), quart(a_m[:, h]),
                                       lmask[:, l:l + 1, :].to_broadcast([P, 4, P]), ALU.mult).then_inc(as_ready, 1)

            for h in range(H):
                pool.wait_ge(onorm_ready, h + 1)
                link(pool.tensor_scalar(q_m[:, h % 2], q_m[:, h % 2], par[:, R_DN:R_DN + 1], None, ALU.mult))
                pool.tensor_tensor(chan[:, 12 + h], chan[:, 12 + h], q_m[:, h % 2], ALU.mult).then_inc(dn_done, 1)

            pool.wait_ge(co_mm, 1)
            it_i = extra[:, 0, :].bitcast(I32)
            ef = extra[:, 1, :]
            link(pool.iota(it_i[:, 0:E], pattern=[[1, E]], base=0, channel_multiplier=0))
            link(pool.iota(it_i[:, 64:80], pattern=[[4 * P, 4], [1, 4]], base=0, channel_multiplier=4))
            link(pool.iota(it_i[:, 96:99], pattern=[[P, 3]], base=P, channel_multiplier=0))
            link(pool.iota(it_i[:, 128:224], pattern=[[4, E], [1, 3]], base=1 - E * CAP, channel_multiplier=0))
            link(pool.iota(it_i[:, 224:240], pattern=[[1, 16]], base=0, channel_multiplier=0))
            link(pool.tensor_copy(ef[:, 0:E], it_i[:, 0:E]))
            link(pool.tensor_scalar(ef[:, 32:64], ef[:, 0:E], float(CAP * P), None, ALU.mult))
            link(pool.tensor_copy(ef[:, 96:99], it_i[:, 96:99]))
            link(pool.tensor_copy(ef[:, 128:240], it_i[:, 128:240]))
            link(pool.affine_select(out=extra[:, 2, 0:P], in_=ones[:], compare_op=ALU.is_ge, fill=0.0, base=-1,
                                    pattern=[[1, P]], channel_multiplier=-1))
            pool.iota(codes[0:1, 0:E], pattern=[[CAP, E]], base=0, channel_multiplier=0).then_inc(iota_ready, 1)
            pool.memset(xg, 0.0).then_inc(xg_clear, 1)

            pool.wait_ge(places_init, 16)
            pool.wait_ge(slot_ready, 1)
            for c in range(NT * TOPK):
                pool.indirect_dma_start(out=places, out_offset=bass.IndirectOffsetOnAxis(ap=it_i[:, 256 + c:257 + c], axis=0),
                                        in_=it_i[:, 64 + c:65 + c], in_offset=None,
                                        bounds_check=E * CAP * P - 1, oob_is_err=False).then_inc(placed, 16)
            pool.wait_ge(xg_clear, 1)
            pool.wait_ge(placed, 16 * NT * TOPK)
            pool.wait_ge(hn_out[0], 16 * (NT // 2))
            pool.wait_ge(hn_out[1], 16 * (NT // 2))
            pool.wait_ge(codes_ready, 1)

            def stand(i):
                return pool.tensor_tensor(guard[:, i:i + 1], guard[:, 0:1], guard[:, 0:1], ALU.mult)

            def gather():
                pool.indirect_dma_start(out=xg, out_offset=None, in_=hn_rows,
                                        in_offset=bass.IndirectOffsetOnAxis(ap=idx[:, 1:2], axis=0),
                                        bounds_check=T - 1, oob_is_err=False).then_inc(xg_in, 16)

            pool.dma_start(idx[:, 0:1], places_by_block[0]).then_inc(idx_in, 16)
            pool.dma_start(idx[:, 2:3], places_by_block[0]).then_inc(row_in, 16)
            pool.wait_ge(tok_ready, 1)
            gather()
            n_blocks = pool.value_load(nblocks[0:1, 0:1], min_val=E, max_val=MAXB - 1)
            with pool.Fori(0, n_blocks) as n:
                c = pool.value_load(codes[0:1, bass.ds(n + 1, 1)], min_val=0, max_val=E * CAP)
                next_places = places_by_block[bass.ds(c, 1)].rearrange("c p o -> (c p) o")
                pool.dma_start(idx[:, 0:1], next_places).then_inc(idx_in, 16)
                pool.wait_ge(stood, n + 1)
                pool.wait_ge(tok_ready, n + 2)
                stand(1)
                pool.wait_ge(xgt_done, n + 1)
                stand(2)
                gather()
                pool.wait_ge(y_ready, n * 2 + 2)
                stand(3)
                pool.wait_ge(row_in, n * 16 + 16)
                stand(4)
                pool.indirect_dma_start(out=y_rows, out_offset=bass.IndirectOffsetOnAxis(ap=idx[:, 2:3], axis=0),
                                        in_=y_sb, in_offset=None, bounds_check=N_ROW - 1,
                                        oob_is_err=False).then_inc(y_out, 16)
                pool.wait_ge(y_out, n * 16 + 16)
                stand(5).then_inc(stood, 1)
                pool.dma_start(idx[:, 2:3], next_places).then_inc(row_in, 16)

        @block.scalar
        def _(act):
            chain = [0]

            def link(ins):
                chain[0] += 1
                ins.then_inc(act_c, 1)
                act.wait_ge(act_c, chain[0])

            act.wait_ge(par_clear, 1)

            def row(dst, src):
                act.dma_start(par_rows[dst:dst + src.shape[0], :], src).then_inc(par_in, 16)

            row(R_DCONV, dn_conv[0].rearrange("k (j p) -> (k j) p", p=P))
            row(R_RCONV, rg_conv[0].rearrange("k (j p) -> (k j) p", p=P))
            row(R_RCB, rg_conv_b[0].rearrange("(j p) -> j p", p=P))
            row(R_BA, rg_b_a[0])
            row(R_BX, rg_b_x[0])
            row(R_LAM, rg_lambda[0].rearrange("(j p) -> j p", p=P))
            row(R_DN, dn_norm)
            row(R_MIX, norm_mix[0].rearrange("(j p) -> j p", p=P))
            row(R_CROSS, norm_cross[0].rearrange("(j p) -> j p", p=P))
            row(R_MEM, norm_mem[0].rearrange("(j p) -> j p", p=P))
            row(R_MOE, norm_moe[0].rearrange("(j p) -> j p", p=P))
            act.dma_start(w_ba[:], w_in[0].rearrange("(k p) n -> p k n", p=P)[:, :, C_BA:C_BA + 2 * H]).then_inc(ba_in, 16)
            act.dma_start(dtb, dn_dt_bias.to_broadcast([P, H])).then_inc(small_in, 16)
            act.dma_start(alog, dn_a_log.to_broadcast([P, H])).then_inc(small_in, 16)
            act.dma_start(brt[:], b_router.to_broadcast([P, E])).then_inc(small_in, 16)
            act.dma_start(w_rt[:], w_router[0].rearrange("(k p) n -> p k n", p=P)).then_inc(small_in, 16)
            act.dma_start(gain_moe[:].rearrange("p (h k) -> p h k", h=2),
                          norm_moe[0].rearrange("(h p k) -> p h k", h=2, p=P)).then_inc(small_in, 16)
            for i, b in enumerate((b_gate, b_up, b_down)):
                act.dma_start(extra[0:E, 2 * i:2 * i + 2, :].rearrange("p a t -> p (a t)"), b[0]).then_inc(bias_in, 16)

            def norm_rows(src, s, waits=()):
                for w in waits:
                    act.wait_ge(*w)
                if s >= 2:
                    act.wait_ge(tr_done, 2 * (s - 1))
                link(act.activation(xn[:, s % 2], src, ACT.Square, accum_out=ss[:, s:s + 1]))
                act.activation(rms[:, s:s + 1], ss[:, s:s + 1], ACT.Sqrt, scale=1.0 / D, bias=eps_t).then_inc(stat_ready, 1)
                act.wait_ge(rstd_ready, s + 1)
                act.activation(xn[:, s % 2], src, ACT.Copy, scale=rstd[:, s:s + 1]).then_inc(xn_ready, 1)

            act.wait_ge(par_clear, 2)
            for t in range(NT):
                norm_rows(resid[:, t], t, [(x_in[t], 16)])

            act.wait_ge(sp_ready, 1)
            act.activation(sp_e, sp_s, ACT.Exp, scale=-1.0).then_inc(exp_small, 1)
            act.wait_ge(small_in, 16 * 5)
            act.activation(alog, alog, ACT.Exp).then_inc(exp_small, 1)
            act.wait_ge(sp_ready, 2)
            act.activation(beta, beta, ACT.Sigmoid).then_inc(beta_ready, 1)

            def tap(j, r, nj, bias):
                act.wait_ge(proj_done, j + 1)
                c = r + 3 * nj + (j if nj == 12 else j - 16)
                w3 = par[:, c:c + 1]
                if bias is None:
                    act.activation(chan[:, j], ps[:, j % 6], ACT.Copy, scale=w3).then_inc(tap_ready, 1)
                else:
                    act.activation(chan[:, j], ps[:, j % 6], ACT.Identity, scale=w3, bias=bias).then_inc(tap_ready, 1)

            def sigmoid_of(j):
                act.wait_ge(tile_done, j + 1)
                if j >= 2:
                    act.wait_ge(silu_done, j - 1)
                act.activation(extra[:, 4 + j % 2], chan[:, j], ACT.Sigmoid).then_inc(sig_ready, 1)

            def square_of(j):
                act.wait_ge(silu_done, j + 1)
                if j == 0:
                    act.wait_ge(bias_out, 16)
                act.activation(chan[:, 16 + j], chan[:, j], ACT.Square).then_inc(sq_ready, 1)

            def sums_of(j):
                act.wait_ge(l2_done, j + 1)
                act.activation(chan[:, 16 + j], ps[:, 6 + j % 2], ACT.Copy).then_inc(l2_evac, 1)

            for j in range(24):
                if j < 12:
                    if j == 0:
                        act.wait_ge(par_ready, 1)
                    tap(j, R_DCONV, 12, None)
                if 1 <= j <= 12:
                    if j == 1:
                        act.wait_ge(bias_out, 16)
                    sigmoid_of(j - 1)
                if 12 <= j < 16:
                    act.wait_ge(proj_done, j + 1)
                    act.wait_ge(silu_done, min(j - 1, 12))
                    if j - 2 >= 12:
                        act.wait_ge(tile_done, j - 1)
                    act.activation(extra[:, 4 + j % 2], ps[:, j % 6], ACT.Sigmoid).then_inc(sig_ready, 1)
                if j == 16:
                    act.wait_ge(l2_evac, 8)
                    act.activation(chan[:, 16:20], chan[:, 16:20], ACT.Sqrt, scale=float(P), bias=sp_in[:, 0:1]).then_inc(norm_ready, 1)
                    act.activation(chan[:, 20:24], chan[:, 20:24], ACT.Sqrt, bias=eps_t).then_inc(norm_ready, 1)
                if 16 <= j < 20:
                    act.wait_ge(qk_ready, 2)
                    tap(j, R_RCONV, 4, par[:, R_RCB + j - 16:R_RCB + j - 15])
                if j >= 20:
                    act.wait_ge(proj_done, j + 1)
                    if j >= 22:
                        act.wait_ge(tile_done, j - 1)
                    act.activation(extra[:, 6 + j % 2], ps[:, j % 6], ACT.Square).then_inc(y2_ready, 1)
                    act.wait_ge(yt_ready, j - 19)
                    act.activation(extra[:, 6 + j % 2], extra[:, 6 + j % 2], ACT.Tanh, scale=GELU_C).then_inc(tanh_ready, 1)
                if 2 <= j < 10:
                    square_of(j - 2)
                if 6 <= j < 14:
                    sums_of(j - 6)

            act.wait_ge(proj_done, 24)
            for n in range(4):
                for g in range(2):
                    act.wait_ge(gate_mm, 2 * n + g + 1)
                    r = (R_BA if g == 0 else R_BX) + n
                    act.activation(act_t[:, 4 * g + n], ps[:, 6 + g], ACT.Sigmoid, bias=par[:, r:r + 1]).then_inc(ri_ready, 1)
            act.wait_ge(ri_ready, 8)
            for n in range(4):
                act.wait_ge(bx_ready, n + 1)
                act.activation(act_t[:, 4 + n], act_t[:, n], ACT.Tanh, scale=nrate[:, n:n + 1]).then_inc(rt_ready, 1)
            act.wait_ge(rt_ready, 4)
            for n in range(4):
                act.activation(act_t[:, n], act_t[:, n], ACT.Exp, scale=rate[:, n:n + 1]).then_inc(rt_ready, 1)

            act.wait_ge(gp_ready, 1)
            act.activation(egp, gp, ACT.Exp).then_inc(kdf_ready, 1)
            for h in range(H):
                act.wait_ge(split_ready, h + 1)
                act.activation(a_m[:, h], a_m[:, h], ACT.Exp, scale=-1.0).then_inc(decay_ready, 1)
                act.activation(qkt[:, h], qkt[:, h], ACT.Exp).then_inc(decay_ready, 1)
                act.wait_ge(kd_in, h + 1)
                if h >= 2:
                    act.wait_ge(qexp_ready, h - 1)
                act.activation(q_m[:, h % 2], ps[:, h], ACT.Exp).then_inc(decay_ready, 1)
                if h == 1:
                    act.wait_ge(kd_in, H)
                    act.activation(kdf, kdf, ACT.Exp).then_inc(kdf_ready, 1)
                    act.wait_ge(mult_in, 1)
                    act.activation(act_t[:, 4:8], act_t[:, 4:8], ACT.Sqrt, scale=2.0).then_inc(mult_ready, 1)

            for h in range(H):
                act.wait_ge(x1t_done, h + 1)
                if h == 0:
                    act.wait_ge(rg_done, 1)
                act.activation(y_m[:, h], ps[:, h], ACT.Copy).then_inc(y1_ready, 1)
            for i in range(24):
                act.wait_ge(qm_done, i + 1)
                if i >= 2:
                    act.wait_ge(p_done, i - 1)
                else:
                    act.wait_ge(qexp_ready, H)
                act.activation(q_m[:, i % 2], ps[:, 3 * (i % 2)], ACT.Copy).then_inc(qm_ready, 1)
            for h in range(H):
                act.wait_ge(wt_done, h + 1)
                act.activation(chan[:, 4 + h], ps[:, 6 + h % 2], ACT.Copy, scale=-1.0).then_inc(wt_ready, 1)
            for c in range(NT):
                for h in range(H):
                    act.wait_ge(vn_done, 4 * c + h + 1)
                    if c > 0:
                        act.wait_ge(o_done, 4 * (c - 1) + h + 1)
                    act.activation(vnew[:, h * P:(h + 1) * P], ps[:, h % 2, 0:P], ACT.Copy).then_inc(vn_ready, 1)
            for h in range(H):
                act.wait_ge(o_done, 4 * (NT - 1) + h + 1)
                if h >= 2:
                    act.wait_ge(dn_done, h - 1)
                act.activation(q_m[:, h % 2], ps[:, 4 + h], ACT.Square).then_inc(osq_ready, 1)
                act.wait_ge(oss_done, h + 1)
                act.activation(q_m[:, h % 2], ps[:, h % 2], ACT.Sqrt, scale=1.0 / P, bias=eps_t).then_inc(orms_ready, 1)

            s = NT
            memf = chan[:, 0:4, :].rearrange("p a t -> p (a t)").rearrange("p (m d) -> p m d", m=MT)
            for m in range(MT):
                norm_rows(memf[:, m], s, [(mem_in, 16)] + ([(dn_done, H)] if m == 0 else []))
                s += 1
            for i in range(8):
                act.wait_ge(mk_mm, i + 1)
                act.activation(extra[:, 0:4, :].rearrange("p a t -> p (a t)")[:, i * M:(i + 1) * M], ps[:, i % 4, 0:M], ACT.Copy).then_inc(mk_evac, 1)
            for i in range(4):
                act.wait_ge(mk_mm, 9 + i)
                act.activation(extra[:, 4 + i], ps[:, i % 4], ACT.Copy).then_inc(mk_evac, 1)
            for t in range(NT):
                norm_rows(resid[:, t], s, [(h1_ready, 2 * t + 2)])
                s += 1
            for i in range(8):
                act.wait_ge(q_mm, i + 1)
                act.activation(chan[:, i], ps[:, i % 4], ACT.Copy).then_inc(q_evac, 1)
            def pt_copies(t):
                for b in range(2):
                    act.wait_ge(pt_mm, 2 * t + b + 1)
                    act.activation(chan[:, 8 + 4 * b:12 + 4 * b, t * P:(t + 1) * P], quarters(4 + b), ACT.Copy).then_inc(pt_evac, 1)

            for t in range(NT):
                act.wait_ge(mx_ready, t + 1)
                if t >= 2:
                    act.wait_ge(pt_mm, 2 * (t - 1))
                pr = xn[:, t % 2].rearrange("p (h m) -> p h m", h=XH)
                scv = ps[:, 2 * (t % 2):2 * (t % 2) + 2, :].rearrange("p b (g m) -> p (b g) m", g=2)
                for h in range(XH):
                    c = 4 * (t % 2) + h
                    act.activation(pr[:, h], scv[:, h], ACT.Exp, scale=XD ** -0.5, bias=nmx[:, c:c + 1],
                                   accum_out=rsum[:, c:c + 1]).then_inc(ex_ready, 1)
                if t >= 1:
                    pt_copies(t - 1)
            pt_copies(NT - 1)
            for i in range(8):
                act.wait_ge(o_mm, i + 1)
                act.activation(chan[:, 16 + i], ps[:, 6 + i % 2], ACT.Copy).then_inc(o_evac, 1)
            for t in range(NT):
                norm_rows(resid[:, t], s, [(h2_ready, 2 * t + 2)] + ([(hn_out[s % 2], 16 * (t // 2))] if t >= 2 else []))
                act.wait_ge(xn_ready, s + 1)
                act.dma_start(hn_rows[t * P:(t + 1) * P, :], xn[:, s % 2]).then_inc(hn_out[s % 2], 16)
                s += 1
            act.wait_ge(top_ready, 1)
            act.activation(gates[:], gates[:], ACT.Exp).then_inc(gexp_ready, 1)

            act.wait_ge(codes_ready, 1)
            n_blocks = act.value_load(nblocks[0:1, 0:1], min_val=E, max_val=MAXB - 1)
            with act.Fori(0, n_blocks) as n:
                act.wait_ge(gt_ready, n + 1)
                act.activation(sig_e, gt, ACT.Sigmoid, scale=1.702).then_inc(sg_ready, 1)
                act.wait_ge(row_in, n * 16 + 16)
                for i in range(2):
                    act.wait_ge(down_done, n * 2 + (i + 1))
                    act.activation(y_sb[:, i * 512:(i + 1) * 512], ps[:, 4 + i], ACT.Copy).then_inc(y_ready, 1)
            for t in range(NT):
                act.wait_ge(comb_ready, t + 1)
                if t >= 2:
                    act.wait_ge(stat_ready, 14 + t - 1)
                act.activation(xn[:, t % 2], resid[:, t], ACT.Square, accum_out=ss[:, t:t + 1]).then_inc(stat_ready, 1)
            act.wait_ge(stat_ready, 14 + NT)
            act.activation(rms[:, 0:4], ss[:, 0:4], ACT.Sqrt, scale=1.0 / D, bias=eps_t).then_inc(stat_ready, 1)

        @block.tensor
        def _(pe):
            pe.wait_ge(consts_ready, 3)
            pe.wait_ge(par_in, 16 * 11)
            pe.transpose(ps[:, 7, 0:P], par_rows[:], ident[:]).then_inc(par_t, 1)

            def transposes(s):
                pe.wait_ge(xn_ready, s + 1)
                for b in range(2):
                    bank = 2 * (s % 2) + 4 + b
                    if s >= 2:
                        pe.wait_ge(tr_evac, 2 * (s - 2) + b + 1)
                    elif s == 1:
                        pe.wait_ge(par_ready, 1)
                    for k in range(4):
                        last = pe.transpose(quarters(bank)[:, k], xn[:, s % 2, (4 * b + k) * P:(4 * b + k + 1) * P], ident[:])
                    last.then_inc(tr_done, 1)

            for t in range(NT):
                transposes(t)
            pe.wait_ge(tr_evac, 2 * NT)
            pe.wait_ge(ba_in, 16)
            for t in range(NT):
                for k in range(KT):
                    last = pe.matmul(ps[:, 7, 8 * t:8 * t + 8], act_t[:, k, t * P:(t + 1) * P], w_ba[:, k], start=(k == 0), stop=(k == KT - 1))
            last.then_inc(ba_done, 1)

            for j in range(24):
                m, c = j // 8, j % 8
                if c == 0:
                    pe.wait_ge(w_in_slot[2 * (m % 3)], 16 * (m // 3 + 1))
                    pe.wait_ge(w_in_slot[2 * (m % 3) + 1], 16 * (m // 3 + 1))
                if j >= 6:
                    pe.wait_ge(tile_done, j - 5)
                for k in range(KT):
                    last = pe.matmul(ps[:, j % 6], slot_w(m, k)[:, c * P:(c + 1) * P], act_t[:, k], start=(k == 0), stop=(k == KT - 1))
                last.then_inc(proj_done, 1)
                if j == 2:
                    pe.wait_ge(g_ready, 1)
                    pe.matmul(ps[:, 7, 64:80], tri[:], g_t, start=True, stop=True).then_inc(gp_done, 1)
                if 5 <= j < 13:
                    i = j - 5
                    pe.wait_ge(sq_ready, i + 1)
                    if i >= 2:
                        pe.wait_ge(l2_evac, i - 1)
                    elif i == 1:
                        pe.wait_ge(gp_ready, 1)
                    pe.matmul(ps[:, 6 + i % 2], ones[:], chan[:, 16 + i], start=True, stop=True).then_inc(l2_done, 1)

            pe.wait_ge(rgw_in, 32)
            pe.wait_ge(tile_done, 20)
            for n in range(4):
                for g in range(2):
                    if n > 0:
                        pe.wait_ge(ri_ready, 2 * (n - 1) + g + 1)
                    pe.matmul(ps[:, 6 + g], rgw[:, g, n], chan[:, 16 + n], start=True, stop=True).then_inc(gate_mm, 1)

            pe.wait_ge(tile_done, 24)
            for h in range(H):
                pe.wait_ge(gu_ready, h + 1)
                pe.matmul(ps[:, h], ones[:], as_m[:, h % 2], start=True, stop=True).then_inc(gb_done, 1)

            pe.wait_ge(qk_ready, 2)
            for h in range(H):
                for w in range(4):
                    if h > 0:
                        pe.wait_ge(kk_evac, 4 * (h - 1) + w + 1)
                    elif w == 2:
                        pe.wait_ge(ri_ready, 8)
                    for c in range(4):
                        kc = chan[:, 4 + h, c * P:(c + 1) * P]
                        o = quarters(4 + w)[:, c]
                        if w == 0:
                            last = pe.matmul(o, kc, kc, start=True, stop=True)
                        elif w == 1:
                            last = pe.matmul(o, kc, chan[:, h, c * P:(c + 1) * P], start=True, stop=True)
                        elif w == 2:
                            last = pe.transpose(o, kc, ident[:])
                        else:
                            last = pe.transpose(o, chan[:, 8 + h, c * P:(c + 1) * P], ident[:])
                    last.then_inc(kk_done, 1)

            pe.wait_ge(decay_ready, 3 * H)
            for h in range(H):
                pe.wait_ge(x1_ready, h + 1)
                for c in range(4):
                    last = pe.transpose(quarters(h)[:, c], quart(x_m[:, h])[:, c], ident[:])
                last.then_inc(x1t_done, 1)

            def level_q(i):
                h = i % 4
                pe.wait_ge(as_ready, 4 + i + 1)
                if i < 4:
                    pe.wait_ge(y1_ready, 4)
                else:
                    pe.wait_ge(y_lev, i - 3)
                for c in range(4):
                    last = pe.matmul(quarters(3 * (i % 2))[:, c], quart(as_m[:, i % 2])[:, c], quart(y_m[:, h])[:, c], start=True, stop=True)
                last.then_inc(qm_done, 1)

            def level_p(i):
                h = i % 4
                pe.wait_ge(qm_ready, i + 1)
                if i >= 2:
                    pe.wait_ge(y_lev, i - 1)
                    pe.wait_ge(x_lev, min(i - 1, 20))
                for c in range(4):
                    qc, xc = quart(q_m[:, i % 2])[:, c], quart(x_m[:, h])[:, c]
                    last = pe.matmul(quarters(3 * (i % 2) + 1)[:, c], xc, qc, start=True, stop=True)
                    if i < 20:
                        last = pe.matmul(quarters(3 * (i % 2) + 2)[:, c], qc, xc, start=True, stop=True)
                last.then_inc(p_done, 1)

            for i in range(25):
                if i < 24:
                    level_q(i)
                if i >= 1:
                    level_p(i - 1)

            for h in range(H):
                pe.wait_ge(y_lev, 20 + h + 1)
                if h >= 2:
                    pe.wait_ge(wt_ready, h - 1)
                for c in range(4):
                    last = pe.matmul(quarters(6 + h % 2)[:, c], quart(chan[:, 4 + h])[:, c], quart(y_m[:, h])[:, c], start=True, stop=True)
                last.then_inc(wt_done, 1)
            pe.wait_ge(wt_ready, 4)

            for c in range(NT):
                for h in range(H):
                    i = 4 * c + h
                    if i >= 2:
                        pe.wait_ge(vn_ready, i - 1)
                    if c > 0:
                        pe.wait_ge(s_ready, 4 * (c - 1) + h + 1)
                    o = ps[:, h % 2, 0:P]
                    last = pe.matmul(o, quart(y_m[:, h])[:, c], quart(chan[:, 8 + h])[:, c], start=True, stop=(c == 0))
                    if c > 0:
                        last = pe.matmul(o, quart(chan[:, 4 + h])[:, c], state[:, h * P:(h + 1) * P], start=False, stop=True)
                    last.then_inc(vn_done, 1)
                for h in range(H):
                    i = 4 * c + h
                    vn = vnew[:, h * P:(h + 1) * P]
                    pe.wait_ge(vn_ready, i + 1)
                    o = quarters(4 + h)[:, c]
                    if c > 0:
                        pe.matmul(o, state[:, h * P:(h + 1) * P], quart(chan[:, h])[:, c], start=True, stop=False)
                    pe.matmul(o, vn, quart(qkt[:, h])[:, c], start=(c == 0), stop=True).then_inc(o_done, 1)
                    if c < NT - 1:
                        if i >= 2:
                            pe.wait_ge(s_ready, i - 1)
                        pe.matmul(ps[:, 2 + h % 2, 0:P], quart(kdec[:, h])[:, c], vn, start=True, stop=True).then_inc(s_done, 1)
            for h in range(H):
                pe.wait_ge(osq_ready, h + 1)
                if h >= 2:
                    pe.wait_ge(orms_ready, h - 1)
                pe.matmul(ps[:, h % 2], ones[:], q_m[:, h % 2], start=True, stop=True).then_inc(oss_done, 1)

            def into_resid(m, tile_of, done, ready, first):
                pe.wait_ge(w_in_slot[2 * (m % 3)], 16 * (m // 3 + 1))
                pe.wait_ge(w_in_slot[2 * (m % 3) + 1], 16 * (m // 3 + 1))
                for w in first:
                    pe.wait_ge(*w)
                for g in range(8):
                    t, n = g // 2, g % 2
                    if g >= 4:
                        pe.wait_ge(ready, g - 3)
                    for k in range(KT):
                        last = pe.matmul(ps[:, g % 4], tile_of(k)[:, t * P:(t + 1) * P], slot_w(m, k)[:, n * 512:(n + 1) * 512],
                                         start=(k == 0), stop=(k == KT - 1))
                    last.then_inc(done, 1)

            into_resid(W_OUT, lambda k: chan[:, 12 + k] if k < 4 else chan[:, 16 + k], out_mm, h1_ready,
                       [(dn_done, H), (rg_done, 1)])

            for m in range(MT):
                transposes(NT + m)
            mem_t = chan[:, 4:8, :].rearrange("p a t -> p (a t)").rearrange("p (k m) -> p k m", k=KT)
            pe.wait_ge(tr_evac, 2 * (NT + MT))
            pe.wait_ge(w_in_slot[2 * (W_CK % 3)], 16 * (W_CK // 3 + 1))
            pe.wait_ge(w_in_slot[2 * (W_CK % 3) + 1], 16 * (W_CK // 3 + 1))
            for i in range(8):
                if i >= 4:
                    pe.wait_ge(mk_evac, i - 3)
                else:
                    pe.wait_ge(h1_ready, i + 5)
                for k in range(KT):
                    last = pe.matmul(ps[:, i % 4, 0:M], slot_w(W_CK, k)[:, i * P:(i + 1) * P], mem_t[:, k], start=(k == 0), stop=(k == KT - 1))
                last.then_inc(mk_mm, 1)
            pe.wait_ge(w_in_slot[2 * (W_CV % 3)], 16 * (W_CV // 3 + 1))
            pe.wait_ge(w_in_slot[2 * (W_CV % 3) + 1], 16 * (W_CV // 3 + 1))
            for i in range(4):
                pe.wait_ge(mk_evac, i + 5)
                for k in range(KT):
                    last = pe.matmul(ps[:, i % 4], mem_t[:, k, (i // 2) * P:(i // 2 + 1) * P], slot_w(W_CV, k)[:, (i % 2) * 512:(i % 2 + 1) * 512],
                                     start=(k == 0), stop=(k == KT - 1))
                last.then_inc(mk_mm, 1)

            s = NT + MT
            for t in range(NT):
                transposes(s)
                s += 1
            pe.wait_ge(tr_evac, 2 * s)
            pe.wait_ge(w_in_slot[2 * (W_CQ % 3)], 16 * (W_CQ // 3 + 1))
            pe.wait_ge(w_in_slot[2 * (W_CQ % 3) + 1], 16 * (W_CQ // 3 + 1))
            for i in range(8):
                pe.wait_ge(mk_evac, 9 + i) if i < 4 else pe.wait_ge(q_evac, i - 3)
                for k in range(KT):
                    last = pe.matmul(ps[:, i % 4], slot_w(W_CQ, k)[:, i * P:(i + 1) * P], act_t[:, k], start=(k == 0), stop=(k == KT - 1))
                last.then_inc(q_mm, 1)

            kt_m = extra[:, 0:4, :].rearrange("p a t -> p (a t)").rearrange("p (i m) -> p i m", i=8)
            v_m = extra[:, 4:8, :].rearrange("p a t -> p (a t)").rearrange("p (m d) -> p m d", m=MT)
            pe.wait_ge(q_evac, 8)

            def prob_transposes(t):
                pe.wait_ge(p_ready, t + 1)
                for b in range(2):
                    if t >= 1:
                        pe.wait_ge(pt_evac, 2 * (t - 1) + b + 1)
                    for i in range(4):
                        c = 4 * b + i
                        last = pe.transpose(quarters(4 + b)[:, i], xn[:, t % 2, c * P:(c + 1) * P], ident[:])
                    last.then_inc(pt_mm, 1)

            for t in range(NT):
                if t >= 2:
                    pe.wait_ge(ex_ready, 4 * (t - 1))
                for h in range(XH):
                    o = ps[:, 2 * (t % 2) + h // 2, (h % 2) * M:(h % 2 + 1) * M]
                    for k in range(2):
                        last = pe.matmul(o, chan[:, 2 * h + k, t * P:(t + 1) * P], kt_m[:, 2 * h + k], start=(k == 0), stop=(k == 1))
                last.then_inc(sc_mm, 1)
                if t >= 1:
                    prob_transposes(t - 1)
            prob_transposes(NT - 1)
            pe.wait_ge(pt_evac, 2 * NT)
            for i in range(8):
                if i >= 2:
                    pe.wait_ge(o_evac, i - 1)
                for m in range(2):
                    last = pe.matmul(ps[:, 6 + i % 2], v_m[:, m, i * P:(i + 1) * P], chan[:, 8 + 2 * (i // 2) + m], start=(m == 0), stop=(m == 1))
                last.then_inc(o_mm, 1)
            into_resid(W_CO, lambda k: chan[:, 16 + k], co_mm, h2_ready, [(o_evac, 8)])

            for t in range(NT):
                transposes(s)
                s += 1
                pe.wait_ge(tr_evac, 2 * s)
                pe.wait_ge(h2_ready, 5)
                for k in range(KT):
                    last = pe.matmul(ps[:, 0, t * E:(t + 1) * E], act_t[:, k, t * P:(t + 1) * P], w_rt[:, k], start=(k == 0), stop=(k == KT - 1))
                last.then_inc(lg_mm, 1)
            pe.wait_ge(oh_ready, 1)
            mask = extra[:, 3, 0:NT * E].rearrange("p (t e) -> p t e", t=NT)
            for t in range(NT):
                for u in range(t + 1):
                    lhs = extra[:, 2, 0:P] if u == t else ones[:]
                    pe.matmul(ps[:, 1, t * E:(t + 1) * E], lhs, mask[:, u], start=(u == 0), stop=(u == t))
            for t in range(NT):
                last = pe.matmul(ps[:, 2, 0:E], ones[:], mask[:, t], start=(t == 0), stop=(t == NT - 1))
            last.then_inc(pos_mm, 1)

            def gathered_transposes(waits):
                for w in waits:
                    pe.wait_ge(*w)
                xgk = xg.rearrange("t (h p k) -> t h k p", h=2, k=HALF)
                for b in range(2):
                    for k in range(4):
                        last = pe.transpose(quarters(6 + b)[:, k], xgk[:, b, k], ident[:])
                last.then_inc(xgt_done, 1)

            pe.wait_ge(codes_ready, 1)
            n_blocks = pe.value_load(nblocks[0:1, 0:1], min_val=E, max_val=MAXB - 1)
            gathered_transposes([(xg_in, 16)])
            g0, g1 = 2 * GM, 2 * GM + 1
            u0, u1 = 2 * ((GM + 1) % 3), 2 * ((GM + 1) % 3) + 1
            d0, d1 = 2 * ((GM + 2) % 3), 2 * ((GM + 2) % 3) + 1
            base = [16 * len([m for m in range(NF) if m % 3 == s]) for s in range(3)]
            with pe.Fori(0, n_blocks) as n:
                pe.wait_ge(xt_ready, n + 1)
                pe.wait_ge(bias3_in, n * 16 + 16)
                for i in range(2):
                    pe.matmul(ps[:, i], ones3[:], bias3[0:3, i * 512:(i + 1) * 512], start=True, stop=False)
                for b, s in enumerate((g0, g1)):
                    pe.wait_ge(w_in_slot[s], n * 16 + (base[s // 2] + 16))
                    for k in range(HALF):
                        for i in range(2):
                            last = pe.matmul(ps[:, i], xt[:, (HALF * b + k) * P:(HALF * b + k + 1) * P],
                                             ring[:, s // 2, HALF * b + k, i * 512:(i + 1) * 512], start=False,
                                             stop=(b == 1 and k == HALF - 1))
                    last.then_inc(gate_half if b == 0 else gate_done, 1)
                for i in range(2):
                    pe.matmul(ps[:, 2 + i], ones3[:], bias3[0:3, D + i * 512:D + (i + 1) * 512], start=True, stop=False)
                    for b, s in enumerate((u0, u1)):
                        if i == 0:
                            pe.wait_ge(w_in_slot[s], n * 16 + (base[s // 2] + 16))
                        for k in range(HALF):
                            last = pe.matmul(ps[:, 2 + i], xt[:, (HALF * b + k) * P:(HALF * b + k + 1) * P],
                                             ring[:, s // 2, HALF * b + k, i * 512:(i + 1) * 512], start=False,
                                             stop=(b == 1 and k == HALF - 1))
                    last.then_inc(up_done, 1)
                pe.wait_ge(xg_in, n * 16 + 32)
                xgk = xg.rearrange("t (h p k) -> t h k p", h=2, k=HALF)
                for b in range(2):
                    for k in range(4):
                        last = pe.transpose(quarters(6 + b)[:, k], xgk[:, b, k], ident[:])
                last.then_inc(xgt_done, 1)
                for i in range(2):
                    pe.matmul(ps[:, 4 + i], ones3[:], bias3[0:3, 2 * D + i * 512:2 * D + (i + 1) * 512], start=True, stop=False)
                hk = hid.rearrange("t (h p k) -> t h k p", h=2, k=HALF)
                for b, s in enumerate((d0, d1)):
                    pe.wait_ge(hid_ready, n * 2 + (b + 1))
                    if b == 0:
                        pe.wait_ge(xt_ready, n + 2)
                    for k in range(4):
                        last = pe.transpose(quarters(6 + b)[:, k], hk[:, b, k], ident[:])
                    last.then_inc(hidt_done, 1)
                    pe.wait_ge(w_in_slot[s], n * 16 + (base[s // 2] + 16))
                    pe.wait_ge(hidt_ready, n * 2 + (b + 1))
                    for k in range(HALF):
                        for i in range(2):
                            last = pe.matmul(ps[:, 4 + i], hid_t[:, (HALF * b + k) * P:(HALF * b + k + 1) * P],
                                             ring[:, s // 2, HALF * b + k, i * 512:(i + 1) * 512], start=False,
                                             stop=(b == 1 and k == HALF - 1))
                            if b == 1 and k == HALF - 1:
                                last.then_inc(down_done, 1)
                    if b == 0:
                        last.then_inc(down_half, 1)

        @block.vector
        def _(dve):
            chain = [0]

            def link(ins):
                chain[0] += 1
                ins.then_inc(dve_c, 1)
                dve.wait_ge(dve_c, chain[0])

            dve.memset(par_rows[:], 0.0).then_inc(par_clear, 1)
            dve.memset(eps_t, EPS).then_inc(par_clear, 1)

            def recip_rms(s):
                dve.wait_ge(stat_ready, s + 1)
                dve.reciprocal(rstd[:, s:s + 1], rms[:, s:s + 1]).then_inc(rstd_ready, 1)

            def evac_t(s, gain, dst):
                for b in range(2):
                    dve.wait_ge(tr_done, 2 * s + b + 1)
                    g = par[:, gain + 4 * b:gain + 4 * b + 4].unsqueeze(2).to_broadcast([P, 4, P])
                    dve.tensor_tensor(dst(b), quarters(2 * (s % 2) + 4 + b), g, ALU.mult).then_inc(tr_evac, 1)

            dve.wait_ge(par_t, 1)
            dve.tensor_copy(par[:], ps[:, 7, 0:P]).then_inc(par_ready, 1)
            dve.wait_ge(par_ready, 1)
            dve.wait_ge(places_init, 16)
            for t in range(NT + 1):
                if t < NT:
                    recip_rms(t)
                if t >= 1:
                    evac_t(t - 1, R_MIX, lambda b: act_t[:, 4 * b:4 * b + 4, (t - 1) * P:t * P])

            bt = ps[:, 7, 0:32].rearrange("p (c w) -> p w c", c=4)
            dve.wait_ge(ba_done, 1)
            dve.wait_ge(small_in, 16 * 5)
            v3 = lambda a: a.rearrange("p (h c) -> p h c", h=4)
            dve.tensor_copy(v3(beta), bt[:, 0:4])
            dve.tensor_tensor(v3(sp_in[:, 0:16]), bt[:, 4:8], dtb.unsqueeze(2).to_broadcast([P, 4, 4]), ALU.add)
            link(dve.tensor_scalar(sp_in[:, 16:20], par[:, R_LAM:R_LAM + 4], -1.0, None, ALU.mult))
            dve.scalar_tensor_tensor(out=sp_s, in0=sp_in, scalar=-1.0, in1=sp_in, op0=ALU.mult, op1=ALU.max).then_inc(sp_ready, 1)
            dve.wait_ge(exp_small, 1)
            link(dve.tensor_scalar(sp_s, sp_e, 2.0, None, ALU.add))
            link(dve.reciprocal(sp_s, sp_s))
            link(dve.tensor_tensor(sp_s, sp_s, sp_e, ALU.mult))
            link(dve.tensor_tensor(sp_s2, sp_s, sp_s, ALU.mult))
            link(dve.tensor_scalar(sp_e, sp_s2, 1.0 / 17, None, ALU.mult))
            for d in (15, 13, 11, 9, 7, 5, 3):
                link(dve.scalar_tensor_tensor(out=sp_e, in0=sp_e, scalar=1.0 / d, in1=sp_s2, op0=ALU.add, op1=ALU.mult))
            link(dve.scalar_tensor_tensor(out=sp_e, in0=sp_e, scalar=1.0, in1=sp_s, op0=ALU.add, op1=ALU.mult))
            link(dve.tensor_scalar(sp_e, sp_e, 2.0, None, ALU.mult))
            link(dve.scalar_tensor_tensor(out=sp_e, in0=sp_in, scalar=0.0, in1=sp_e, op0=ALU.max, op1=ALU.add))
            link(dve.tensor_scalar(rate, sp_e[:, 16:20], -8.0, None, ALU.mult))
            link(dve.tensor_scalar(nrate, sp_e[:, 16:20], 8.0, None, ALU.mult))
            dve.wait_ge(exp_small, 2)
            dve.scalar_tensor_tensor(out=v3(g_t), in0=v3(sp_e[:, 0:16]), scalar=-1.0, in1=alog.unsqueeze(2).to_broadcast([P, 4, 4]),
                                     op0=ALU.mult, op1=ALU.mult).then_inc(g_ready, 1)
            dve.memset(sp_in[:, 0:1], P * EPS).then_inc(sp_ready, 1)

            for j in range(24):
                if j < 12 or 16 <= j < 20:
                    nj, r, jj = (12, R_DCONV, j) if j < 12 else (4, R_RCONV, j - 16)
                    dve.wait_ge(tap_ready, (j if j < 12 else j - 4) + 1)
                    for d in (1, 2, 3):
                        w = par[:, r + (3 - d) * nj + jj:][:, 0:1]
                        ins = dve.scalar_tensor_tensor(out=chan[:, j, d:], in0=ps[:, j % 6, 0:T - d], scalar=w,
                                                       in1=chan[:, j, d:], op0=ALU.mult, op1=ALU.add)
                        if d < 3:
                            link(ins)
                        else:
                            ins.then_inc(tile_done, 1)
                elif j < 16:
                    dve.wait_ge(sig_ready, j + 1)
                    dve.wait_ge(bias_out, 16)
                    dve.tensor_tensor(chan[:, j], ps[:, j % 6], extra[:, 4 + j % 2], ALU.mult).then_inc(tile_done, 1)
                else:
                    tb = extra[:, 6 + j % 2]
                    dve.wait_ge(y2_ready, j - 19)
                    link(dve.tensor_scalar(tb, tb, 0.044715, 1.0, ALU.mult, ALU.add))
                    dve.tensor_tensor(tb, tb, ps[:, j % 6], ALU.mult).then_inc(yt_ready, 1)
                    dve.wait_ge(tanh_ready, j - 19)
                    dve.scalar_tensor_tensor(out=chan[:, j], in0=tb, scalar=1.0, in1=ps[:, j % 6], op0=ALU.add, op1=ALU.mult).then_inc(tile_done, 1)
                if j == 2:
                    dve.wait_ge(gp_done, 1)
                    dve.tensor_copy(gp, ps[:, 7, 64:80]).then_inc(gp_ready, 1)
                if j == 15:
                    for i in range(2):
                        dve.wait_ge(norm_ready, i + 1)
                        link(dve.reciprocal(chan[:, 16 + 4 * i:20 + 4 * i], chan[:, 16 + 4 * i:20 + 4 * i]))
                        dve.tensor_tensor(chan[:, 4 * i:4 * i + 4], chan[:, 4 * i:4 * i + 4], chan[:, 16 + 4 * i:20 + 4 * i], ALU.mult).then_inc(qk_ready, 1)

            for h in range(H):
                dve.wait_ge(proj_done, 24)
                if h >= 2:
                    dve.wait_ge(gb_done, h - 1)
                dve.tensor_tensor(quart(as_m[:, h % 2]), tri[:].unsqueeze(1).to_broadcast([P, 4, P]),
                                  g_t[:, 4 * h:4 * h + 4].unsqueeze(2).to_broadcast([P, 4, P]), ALU.mult).then_inc(gu_ready, 1)
            for h in range(H):
                dve.wait_ge(gb_done, h + 1)
                dve.wait_ge(gp_ready, 1)
                g4 = gp[:, 4 * h:4 * h + 4].unsqueeze(2)
                dve.tensor_tensor(quart(a_m[:, h]), quarters(h), g4.to_broadcast([P, 4, P]), ALU.subtract).then_inc(d_ready, 1)
                dve.tensor_tensor(kdf[:, 4 * h:4 * h + 4].unsqueeze(2), quarters(h)[:, :, P - 1:P], g4, ALU.subtract).then_inc(kd_in, 1)

            four = extra[:, 0:4]
            dve.wait_ge(rt_ready, 4)
            link(dve.tensor_scalar(four, act_t[:, 4:8], 1.0, None, ALU.add))
            link(dve.reciprocal(four, four))
            dve.tensor_tensor(act_t[:, 4:8], act_t[:, 4:8], four, ALU.mult).then_inc(mult_in, 1)
            dve.wait_ge(mult_ready, 1)
            link(dve.memset(act_t[:, 4:8, 0:1], 1.0))
            link(dve.tensor_tensor(chan[:, 16:20], chan[:, 16:20], act_t[:, 4:8], ALU.mult))
            dve.wait_ge(rt_ready, 8)
            for n in range(4):
                last = dve.tensor_tensor_scan(four[:, n], act_t[:, n], chan[:, 16 + n], 0.0, ALU.mult, ALU.add)
            link(last)
            dve.scalar_tensor_tensor(out=chan[:, 20:24], in0=four, scalar=0.5, in1=chan[:, 20:24], op0=ALU.mult, op1=ALU.mult).then_inc(rg_done, 1)

            dve.wait_ge(beta_ready, 1)
            dve.wait_ge(kdf_ready, 2)
            link(dve.tensor_tensor(beg, beta, egp, ALU.mult))
            for h in range(H):
                bc = lambda a: a[:, 4 * h:4 * h + 4].unsqueeze(2).to_broadcast([P, 4, P])
                dve.wait_ge(kk_done, 4 * h + 1)
                dve.wait_ge(masked_ready, h + 1)
                dve.tensor_tensor(quart(a_m[:, h]), quarters(4), quart(a_m[:, h]), ALU.mult).then_inc(kk_evac, 1)
                dve.wait_ge(kk_done, 4 * h + 2)
                dve.tensor_tensor(quart(qkt[:, h]), quarters(5), quart(qkt[:, h]), ALU.mult).then_inc(kk_evac, 1)
                dve.wait_ge(kk_done, 4 * h + 3)
                dve.tensor_tensor(quart(chan[:, 4 + h]), quarters(6), bc(beg), ALU.mult)
                dve.tensor_tensor(quart(kdec[:, h]), quarters(6), bc(kdf), ALU.mult).then_inc(kk_evac, 1)
                dve.wait_ge(kk_done, 4 * h + 4)
                dve.tensor_tensor(quart(chan[:, 8 + h]), quarters(7), bc(beta), ALU.mult).then_inc(kk_evac, 1)

            for h in range(H):
                dve.wait_ge(as_ready, h + 1)
                dve.tensor_tensor(quart(x_m[:, h]), ident[:].unsqueeze(1).to_broadcast([P, 4, P]), quart(as_m[:, h % 2]), ALU.subtract).then_inc(x1_ready, 1)
            for i in range(24):
                h = i % 4
                dve.wait_ge(p_done, i + 1)
                dve.wait_ge(y1_ready, 4)
                dve.tensor_tensor(y_m[:, h], y_m[:, h], ps[:, 3 * (i % 2) + 1], ALU.subtract).then_inc(y_lev, 1)
                if i < 20:
                    dve.tensor_tensor(x_m[:, h], x_m[:, h], ps[:, 3 * (i % 2) + 2], ALU.subtract).then_inc(x_lev, 1)

            for c in range(NT - 1):
                for h in range(H):
                    i = 4 * c + h
                    st = state[:, h * P:(h + 1) * P]
                    dve.wait_ge(s_done, i + 1)
                    if c == 0:
                        dve.tensor_copy(st, ps[:, 2 + h % 2, 0:P]).then_inc(s_ready, 1)
                    else:
                        dve.wait_ge(o_done, i + 1)
                        dve.wait_ge(s_ready, i - 3)
                        dve.scalar_tensor_tensor(out=st, in0=st, scalar=elast[:, 4 * h + c:4 * h + c + 1], in1=ps[:, 2 + h % 2, 0:P],
                                                 op0=ALU.mult, op1=ALU.add).then_inc(s_ready, 1)
            for h in range(H):
                dve.wait_ge(orms_ready, h + 1)
                link(dve.reciprocal(q_m[:, h % 2], q_m[:, h % 2]))
                dve.tensor_tensor(q_m[:, h % 2], q_m[:, h % 2], ps[:, 4 + h], ALU.mult).then_inc(onorm_ready, 1)

            def add_resid(g, done, ready):
                dve.wait_ge(done, g + 1)
                r = resid[:, g // 2, (g % 2) * 512:(g % 2 + 1) * 512]
                dve.tensor_tensor(r, r, ps[:, g % 4], ALU.add).then_inc(ready, 1)

            s = NT
            for g in range(8):
                add_resid(g, out_mm, h1_ready)
            mem_t = chan[:, 4:8, :].rearrange("p a t -> p (a t)").rearrange("p (k m) -> p k m", k=KT)
            for m in range(MT + 1):
                if m < MT:
                    recip_rms(s + m)
                if m >= 1:
                    evac_t(s + m - 1, R_MEM, lambda b: mem_t[:, 4 * b:4 * b + 4, (m - 1) * P:m * P])
            s += MT
            for t in range(NT + 1):
                if t < NT:
                    recip_rms(s + t)
                if t >= 1:
                    evac_t(s + t - 1, R_CROSS, lambda b: act_t[:, 4 * b:4 * b + 4, (t - 1) * P:t * P])
            s += NT
            for t in range(NT):
                o = 4 * (t % 2)
                scv = ps[:, 2 * (t % 2):2 * (t % 2) + 2, :].rearrange("p b (g m) -> p (b g) m", g=2)
                dve.wait_ge(sc_mm, t + 1)
                link(dve.tensor_reduce(mx[:, o:o + 4], scv, AX_X, ALU.max))
                dve.tensor_scalar(nmx[:, o:o + 4], mx[:, o:o + 4], -(XD ** -0.5), None, ALU.mult).then_inc(mx_ready, 1)
                dve.wait_ge(ex_ready, 4 * t + 4)
                link(dve.reciprocal(rinv[:, o:o + 4], rsum[:, o:o + 4]))
                pr = xn[:, t % 2].rearrange("p (h m) -> p h m", h=XH)
                dve.tensor_tensor(pr, pr, rinv[:, o:o + 4].unsqueeze(2).to_broadcast([P, 4, M]), ALU.mult).then_inc(p_ready, 1)
            for g in range(8):
                add_resid(g, co_mm, h2_ready)
                if g % 2 == 1:
                    t = g // 2
                    recip_rms(s + t)
                    if t >= 1:
                        evac_t(s + t - 1, R_MOE, lambda b: act_t[:, 4 * b:4 * b + 4, (t - 1) * P:t * P])
            evac_t(s + NT - 1, R_MOE, lambda b: act_t[:, 4 * b:4 * b + 4, (NT - 1) * P:NT * P])
            s += NT

            dve.wait_ge(iota_ready, 1)
            lg = extra[:, 4, 0:NT * E].rearrange("p (t e) -> p t e", t=NT)
            top = extra[:, 5, 0:64]
            topi = extra[:, 5, 64:96].bitcast(U32)
            topf = extra[:, 5, 128:160]
            for t in range(NT):
                dve.wait_ge(lg_mm, NT)
                link(dve.tensor_tensor(lg[:, t], ps[:, 0, t * E:(t + 1) * E], brt[:], ALU.add))
                link(dve.max(top[:, 8 * t:8 * t + 8], lg[:, t]))
                link(dve.max_index(topi[:, 8 * t:8 * t + 8], top[:, 8 * t:8 * t + 8], lg[:, t]))
            link(dve.tensor_copy(topf, topi))
            t4 = top[:, 0:32].rearrange("p (t k) -> p t k", t=NT)
            dve.tensor_tensor(gates[:], t4[:, :, 0:4], t4[:, :, 0:1].to_broadcast([P, NT, TOPK]), ALU.subtract).then_inc(top_ready, 1)
            ef = extra[:, 1, :]
            it_i = extra[:, 0, :].bitcast(I32)
            oh = extra[:, 6, :].rearrange("p (t k e) -> p t k e", t=NT, k=TOPK)
            tf4 = topf.rearrange("p (t k) -> p t k", t=NT)[:, :, 0:4]
            for t in range(NT):
                last = dve.tensor_tensor(oh[:, t], ef[:, 0:E].unsqueeze(1).to_broadcast([P, TOPK, E]),
                                         tf4[:, t].unsqueeze(2).to_broadcast([P, TOPK, E]), ALU.is_equal)
            link(last)
            mask = extra[:, 3, 0:NT * E].rearrange("p (t e) -> p t e", t=NT)
            for t in range(NT):
                last = dve.tensor_reduce(mask[:, t], oh[:, t].rearrange("p k e -> p e k"), AX_X, ALU.add)
            last.then_inc(oh_ready, 1)
            dve.wait_ge(gexp_ready, 1)
            link(dve.tensor_reduce(top[:, 40:44], gates[:], AX_X, ALU.add))
            link(dve.reciprocal(top[:, 40:44], top[:, 40:44]))
            link(dve.tensor_tensor(gates[:], gates[:], top[:, 40:44].unsqueeze(2).to_broadcast([P, NT, TOPK]), ALU.mult))
            dve.wait_ge(pos_mm, 1)
            posp = extra[:, 7, 0:NT * E].rearrange("p (t e) -> p t e", t=NT)
            link(dve.tensor_tensor(posp, ps[:, 1, 0:NT * E].rearrange("p (t e) -> p t e", t=NT),
                                   ef[:, 32:64].unsqueeze(1).to_broadcast([P, NT, E]), ALU.add))
            for t in range(NT):
                last = dve.tensor_tensor(oh[:, t], oh[:, t], posp[:, t:t + 1].to_broadcast([P, TOPK, E]), ALU.mult)
            link(last)
            link(dve.tensor_reduce(topf[:, 0:16], extra[:, 6, :].rearrange("p (a e) -> p a e", e=E), AX_X, ALU.add))
            dve.tensor_copy(it_i[:, 256:272], topf[:, 0:16]).then_inc(slot_ready, 1)
            cnt = extra[0:1, 7, 256:288]
            link(dve.tensor_copy(cnt, ps[0:1, 2, 0:E]))
            flag, rank = extra[0:1, 7, 288:384], extra[0:1, 7, 384:480]
            link(dve.tensor_tensor(flag.rearrange("p (e b) -> p e b", b=3), cnt.unsqueeze(2).to_broadcast([1, E, 3]),
                                   ef[0:1, 96:99].unsqueeze(1).to_broadcast([1, E, 3]), ALU.is_gt))
            link(dve.tensor_tensor_scan(rank, ones[0:1, 0:96], flag, 0.0, ALU.mult, ALU.add))
            link(dve.tensor_scalar(extra[0:1, 7, 480:481], rank[:, 95:96], float(E), None, ALU.add))
            link(dve.tensor_copy(nblocks[:], extra[0:1, 7, 480:481]))
            link(dve.tensor_tensor(rank, rank, flag, ALU.subtract))
            link(dve.tensor_tensor(flag, flag, ef[0:1, 128:224], ALU.mult))
            sel = act_t[0:1, 0:3, :].rearrange("p a t -> p (a t)").rearrange("p (j f) -> p j f", j=16)
            dve.wait_ge(lg_mm, NT)
            link(dve.tensor_tensor(sel, rank.unsqueeze(1).to_broadcast([1, 16, 96]), ef[0:1, 224:240].unsqueeze(2).to_broadcast([1, 16, 96]), ALU.is_equal))
            link(dve.tensor_tensor(sel, sel, flag.unsqueeze(1).to_broadcast([1, 16, 96]), ALU.mult))
            link(dve.tensor_reduce(flag[:, 0:16], sel, AX_X, ALU.add))
            link(dve.tensor_scalar(flag[:, 0:16], flag[:, 0:16], float(E * CAP), None, ALU.add))
            link(dve.tensor_copy(codes[0:1, E:MAXB], flag[:, 0:16]))
            link(dve.tensor_scalar(experts[:], codes[:], 2, None, ALU.arith_shift_right))
            dve.tensor_scalar(experts[:], experts[:], E - 1, None, ALU.min).then_inc(codes_ready, 1)

            dve.wait_ge(codes_ready, 1)
            n_blocks = dve.value_load(nblocks[0:1, 0:1], min_val=E, max_val=MAXB - 1)

            def evac_xt():
                for b in range(2):
                    g = gain_moe[:, 4 * b:4 * b + 4].unsqueeze(2).to_broadcast([P, 4, P])
                    last = dve.tensor_tensor(quart(xt[:, 512 * b:512 * (b + 1)]), quarters(6 + b), g, ALU.mult)
                return last

            dve.wait_ge(idx_in, 16)
            dve.tensor_scalar(idx[:, 1:2], idx[:, 0:1], 2, None, ALU.arith_shift_right).then_inc(tok_ready, 1)
            dve.wait_ge(xgt_done, 1)
            evac_xt().then_inc(xt_ready, 1)
            with dve.Fori(0, n_blocks) as n:
                dve.wait_ge(gate_done, n + 1)
                dve.tensor_scalar(gt, ps[:, 0:2, :].rearrange("p b f -> p (b f)"), 7.0, None, ALU.min).then_inc(gt_ready, 1)
                dve.wait_ge(sg_ready, n + 1)
                dve.tensor_tensor(gt, gt, sig_e, ALU.mult).then_inc(gs_ready, 1)
                dve.wait_ge(idx_in, n * 16 + 32)
                dve.tensor_scalar(idx[:, 1:2], idx[:, 0:1], 2, None, ALU.arith_shift_right).then_inc(tok_ready, 1)
                for i in range(2):
                    hs = slice(i * 512, (i + 1) * 512)
                    dve.wait_ge(up_done, n * 2 + (i + 1))
                    dve.tensor_scalar(up[:, hs], ps[:, 2 + i], 7.0, -7.0, ALU.min, ALU.max).then_inc(up_ready, 1)
                    dve.wait_ge(up_ready, n * 2 + (i + 1))
                    if i == 0:
                        dve.wait_ge(gs_ready, n + 1)
                    dve.scalar_tensor_tensor(out=hid[:, hs], in0=up[:, hs], scalar=1.0, in1=gt[:, hs], op0=ALU.add, op1=ALU.mult).then_inc(hid_ready, 1)
                dve.wait_ge(xgt_done, n + 2)
                evac_xt().then_inc(xt_ready, 1)
                for b in range(2):
                    dve.wait_ge(hidt_done, n * 2 + (b + 1))
                    dve.tensor_copy(hid_t[:, 512 * b:512 * (b + 1)], ps[:, 6 + b]).then_inc(hidt_ready, 1)

            yv = ring[:, :, :, :].rearrange("p a k d -> p (a k) d")
            for t in range(NT):
                dve.wait_ge(y_in[t], 16)
                for k in range(TOPK):
                    ins = dve.scalar_tensor_tensor(out=resid[:, t], in0=yv[:, 4 * t + k], scalar=gates[:, t, k:k + 1], in1=resid[:, t],
                                                   op0=ALU.mult, op1=ALU.add)
                    ins.then_inc(comb_ready if k == TOPK - 1 else tail_c, 1)
                    if k < TOPK - 1:
                        dve.wait_ge(tail_c, 3 * t + k + 1)
            dve.wait_ge(stat_ready, 14 + NT + 1)
            dve.reciprocal(rstd[:, 0:4], rms[:, 0:4]).then_inc(rstd_ready, 1)
            dve.wait_ge(rstd_ready, 15)
            dve.wait_ge(nf_in, 16)
            for t in range(NT):
                dve.scalar_tensor_tensor(out=resid[:, t], in0=resid[:, t], scalar=rstd[:, t:t + 1], in1=nf_b, op0=ALU.mult, op1=ALU.mult).then_inc(fin_ready, 1)


_INS = ["x", "mem", "norm_mix", "w_in", "dn_conv", "dn_a_log", "dn_dt_bias", "dn_norm", "rg_conv", "rg_conv_b",
        "rg_w_a", "rg_b_a", "rg_w_x", "rg_b_x", "rg_lambda", "w_out", "norm_cross", "norm_mem", "w_cq", "w_ckv",
        "w_co", "norm_moe", "w_router", "b_router", "w_gate", "b_gate", "w_up", "b_up", "w_down", "b_down",
        "norm_final"]


def kernel(**inputs):
    import numpy as _np
    import concourse.bacc as _bacc
    from concourse import mybir as _mybir
    from concourse.bass_utils import run_bass_kernel_spmd as _run

    nc = _bacc.Bacc("TRN2", target_bir_lowering=False, num_devices=1)
    arrays, args = {}, []
    for name in _INS:
        a = _np.ascontiguousarray(inputs[name])
        arrays[f"in_{name}_dram"] = a
        args.append(nc.dram_tensor(f"in_{name}_dram", a.shape, _mybir.dt.from_np(a.dtype), kind="ExternalInput").ap())
    shape = inputs["x"].shape
    args.append(nc.dram_tensor("out_0_dram", shape, _mybir.dt.float32, kind="ExternalOutput").ap())
    build_layer(nc, *args)
    r = _run(nc, [arrays], core_ids=[0])
    return r.results[0]["out_0_dram"]
```

```python
from contextlib import ExitStack

import concourse.bass as bass
from concourse import mybir

ALU = mybir.AluOpType
ACT = mybir.ActivationFunctionType
AX_X = mybir.AxisListType.X
F32 = mybir.dt.float32
BF16 = mybir.dt.bfloat16
F32R = mybir.dt.float32r
I32 = mybir.dt.int32
U32 = mybir.dt.uint32

P = 128
EPS = 1e-6
GELU_C = 0.7978845608028654


def build_layer(nc, x, mem, norm_mix, w_in, dn_conv, dn_a_log, dn_dt_bias, dn_norm, rg_conv, rg_conv_b,
                rg_w_a, rg_b_a, rg_w_x, rg_b_x, rg_lambda, w_out, norm_cross, norm_mem, w_cq, w_ckv,
                w_co, norm_moe, w_router, b_router, w_gate, b_gate, w_up, b_up, w_down, b_down,
                norm_final, out):
    T, D = x.shape[1], x.shape[2]
    NT = T // P
    KT = D // P
    HALF = KT // 2
    H = dn_a_log.shape[1]
    M = mem.shape[1]
    MT = M // P
    XH = 4
    XD = D // XH
    E = w_router.shape[2]
    TOPK = 4
    N_ROW = T * TOPK
    CAP = NT
    NSPLIT = 4
    MAXB = 50
    N_MORE = MAXB - E
    GU = 2 * KT
    SPLIT = GU + HALF
    NOBODY = 1 << 20
    LEVELS = [1, 2, 4, 8, 16, 32, 64]
    assert D == 1024 and T == 512 and H == 4 and M == 256 and E == 32

    hn_rows = nc.dram_tensor("hn_rows", [T, D], F32, kind="Internal").ap()
    y_rows = nc.dram_tensor("y_rows", [N_ROW, D], F32, kind="Internal").ap()
    places = nc.dram_tensor("places", [(E * CAP + 1) * P, 1], I32, kind="Internal").ap()
    bias_parts = nc.dram_tensor("bias_parts", [E, 3, 3 * D], BF16, kind="Internal").ap()
    places_by_block = places.rearrange("(c p) o -> c p o", p=P)

    with ExitStack() as ctx:
        def sb(name, shape, dt=F32):
            return ctx.enter_context(nc.sbuf_tensor(name, shape, dt))

        def sem(name):
            return ctx.enter_context(nc.semaphore(name))

        ps = ctx.enter_context(nc.psum_tensor("ps", [P, 8, 512], F32))

        def quarters(bank):
            return ps[:, bank, :].rearrange("p (c f) -> p c f", c=4)

        resid = sb("resid", [P, NT, D])
        ring = sb("ring", [P, 3, KT, D])
        ident = sb("ident", [P, P])
        ones = sb("ones", [P, P])
        tri = sb("tri", [P, P])
        par_rows = sb("par_rows", [P, P])
        par = sb("par", [P, P])
        w_ba = sb("w_ba", [P, KT, 2 * H])
        w_rt = sb("w_rt", [P, KT, E])
        brt = sb("brt", [P, E])
        small = sb("small", [P, 320])
        ones3 = sb("ones3", [3, P], BF16)
        codes = sb("codes", [1, MAXB], I32)
        experts = sb("experts", [1, MAXB], I32)
        nblocks = sb("nblocks", [1, 2], I32)
        gates = sb("gates", [P, NT, TOPK])
        guard = sb("guard", [1, 8])
        gain_moe = sb("gain_moe", [P, KT])

        idx = sb("idx", [P, 2], I32)
        xn = sb("xn", [P, 2, D])
        extra = sb("extra", [P, 8, T])
        with ExitStack() as dense:
            act_t = dense.enter_context(nc.sbuf_tensor("act_t", [P, KT, T], F32))
            chan = dense.enter_context(nc.sbuf_tensor("chan", [P, 24, T], F32))
        wsp = sb("wsp", [P, NSPLIT, 2, D], F32R)
        x_hi, x_lo = sb("x_hi", [P, D], F32R), sb("x_lo", [P, D], F32R)
        hid_hi, hid_lo = sb("hid_hi", [P, HALF * P], F32R), sb("hid_lo", [P, HALF * P], F32R)
        hid_t = sb("hid_t", [P, HALF * P])
        xg, gt, up, y_sb = (sb(n, [P, D]) for n in ("xg", "gt", "up", "y_sb"))
        row_tab, tok_tab = extra[:, 3, 384:384 + MAXB].bitcast(I32), extra[:, 3, 448:448 + MAXB].bitcast(I32)
        bias3 = extra[0:3, 4:7, :].rearrange("p a t -> p (a t)").bitcast(BF16)
        sig_e = up
        hid = up
        zero_i = extra[:, 3, 500:501].bitcast(I32)
        codes_f = extra[0:1, 2, P:P + MAXB]
        codes_col = extra[0:MAXB, 2, 256:257].bitcast(I32)
        blk_i, blk_f = extra[0:MAXB, 3, P:2 * P].bitcast(I32), extra[0:MAXB, 3, 2 * P:3 * P]

        at = [0]

        def cols(n):
            at[0] += n
            assert at[0] <= 320
            return small[:, at[0] - n:at[0]]

        eps_t = cols(1)
        ss = cols(14)
        rms = cols(14)
        rstd = cols(14)
        dtb = cols(H)
        alog = cols(H)
        sp_in = cols(20)
        sp_e = cols(20)
        sp_s = cols(20)
        sp_s2 = cols(20)
        g_t = cols(16)
        beta = cols(16)
        gp = cols(16)
        egp = cols(16)
        kdf = cols(16)
        beg = cols(16)
        elast = cols(16)
        rate = cols(4)
        nrate = cols(4)
        mx = cols(8)
        nmx = cols(8)
        rsum = cols(8)
        rinv = cols(8)

        R_DCONV, R_RCONV, R_RCB, R_BA, R_BX, R_LAM, R_DN = 0, 48, 64, 68, 72, 76, 80
        R_MIX, R_CROSS, R_MEM, R_MOE, R_END = 81, 89, 97, 105, 113

        xn_flat = xn[:, :, :].rearrange("p a d -> p (a d)")
        rgw = xn_flat[:, 0:1024].rearrange("p (g n o) -> p g n o", g=2, n=4)
        lmask = xn_flat[:, 1024:1024 + 7 * P].rearrange("p (l s) -> p l s", l=7)

        tmp = ring[:, 2, :, :].rearrange("p k d -> p (k d)").rearrange("p (a f) -> p a f", f=T)
        a_m, x_m, kdec = tmp[:, 0:4], tmp[:, 4:8], tmp[:, 8:12]
        as_m, q_m = tmp[:, 12:14], tmp[:, 14:16]
        vnew, state = tmp[:, 12, :], tmp[:, 13, :]
        y_m, qkt = extra[:, 0:4], extra[:, 4:8]

        def quart(ap):
            return ap.rearrange("p (c f) -> p c f", c=4)


        x_in = [sem(f"x_in{t}") for t in range(NT)]
        w_in_slot = [sem(f"w_in_slot{i}") for i in range(6)]
        par_in, ba_in, rgw_in, small_in, bias_in = (sem(n) for n in ("par_in", "ba_in", "rgw_in", "small_in", "bias_in"))
        consts_ready, par_clear = sem("consts_ready"), sem("par_clear")
        par_t, par_ready = sem("par_t"), sem("par_ready")
        xn_ready, tr_done, tr_evac = sem("xn_ready"), sem("tr_done"), sem("tr_evac")
        stat_ready, rstd_ready = sem("stat_ready"), sem("rstd_ready")
        dve_c, act_c, pool_c = sem("dve_chain"), sem("act_chain"), sem("pool_chain")
        ba_done, g_ready, gp_done, gp_ready = sem("ba_done"), sem("g_ready"), sem("gp_done"), sem("gp_ready")
        exp_small, beta_ready, sp_ready = sem("exp_small"), sem("beta_ready"), sem("sp_ready")
        proj_done, tap_ready, tile_done, sig_ready, silu_done = (sem(n) for n in ("proj_done", "tap_ready", "tile_done", "sig_ready", "silu_done"))
        sq_ready, l2_done, l2_evac, norm_ready, qk_ready = (sem(n) for n in ("sq_ready", "l2_done", "l2_evac", "norm_ready", "qk_ready"))
        y2_ready, yt_ready, tanh_ready = sem("y2_ready"), sem("yt_ready"), sem("tanh_ready")
        gate_mm, ri_ready, bx_ready, rt_ready, mult_in, mult_ready, rg_done = (sem(n) for n in ("gate_mm", "ri_ready", "bx_ready", "rt_ready", "mult_in", "mult_ready", "rg_done"))
        masks_ready = sem("masks_ready")
        gu_ready, gb_done, d_ready, split_ready, decay_ready, masked_ready = (sem(n) for n in ("gu_ready", "gb_done", "d_ready", "split_ready", "decay_ready", "masked_ready"))
        kk_done, kk_evac, qexp_ready, kd_in, kdf_ready = (sem(n) for n in ("kk_done", "kk_evac", "qexp_ready", "kd_in", "kdf_ready"))
        x1_ready, x1t_done, y1_ready = sem("x1_ready"), sem("x1t_done"), sem("y1_ready")
        as_ready, qm_done, qm_ready, p_done, y_lev, x_lev = (sem(n) for n in ("as_ready", "qm_done", "qm_ready", "p_done", "y_lev", "x_lev"))
        wt_done, wt_ready = sem("wt_done"), sem("wt_ready")
        vn_done, vn_ready, s_done, s_ready, o_done = (sem(n) for n in ("vn_done", "vn_ready", "s_done", "s_ready", "o_done"))
        osq_ready, oss_done, orms_ready, onorm_ready, dn_done = (sem(n) for n in ("osq_ready", "oss_done", "orms_ready", "onorm_ready", "dn_done"))
        out_mm, h1_ready = sem("out_mm"), sem("h1_ready")
        mem_in, mk_mm, mk_evac = sem("mem_in"), sem("mk_mm"), sem("mk_evac")
        q_mm, q_evac = sem("q_mm"), sem("q_evac")
        sc_mm, mx_ready, ex_ready, p_ready, pt_mm, pt_evac = (sem(n) for n in ("sc_mm", "mx_ready", "ex_ready", "p_ready", "pt_mm", "pt_evac"))
        o_mm, o_evac, co_mm, h2_ready = sem("o_mm"), sem("o_evac"), sem("co_mm"), sem("h2_ready")
        hn_out = [sem(f"hn_out{i}") for i in range(2)]
        lg_mm, lg_ready, top_ready, gexp_ready, oh_ready, pos_mm, slot_ready = (sem(n) for n in ("lg_mm", "lg_ready", "top_ready", "gexp_ready", "oh_ready", "pos_mm", "slot_ready"))
        codes_ready, places_init, placed, iota_ready = (sem(n) for n in ("codes_ready", "places_init", "placed", "iota_ready"))
        bias_split, bias_out = sem("bias_split"), sem("bias_out")
        xg_clear, xg_in, xgt_done, xt_ready = (sem(n) for n in ("xg_clear", "xg_in", "xgt_done", "xt_ready"))
        bias3_in = sem("bias3_in")
        tab_step, tab_mm, blk_in, row_ready = (sem(n) for n in ("tab_step", "tab_mm", "blk_in", "row_ready"))
        hidhi_ready, hidlo_ready = sem("hidhi_ready"), sem("hidlo_ready")
        gt_ready, sg_ready, hid_ready, hidt_done, hidt_ready = (sem(n) for n in ("gt_ready", "sg_ready", "hid_ready", "hidt_done", "hidt_ready"))
        down_done, y_ready, y_out = sem("down_done"), sem("y_ready"), sem("y_out")
        y_in = [sem(f"y_in{t}") for t in range(NT)]
        comb_ready, nf_in, fin_ready, out_sent = sem("comb_ready"), sem("nf_in"), sem("fin_ready"), sem("out_sent")
        stood, hi_ready, lo_ready, split_used, xhi_ready, xlo_ready, bias3_used, down_half, gs_ready, up_ready, tail_c = (sem(n) for n in ("stood", "hi_ready", "lo_ready", "split_used", "xhi_ready", "xlo_ready", "bias3_used", "down_half", "gs_ready", "up_ready", "tail_c"))

        block = ctx.enter_context(nc.Block())

        def front(w, c0):
            v = w[0].rearrange("(h k p) n -> h p k n", h=2, p=P)
            return [v[h, :, :, c0:c0 + D] for h in range(2)]

        C_BA = 4 * H * P
        FRONT = [front(w_in, 0), front(w_in, D), front(w_in, C_BA + 2 * H),
                 front(w_out, 0), front(w_ckv, 0), front(w_ckv, D), front(w_cq, 0), front(w_co, 0)]
        NF = len(FRONT)
        W_QK, W_VZ, W_RXY, W_OUT, W_CK, W_CV, W_CQ, W_CO = range(NF)
        USED = [(proj_done, 8), (proj_done, 16), (proj_done, 24), (out_mm, 8), (mk_mm, 8), (mk_mm, 12), (q_mm, 8), (co_mm, 8)]

        def slot_w(m, k):
            return ring[:, m % 3, k, :]

        expert_w = [w[0].rearrange("e (h p k) n -> e h p k n", h=2, p=P) for w in (w_gate, w_up, w_down)]

        GM = NF % 3
        base = [16 * len([m for m in range(NF) if m % 3 == s]) for s in range(3)]

        @block.sync
        def _(sp):
            for t in range(NT):
                sp.dma_start(resid[:, t, :], x[0, t * P:(t + 1) * P, :]).then_inc(x_in[t], 16)
            sp.wait_ge(par_in, 16 * 11)
            sp.wait_ge(ba_in, 16)
            for m in range(NF):
                if m == W_CV:
                    sp.wait_ge(dn_done, H)
                    sp.dma_start(chan[:, 0:4, :].rearrange("p a t -> p (a t)").rearrange("p (m d) -> p m d", m=MT),
                                 mem[0].rearrange("(m p) d -> p m d", p=P)).then_inc(mem_in, 16)
                if m >= 3:
                    sp.wait_ge(*USED[m - 3])
                for h in range(2):
                    s = 2 * (m % 3) + h
                    sp.dma_start(ring[:, m % 3, HALF * h:HALF * (h + 1), :], FRONT[m][h]).then_inc(w_in_slot[s], 16)
                if m == W_RXY:
                    sp.wait_ge(tr_evac, 2 * NT)
                    sp.dma_start(rgw[:, 0], rg_w_a[0].rearrange("n i o -> i n o")).then_inc(rgw_in, 16)
                    sp.dma_start(rgw[:, 1], rg_w_x[0].rearrange("n i o -> i n o")).then_inc(rgw_in, 16)

            for j in range(3):
                sp.wait_ge(*USED[NF + j - 3])
                for h in range(2):
                    sp.dma_start(ring[:, (GM + j) % 3, HALF * h:HALF * (h + 1), :],
                                 expert_w[j][0, h]).then_inc(w_in_slot[2 * ((GM + j) % 3) + h], 16)
            sp.wait_ge(codes_ready, 1)
            sp.dma_start(bias3, bias_parts[0]).then_inc(bias3_in, 16)
            n_blocks = sp.value_load(nblocks[0:1, 0:1], min_val=E, max_val=MAXB - 3)
            n_more = sp.value_load(nblocks[0:1, 1:2], min_val=E - 1, max_val=MAXB - 4)
            with sp.Fori(0, n_more) as n:
                e = sp.value_load(experts[0:1, bass.ds(n + 1, 1)], min_val=0, max_val=E - 1)
                for j in range(3):
                    if j == 2:
                        sp.wait_ge(bias3_used, n + 1)
                        sp.dma_start(bias3, bias_parts[bass.ds(e, 1)].rearrange("o a b -> (o a) b")).then_inc(bias3_in, 16)
                    for h in range(2):
                        if j == 2 and h == 0:
                            sp.wait_ge(down_half, n + 1)
                        else:
                            sp.wait_ge(lo_ready, n * SPLIT + min(KT * j + HALF * (h + 1), SPLIT))
                        sp.dma_start(ring[:, (GM + j) % 3, HALF * h:HALF * (h + 1), :],
                                     expert_w[j][bass.ds(e, 1), h].rearrange("o p k n -> (o p) k n"))\
                            .then_inc(w_in_slot[2 * ((GM + j) % 3) + h], 16)
            sp.wait_ge(lo_ready, n_more * SPLIT + HALF)
            sp.dma_start(ring[:, GM, 0:HALF, :], expert_w[0][0, 0]).then_inc(w_in_slot[2 * GM], 16)
            sp.wait_ge(y_out, n_blocks * 16)
            sp.dma_start(up[:], norm_final.rearrange("(o d) -> o d", o=1).to_broadcast([P, D])).then_inc(nf_in, 16)
            y_tok = y_rows.rearrange("(t p k) d -> t p k d", p=P, k=TOPK)
            for t in range(NT):
                sp.dma_start(ring[:, :, :, :].rearrange("p a k d -> p (a k) d")[:, 4 * t:4 * t + 4, :], y_tok[t]).then_inc(y_in[t], 16)
            for t in range(NT):
                sp.wait_ge(fin_ready, t + 1)
                sp.dma_start(out[0, t * P:(t + 1) * P, :], resid[:, t, :]).then_inc(out_sent, 16)
            sp.wait_ge(out_sent, 16 * NT)

        @block.gpsimd
        def _(pool):
            chain = [0]

            def link(ins):
                chain[0] += 1
                ins.then_inc(pool_c, 1)
                pool.wait_ge(pool_c, chain[0])

            link(pool.memset(ones[:], 1.0))
            link(pool.memset(ident[:], 0.0))
            pool.affine_select(out=ident[:], in_=ident[:], compare_op=ALU.not_equal, fill=1.0, base=0,
                               pattern=[[-1, P]], channel_multiplier=1).then_inc(consts_ready, 1)
            pool.affine_select(out=tri[:], in_=ones[:], compare_op=ALU.is_ge, fill=0.0, base=0,
                               pattern=[[1, P]], channel_multiplier=-1).then_inc(consts_ready, 1)
            pool.memset(ones3[:], 1.0).then_inc(consts_ready, 1)
            pool.memset(guard[:], 0.0).then_inc(stood, 1)
            nobody = act_t[:, 0, 0:E * CAP + 1].bitcast(I32)
            link(pool.memset(nobody, NOBODY))
            pool.dma_start(places.rearrange("(p c) o -> p (c o)", p=P), nobody).then_inc(places_init, 16)

            b_f = extra[0:E, 0:6, :].rearrange("p a t -> p (a t)")
            parts = chan[0:E, 15:24, :].rearrange("p a t -> p (a t)").bitcast(BF16).rearrange("p (s f) -> p s f", s=3)
            pool.wait_ge(bias_in, 48)
            link(pool.tensor_copy(parts[:, 0], b_f))
            link(pool.tensor_tensor(b_f, b_f, parts[:, 0], ALU.subtract))
            link(pool.tensor_copy(parts[:, 1], b_f))
            link(pool.tensor_tensor(b_f, b_f, parts[:, 1], ALU.subtract))
            link(pool.tensor_copy(parts[:, 2], b_f))
            pool.dma_start(bias_parts, parts).then_inc(bias_out, 16)

            pool.wait_ge(tr_evac, 2 * NT)
            for l, w in enumerate(LEVELS):
                nb = P // (2 * w)
                v = lmask[:, l, :].rearrange("p (b j) -> p b j", b=nb)
                src = ones[:, :].rearrange("p (b j) -> p b j", b=nb)
                link(pool.affine_select(out=v, in_=src, compare_op=ALU.is_ge, fill=0.0, base=-w,
                                        pattern=[[-2 * w, nb], [0, 2 * w]], channel_multiplier=1))
                link(pool.affine_select(out=v, in_=v, compare_op=ALU.is_ge, fill=0.0, base=2 * w - 1,
                                        pattern=[[2 * w, nb], [0, 2 * w]], channel_multiplier=-1))
                link(pool.affine_select(out=v, in_=v, compare_op=ALU.is_ge, fill=0.0, base=w - 1,
                                        pattern=[[0, nb], [-1, 2 * w]], channel_multiplier=0))

            for j in range(12):
                pool.wait_ge(sig_ready, j + 1)
                pool.tensor_tensor(chan[:, j], chan[:, j], extra[:, 4 + j % 2], ALU.mult).then_inc(silu_done, 1)

            for n in range(4):
                pool.wait_ge(ri_ready, 2 * n + 2)
                pool.tensor_tensor(chan[:, 16 + n], chan[:, 16 + n], act_t[:, 4 + n], ALU.mult).then_inc(bx_ready, 1)

            for h in range(H):
                pool.wait_ge(d_ready, h + 1)
                link(pool.tensor_scalar(qkt[:, h], a_m[:, h], 0.0, None, ALU.min))
                pool.tensor_scalar(a_m[:, h], a_m[:, h], 0.0, None, ALU.max).then_inc(split_ready, 1)
            for h in range(H):
                pool.wait_ge(decay_ready, 3 * h + 2)
                link(pool.affine_select(out=quart(a_m[:, h]), in_=quart(a_m[:, h]), compare_op=ALU.is_ge, fill=0.0,
                                        base=-1, pattern=[[0, 4], [-1, P]], channel_multiplier=1))
                link(pool.tensor_tensor(quart(a_m[:, h]), quart(a_m[:, h]),
                                        beta[:, 4 * h:4 * h + 4].unsqueeze(2).to_broadcast([P, 4, P]), ALU.mult))
                pool.affine_select(out=quart(qkt[:, h]), in_=quart(qkt[:, h]), compare_op=ALU.is_ge, fill=0.0,
                                   base=0, pattern=[[0, 4], [1, P]], channel_multiplier=-1).then_inc(masked_ready, 1)
                pool.wait_ge(decay_ready, 3 * h + 3)
                pool.wait_ge(kk_done, 4 * h + 2)
                link(pool.tensor_tensor(chan[:, h], chan[:, h], q_m[:, h % 2], ALU.mult))
                pool.tensor_copy(elast[:, 4 * h:4 * h + 4].unsqueeze(2), quart(q_m[:, h % 2])[:, :, P - 1:P]).then_inc(qexp_ready, 1)

            pool.wait_ge(kk_evac, 4 * H)
            for l in range(7):
                for h in range(H):
                    i = 4 * l + h
                    if l == 0 and h >= 2:
                        pool.wait_ge(x1_ready, h - 1)
                    if l > 0:
                        if i - 4 >= 2:
                            pool.wait_ge(qm_done, i - 5)
                        else:
                            pool.wait_ge(x1_ready, H)
                    pool.tensor_tensor(quart(as_m[:, i % 2]), quart(a_m[:, h]),
                                       lmask[:, l:l + 1, :].to_broadcast([P, 4, P]), ALU.mult).then_inc(as_ready, 1)

            for h in range(H):
                pool.wait_ge(onorm_ready, h + 1)
                link(pool.tensor_scalar(q_m[:, h % 2], q_m[:, h % 2], par[:, R_DN:R_DN + 1], None, ALU.mult))
                pool.tensor_tensor(chan[:, 12 + h], chan[:, 12 + h], q_m[:, h % 2], ALU.mult).then_inc(dn_done, 1)

            pool.wait_ge(co_mm, 1)
            it_i = extra[:, 0, :].bitcast(I32)
            ef = extra[:, 1, :]
            link(pool.iota(it_i[:, 0:E], pattern=[[1, E]], base=0, channel_multiplier=0))
            link(pool.iota(it_i[:, 64:80], pattern=[[4 * P, 4], [1, 4]], base=0, channel_multiplier=4))
            link(pool.iota(it_i[:, 96:99], pattern=[[P, 3]], base=P, channel_multiplier=0))
            link(pool.iota(it_i[:, 128:224], pattern=[[4, E], [1, 3]], base=1 - E * CAP, channel_multiplier=0))
            link(pool.iota(it_i[:, 224:224 + N_MORE], pattern=[[1, N_MORE]], base=0, channel_multiplier=0))
            link(pool.tensor_copy(ef[:, 0:E], it_i[:, 0:E]))
            link(pool.tensor_scalar(ef[:, 32:64], ef[:, 0:E], float(CAP * P), None, ALU.mult))
            link(pool.tensor_copy(ef[:, 96:99], it_i[:, 96:99]))
            link(pool.tensor_copy(ef[:, 128:224 + N_MORE], it_i[:, 128:224 + N_MORE]))
            link(pool.affine_select(out=extra[:, 2, 0:P], in_=ones[:], compare_op=ALU.is_ge, fill=0.0, base=-1,
                                    pattern=[[1, P]], channel_multiplier=-1))
            link(pool.memset(extra[:, 3, 500:501], 0.0))
            pool.iota(codes[0:1, 0:E], pattern=[[CAP, E]], base=0, channel_multiplier=0).then_inc(iota_ready, 1)
            pool.wait_ge(co_mm, 8)
            pool.memset(xg[:], 0.0).then_inc(xg_clear, 1)

            pool.wait_ge(places_init, 16)
            pool.wait_ge(slot_ready, 1)
            for c in range(NT * TOPK):
                pool.indirect_dma_start(out=places, out_offset=bass.IndirectOffsetOnAxis(ap=it_i[:, 256 + c:257 + c], axis=0),
                                        in_=it_i[:, 64 + c:65 + c], in_offset=None,
                                        bounds_check=E * CAP * P - 1, oob_is_err=False).then_inc(placed, 16)
            pool.wait_ge(xg_clear, 1)
            pool.wait_ge(placed, 16 * NT * TOPK)
            pool.wait_ge(hn_out[0], 16 * (NT // 2))
            pool.wait_ge(hn_out[1], 16 * (NT // 2))
            pool.wait_ge(codes_ready, 1)

            def stand(i):
                return pool.tensor_tensor(guard[:, i:i + 1], guard[:, 0:1], guard[:, 0:1], ALU.mult)

            def gather():
                pool.indirect_dma_start(out=xg[:], out_offset=None, in_=hn_rows,
                                        in_offset=bass.IndirectOffsetOnAxis(ap=idx[:, 0:1], axis=0),
                                        bounds_check=T - 1, oob_is_err=False).then_inc(xg_in, 16)

            pool.wait_ge(tab_step, 2)
            pool.indirect_dma_start(out=blk_i, out_offset=None, in_=places_by_block,
                                    in_offset=bass.IndirectOffsetOnAxis(ap=codes_col, axis=0),
                                    bounds_check=E * CAP, oob_is_err=False).then_inc(blk_in, 16)
            pool.wait_ge(tab_step, 4)

            def take(col, table, at):
                return pool.tensor_tensor(idx[:, col:col + 1], table[:, at], zero_i, ALU.add)

            for c in range(2):
                if c > 0:
                    pool.wait_ge(xgt_done, c)
                link(take(0, tok_tab, slice(c, c + 1)))
                gather()
            take(1, row_tab, slice(0, 1)).then_inc(row_ready, 1)
            n_blocks = pool.value_load(nblocks[0:1, 0:1], min_val=E, max_val=MAXB - 3)
            with pool.Fori(0, n_blocks) as n:
                pool.wait_ge(xgt_done, n + 2)
                stand(4)
                take(0, tok_tab, bass.ds(n + 2, 1)).then_inc(stood, 1)
                pool.wait_ge(stood, n + 2)
                stand(1)
                gather()
                pool.wait_ge(y_ready, n * 2 + 2)
                stand(2)
                pool.wait_ge(row_ready, n + 1)
                stand(3)
                pool.indirect_dma_start(out=y_rows, out_offset=bass.IndirectOffsetOnAxis(ap=idx[:, 1:2], axis=0),
                                        in_=y_sb[:], in_offset=None, bounds_check=N_ROW - 1,
                                        oob_is_err=False).then_inc(y_out, 16)
                pool.wait_ge(y_out, n * 16 + 16)
                stand(5)
                take(1, row_tab, bass.ds(n + 1, 1)).then_inc(row_ready, 1)

        @block.scalar
        def _(act):
            chain = [0]

            def link(ins):
                chain[0] += 1
                ins.then_inc(act_c, 1)
                act.wait_ge(act_c, chain[0])

            act.wait_ge(par_clear, 1)

            def row(dst, src):
                act.dma_start(par_rows[dst:dst + src.shape[0], :], src).then_inc(par_in, 16)

            row(R_DCONV, dn_conv[0].rearrange("k (j p) -> (k j) p", p=P))
            row(R_RCONV, rg_conv[0].rearrange("k (j p) -> (k j) p", p=P))
            row(R_RCB, rg_conv_b[0].rearrange("(j p) -> j p", p=P))
            row(R_BA, rg_b_a[0])
            row(R_BX, rg_b_x[0])
            row(R_LAM, rg_lambda[0].rearrange("(j p) -> j p", p=P))
            row(R_DN, dn_norm)
            row(R_MIX, norm_mix[0].rearrange("(j p) -> j p", p=P))
            row(R_CROSS, norm_cross[0].rearrange("(j p) -> j p", p=P))
            row(R_MEM, norm_mem[0].rearrange("(j p) -> j p", p=P))
            row(R_MOE, norm_moe[0].rearrange("(j p) -> j p", p=P))
            act.dma_start(w_ba[:], w_in[0].rearrange("(k p) n -> p k n", p=P)[:, :, C_BA:C_BA + 2 * H]).then_inc(ba_in, 16)
            act.dma_start(dtb, dn_dt_bias.to_broadcast([P, H])).then_inc(small_in, 16)
            act.dma_start(alog, dn_a_log.to_broadcast([P, H])).then_inc(small_in, 16)
            act.dma_start(brt[:], b_router.to_broadcast([P, E])).then_inc(small_in, 16)
            act.dma_start(w_rt[:], w_router[0].rearrange("(k p) n -> p k n", p=P)).then_inc(small_in, 16)
            act.dma_start(gain_moe[:].rearrange("p (h k) -> p h k", h=2),
                          norm_moe[0].rearrange("(h p k) -> p h k", h=2, p=P)).then_inc(small_in, 16)
            for i, b in enumerate((b_gate, b_up, b_down)):
                act.dma_start(extra[0:E, 2 * i:2 * i + 2, :].rearrange("p a t -> p (a t)"), b[0]).then_inc(bias_in, 16)

            def norm_rows(src, s, waits=()):
                for w in waits:
                    act.wait_ge(*w)
                if s >= 2:
                    act.wait_ge(tr_done, 2 * (s - 1))
                link(act.activation(xn[:, s % 2], src, ACT.Square, accum_out=ss[:, s:s + 1]))
                act.activation(rms[:, s:s + 1], ss[:, s:s + 1], ACT.Sqrt, scale=1.0 / D, bias=eps_t).then_inc(stat_ready, 1)
                act.wait_ge(rstd_ready, s + 1)
                act.activation(xn[:, s % 2], src, ACT.Copy, scale=rstd[:, s:s + 1]).then_inc(xn_ready, 1)

            act.wait_ge(par_clear, 2)
            for t in range(NT):
                norm_rows(resid[:, t], t, [(x_in[t], 16)])

            act.wait_ge(sp_ready, 1)
            act.activation(sp_e, sp_s, ACT.Exp, scale=-1.0).then_inc(exp_small, 1)
            act.wait_ge(small_in, 16 * 5)
            act.activation(alog, alog, ACT.Exp).then_inc(exp_small, 1)
            act.wait_ge(sp_ready, 2)
            act.activation(beta, beta, ACT.Sigmoid).then_inc(beta_ready, 1)

            def tap(j, r, nj, bias):
                act.wait_ge(proj_done, j + 1)
                c = r + 3 * nj + (j if nj == 12 else j - 16)
                w3 = par[:, c:c + 1]
                if bias is None:
                    act.activation(chan[:, j], ps[:, j % 6], ACT.Copy, scale=w3).then_inc(tap_ready, 1)
                else:
                    act.activation(chan[:, j], ps[:, j % 6], ACT.Identity, scale=w3, bias=bias).then_inc(tap_ready, 1)

            def sigmoid_of(j):
                act.wait_ge(tile_done, j + 1)
                if j >= 2:
                    act.wait_ge(silu_done, j - 1)
                act.activation(extra[:, 4 + j % 2], chan[:, j], ACT.Sigmoid).then_inc(sig_ready, 1)

            def square_of(j):
                act.wait_ge(silu_done, j + 1)
                if j == 0:
                    act.wait_ge(bias_out, 16)
                act.activation(chan[:, 16 + j], chan[:, j], ACT.Square).then_inc(sq_ready, 1)

            def sums_of(j):
                act.wait_ge(l2_done, j + 1)
                act.activation(chan[:, 16 + j], ps[:, 6 + j % 2], ACT.Copy).then_inc(l2_evac, 1)

            for j in range(24):
                if j < 12:
                    if j == 0:
                        act.wait_ge(par_ready, 1)
                    tap(j, R_DCONV, 12, None)
                if 1 <= j <= 12:
                    if j == 1:
                        act.wait_ge(bias_out, 16)
                    sigmoid_of(j - 1)
                if 12 <= j < 16:
                    act.wait_ge(proj_done, j + 1)
                    act.wait_ge(silu_done, min(j - 1, 12))
                    if j - 2 >= 12:
                        act.wait_ge(tile_done, j - 1)
                    act.activation(extra[:, 4 + j % 2], ps[:, j % 6], ACT.Sigmoid).then_inc(sig_ready, 1)
                if j == 16:
                    act.wait_ge(l2_evac, 8)
                    act.activation(chan[:, 16:20], chan[:, 16:20], ACT.Sqrt, scale=float(P), bias=sp_in[:, 0:1]).then_inc(norm_ready, 1)
                    act.activation(chan[:, 20:24], chan[:, 20:24], ACT.Sqrt, bias=eps_t).then_inc(norm_ready, 1)
                if 16 <= j < 20:
                    act.wait_ge(qk_ready, 2)
                    tap(j, R_RCONV, 4, par[:, R_RCB + j - 16:R_RCB + j - 15])
                if j >= 20:
                    act.wait_ge(proj_done, j + 1)
                    if j >= 22:
                        act.wait_ge(tile_done, j - 1)
                    act.activation(extra[:, 6 + j % 2], ps[:, j % 6], ACT.Square).then_inc(y2_ready, 1)
                    act.wait_ge(yt_ready, j - 19)
                    act.activation(extra[:, 6 + j % 2], extra[:, 6 + j % 2], ACT.Tanh, scale=GELU_C).then_inc(tanh_ready, 1)
                if 2 <= j < 10:
                    square_of(j - 2)
                if 6 <= j < 14:
                    sums_of(j - 6)

            act.wait_ge(proj_done, 24)
            for n in range(4):
                for g in range(2):
                    act.wait_ge(gate_mm, 2 * n + g + 1)
                    r = (R_BA if g == 0 else R_BX) + n
                    act.activation(act_t[:, 4 * g + n], ps[:, 6 + g], ACT.Sigmoid, bias=par[:, r:r + 1]).then_inc(ri_ready, 1)
            act.wait_ge(ri_ready, 8)
            for n in range(4):
                act.wait_ge(bx_ready, n + 1)
                act.activation(act_t[:, 4 + n], act_t[:, n], ACT.Tanh, scale=nrate[:, n:n + 1]).then_inc(rt_ready, 1)
            act.wait_ge(rt_ready, 4)
            for n in range(4):
                act.activation(act_t[:, n], act_t[:, n], ACT.Exp, scale=rate[:, n:n + 1]).then_inc(rt_ready, 1)

            act.wait_ge(gp_ready, 1)
            act.activation(egp, gp, ACT.Exp).then_inc(kdf_ready, 1)
            for h in range(H):
                act.wait_ge(split_ready, h + 1)
                act.activation(a_m[:, h], a_m[:, h], ACT.Exp, scale=-1.0).then_inc(decay_ready, 1)
                act.activation(qkt[:, h], qkt[:, h], ACT.Exp).then_inc(decay_ready, 1)
                act.wait_ge(kd_in, h + 1)
                if h >= 2:
                    act.wait_ge(qexp_ready, h - 1)
                act.activation(q_m[:, h % 2], ps[:, h], ACT.Exp).then_inc(decay_ready, 1)
                if h == 1:
                    act.wait_ge(kd_in, H)
                    act.activation(kdf, kdf, ACT.Exp).then_inc(kdf_ready, 1)
                    act.wait_ge(mult_in, 1)
                    act.activation(act_t[:, 4:8], act_t[:, 4:8], ACT.Sqrt, scale=2.0).then_inc(mult_ready, 1)

            for h in range(H):
                act.wait_ge(x1t_done, h + 1)
                if h == 0:
                    act.wait_ge(rg_done, 1)
                act.activation(y_m[:, h], ps[:, h], ACT.Copy).then_inc(y1_ready, 1)
            for i in range(24):
                act.wait_ge(qm_done, i + 1)
                if i >= 2:
                    act.wait_ge(p_done, i - 1)
                else:
                    act.wait_ge(qexp_ready, H)
                act.activation(q_m[:, i % 2], ps[:, 3 * (i % 2)], ACT.Copy).then_inc(qm_ready, 1)
            for h in range(H):
                act.wait_ge(wt_done, h + 1)
                act.activation(chan[:, 4 + h], ps[:, 6 + h % 2], ACT.Copy, scale=-1.0).then_inc(wt_ready, 1)
            for c in range(NT):
                for h in range(H):
                    act.wait_ge(vn_done, 4 * c + h + 1)
                    if c > 0:
                        act.wait_ge(o_done, 4 * (c - 1) + h + 1)
                    act.activation(vnew[:, h * P:(h + 1) * P], ps[:, h % 2, 0:P], ACT.Copy).then_inc(vn_ready, 1)
            for h in range(H):
                act.wait_ge(o_done, 4 * (NT - 1) + h + 1)
                if h >= 2:
                    act.wait_ge(dn_done, h - 1)
                act.activation(q_m[:, h % 2], ps[:, 4 + h], ACT.Square).then_inc(osq_ready, 1)
                act.wait_ge(oss_done, h + 1)
                act.activation(q_m[:, h % 2], ps[:, h % 2], ACT.Sqrt, scale=1.0 / P, bias=eps_t).then_inc(orms_ready, 1)

            s = NT
            memf = chan[:, 0:4, :].rearrange("p a t -> p (a t)").rearrange("p (m d) -> p m d", m=MT)
            for m in range(MT):
                norm_rows(memf[:, m], s, [(mem_in, 16)] + ([(dn_done, H)] if m == 0 else []))
                s += 1
            for i in range(8):
                act.wait_ge(mk_mm, i + 1)
                act.activation(extra[:, 0:4, :].rearrange("p a t -> p (a t)")[:, i * M:(i + 1) * M], ps[:, i % 4, 0:M], ACT.Copy).then_inc(mk_evac, 1)
            for i in range(4):
                act.wait_ge(mk_mm, 9 + i)
                act.activation(extra[:, 4 + i], ps[:, i % 4], ACT.Copy).then_inc(mk_evac, 1)
            for t in range(NT):
                norm_rows(resid[:, t], s, [(h1_ready, 2 * t + 2)])
                s += 1
            for i in range(8):
                act.wait_ge(q_mm, i + 1)
                act.activation(chan[:, i], ps[:, i % 4], ACT.Copy).then_inc(q_evac, 1)
            def pt_copies(t):
                for b in range(2):
                    act.wait_ge(pt_mm, 2 * t + b + 1)
                    act.activation(chan[:, 8 + 4 * b:12 + 4 * b, t * P:(t + 1) * P], quarters(4 + b), ACT.Copy).then_inc(pt_evac, 1)

            for t in range(NT):
                act.wait_ge(mx_ready, t + 1)
                if t >= 2:
                    act.wait_ge(pt_mm, 2 * (t - 1))
                pr = xn[:, t % 2].rearrange("p (h m) -> p h m", h=XH)
                scv = ps[:, 2 * (t % 2):2 * (t % 2) + 2, :].rearrange("p b (g m) -> p (b g) m", g=2)
                for h in range(XH):
                    c = 4 * (t % 2) + h
                    act.activation(pr[:, h], scv[:, h], ACT.Exp, scale=XD ** -0.5, bias=nmx[:, c:c + 1],
                                   accum_out=rsum[:, c:c + 1]).then_inc(ex_ready, 1)
                if t >= 1:
                    pt_copies(t - 1)
            pt_copies(NT - 1)
            for i in range(8):
                act.wait_ge(o_mm, i + 1)
                act.activation(chan[:, 16 + i], ps[:, 6 + i % 2], ACT.Copy).then_inc(o_evac, 1)
            for t in range(NT):
                norm_rows(resid[:, t], s, [(h2_ready, 2 * t + 2)] + ([(hn_out[s % 2], 16 * (t // 2))] if t >= 2 else []))
                act.wait_ge(xn_ready, s + 1)
                act.dma_start(hn_rows[t * P:(t + 1) * P, :], xn[:, s % 2]).then_inc(hn_out[s % 2], 16)
                s += 1
            act.wait_ge(top_ready, 1)
            act.activation(gates[:], gates[:], ACT.Exp).then_inc(gexp_ready, 1)

            act.wait_ge(codes_ready, 1)
            n_blocks = act.value_load(nblocks[0:1, 0:1], min_val=E, max_val=MAXB - 3)

            def hi(c, block=None):
                k = c % KT if c < GU else HALF + c - GU
                m = (GM + c // KT) % 3
                s = 2 * m + k // HALF
                if c % HALF == 0:
                    act.wait_ge(w_in_slot[s], base[m] + 16 if block is None else block * 16 + (base[m] + 16))
                if block is not None:
                    act.wait_ge(split_used, block * SPLIT + (c - NSPLIT + 1))
                act.activation(wsp[:, c % NSPLIT, 0], ring[:, m, k], ACT.Copy).then_inc(hi_ready, 1)

            for c in range(NSPLIT):
                hi(c)
            act.wait_ge(xt_ready, 1)
            act.activation(x_hi[:], gt[:], ACT.Copy).then_inc(xhi_ready, 1)
            with act.Fori(0, n_blocks) as n:
                for c in range(NSPLIT, 12):
                    hi(c, n)
                act.wait_ge(gt_ready, n + 1)
                act.activation(sig_e[:], gt[:], ACT.Sigmoid, scale=1.702).then_inc(sg_ready, 1)
                for c in range(12, SPLIT):
                    hi(c, n)
                act.wait_ge(hidt_done, n * 2 + 1)
                act.activation(hid_t[:], ps[:, 0], ACT.Copy).then_inc(hidt_ready, 1)
                act.wait_ge(hidt_done, n * 2 + 2)
                act.activation(hid_hi[:], ps[:, 1], ACT.Copy).then_inc(hidhi_ready, 1)
                act.wait_ge(xt_ready, n + 2)
                act.activation(x_hi[:], gt[:], ACT.Copy).then_inc(xhi_ready, 1)
                for c in range(NSPLIT):
                    if c == 0:
                        act.wait_ge(w_in_slot[2 * GM], n * 16 + (base[GM] + 32))
                    act.wait_ge(split_used, n * SPLIT + (SPLIT + c - NSPLIT + 1))
                    act.activation(wsp[:, c, 0], ring[:, GM, c], ACT.Copy).then_inc(hi_ready, 1)
                act.wait_ge(row_ready, n + 1)
                for i in range(2):
                    act.wait_ge(*((down_done, n + 1) if i == 0 else (split_used, n * SPLIT + SPLIT)))
                    act.activation(y_sb[:, i * 512:(i + 1) * 512], ps[:, 4 + i], ACT.Copy).then_inc(y_ready, 1)
            for t in range(NT):
                act.wait_ge(comb_ready, t + 1)
                if t >= 2:
                    act.wait_ge(stat_ready, 14 + t - 1)
                act.activation(xn[:, t % 2], resid[:, t], ACT.Square, accum_out=ss[:, t:t + 1]).then_inc(stat_ready, 1)
            act.wait_ge(stat_ready, 14 + NT)
            act.activation(rms[:, 0:4], ss[:, 0:4], ACT.Sqrt, scale=1.0 / D, bias=eps_t).then_inc(stat_ready, 1)

        @block.tensor
        def _(pe):
            pe.wait_ge(consts_ready, 3)
            pe.wait_ge(par_in, 16 * 11)
            pe.transpose(ps[:, 7, 0:P], par_rows[:], ident[:]).then_inc(par_t, 1)

            def transposes(s):
                pe.wait_ge(xn_ready, s + 1)
                for b in range(2):
                    bank = 2 * (s % 2) + 4 + b
                    if s >= 2:
                        pe.wait_ge(tr_evac, 2 * (s - 2) + b + 1)
                    elif s == 1:
                        pe.wait_ge(par_ready, 1)
                    for k in range(4):
                        last = pe.transpose(quarters(bank)[:, k], xn[:, s % 2, (4 * b + k) * P:(4 * b + k + 1) * P], ident[:])
                    last.then_inc(tr_done, 1)

            for t in range(NT):
                transposes(t)
            pe.wait_ge(tr_evac, 2 * NT)
            pe.wait_ge(ba_in, 16)
            for t in range(NT):
                for k in range(KT):
                    last = pe.matmul(ps[:, 7, 8 * t:8 * t + 8], act_t[:, k, t * P:(t + 1) * P], w_ba[:, k], start=(k == 0), stop=(k == KT - 1))
            last.then_inc(ba_done, 1)

            for j in range(24):
                m, c = j // 8, j % 8
                if c == 0:
                    pe.wait_ge(w_in_slot[2 * (m % 3)], 16 * (m // 3 + 1))
                    pe.wait_ge(w_in_slot[2 * (m % 3) + 1], 16 * (m // 3 + 1))
                if j >= 6:
                    pe.wait_ge(tile_done, j - 5)
                for k in range(KT):
                    last = pe.matmul(ps[:, j % 6], slot_w(m, k)[:, c * P:(c + 1) * P], act_t[:, k], start=(k == 0), stop=(k == KT - 1))
                last.then_inc(proj_done, 1)
                if j == 2:
                    pe.wait_ge(g_ready, 1)
                    pe.matmul(ps[:, 7, 64:80], tri[:], g_t, start=True, stop=True).then_inc(gp_done, 1)
                if 5 <= j < 13:
                    i = j - 5
                    pe.wait_ge(sq_ready, i + 1)
                    if i >= 2:
                        pe.wait_ge(l2_evac, i - 1)
                    elif i == 1:
                        pe.wait_ge(gp_ready, 1)
                    pe.matmul(ps[:, 6 + i % 2], ones[:], chan[:, 16 + i], start=True, stop=True).then_inc(l2_done, 1)

            pe.wait_ge(rgw_in, 32)
            pe.wait_ge(tile_done, 20)
            for n in range(4):
                for g in range(2):
                    if n > 0:
                        pe.wait_ge(ri_ready, 2 * (n - 1) + g + 1)
                    pe.matmul(ps[:, 6 + g], rgw[:, g, n], chan[:, 16 + n], start=True, stop=True).then_inc(gate_mm, 1)

            pe.wait_ge(tile_done, 24)
            for h in range(H):
                pe.wait_ge(gu_ready, h + 1)
                pe.matmul(ps[:, h], ones[:], as_m[:, h % 2], start=True, stop=True).then_inc(gb_done, 1)

            pe.wait_ge(qk_ready, 2)
            for h in range(H):
                for w in range(4):
                    if h > 0:
                        pe.wait_ge(kk_evac, 4 * (h - 1) + w + 1)
                    elif w == 2:
                        pe.wait_ge(ri_ready, 8)
                    for c in range(4):
                        kc = chan[:, 4 + h, c * P:(c + 1) * P]
                        o = quarters(4 + w)[:, c]
                        if w == 0:
                            last = pe.matmul(o, kc, kc, start=True, stop=True)
                        elif w == 1:
                            last = pe.matmul(o, kc, chan[:, h, c * P:(c + 1) * P], start=True, stop=True)
                        elif w == 2:
                            last = pe.transpose(o, kc, ident[:])
                        else:
                            last = pe.transpose(o, chan[:, 8 + h, c * P:(c + 1) * P], ident[:])
                    last.then_inc(kk_done, 1)

            pe.wait_ge(decay_ready, 3 * H)
            for h in range(H):
                pe.wait_ge(x1_ready, h + 1)
                for c in range(4):
                    last = pe.transpose(quarters(h)[:, c], quart(x_m[:, h])[:, c], ident[:])
                last.then_inc(x1t_done, 1)

            def level_q(i):
                h = i % 4
                pe.wait_ge(as_ready, 4 + i + 1)
                if i < 4:
                    pe.wait_ge(y1_ready, 4)
                else:
                    pe.wait_ge(y_lev, i - 3)
                for c in range(4):
                    last = pe.matmul(quarters(3 * (i % 2))[:, c], quart(as_m[:, i % 2])[:, c], quart(y_m[:, h])[:, c], start=True, stop=True)
                last.then_inc(qm_done, 1)

            def level_p(i):
                h = i % 4
                pe.wait_ge(qm_ready, i + 1)
                if i >= 2:
                    pe.wait_ge(y_lev, i - 1)
                    pe.wait_ge(x_lev, min(i - 1, 20))
                for c in range(4):
                    qc, xc = quart(q_m[:, i % 2])[:, c], quart(x_m[:, h])[:, c]
                    last = pe.matmul(quarters(3 * (i % 2) + 1)[:, c], xc, qc, start=True, stop=True)
                    if i < 20:
                        last = pe.matmul(quarters(3 * (i % 2) + 2)[:, c], qc, xc, start=True, stop=True)
                last.then_inc(p_done, 1)

            for i in range(25):
                if i < 24:
                    level_q(i)
                if i >= 1:
                    level_p(i - 1)

            for h in range(H):
                pe.wait_ge(y_lev, 20 + h + 1)
                if h >= 2:
                    pe.wait_ge(wt_ready, h - 1)
                for c in range(4):
                    last = pe.matmul(quarters(6 + h % 2)[:, c], quart(chan[:, 4 + h])[:, c], quart(y_m[:, h])[:, c], start=True, stop=True)
                last.then_inc(wt_done, 1)
            pe.wait_ge(wt_ready, 4)

            for c in range(NT):
                for h in range(H):
                    i = 4 * c + h
                    if i >= 2:
                        pe.wait_ge(vn_ready, i - 1)
                    if c > 0:
                        pe.wait_ge(s_ready, 4 * (c - 1) + h + 1)
                    o = ps[:, h % 2, 0:P]
                    last = pe.matmul(o, quart(y_m[:, h])[:, c], quart(chan[:, 8 + h])[:, c], start=True, stop=(c == 0))
                    if c > 0:
                        last = pe.matmul(o, quart(chan[:, 4 + h])[:, c], state[:, h * P:(h + 1) * P], start=False, stop=True)
                    last.then_inc(vn_done, 1)
                for h in range(H):
                    i = 4 * c + h
                    vn = vnew[:, h * P:(h + 1) * P]
                    pe.wait_ge(vn_ready, i + 1)
                    o = quarters(4 + h)[:, c]
                    if c > 0:
                        pe.matmul(o, state[:, h * P:(h + 1) * P], quart(chan[:, h])[:, c], start=True, stop=False)
                    pe.matmul(o, vn, quart(qkt[:, h])[:, c], start=(c == 0), stop=True).then_inc(o_done, 1)
                    if c < NT - 1:
                        if i >= 2:
                            pe.wait_ge(s_ready, i - 1)
                        pe.matmul(ps[:, 2 + h % 2, 0:P], quart(kdec[:, h])[:, c], vn, start=True, stop=True).then_inc(s_done, 1)
            for h in range(H):
                pe.wait_ge(osq_ready, h + 1)
                if h >= 2:
                    pe.wait_ge(orms_ready, h - 1)
                pe.matmul(ps[:, h % 2], ones[:], q_m[:, h % 2], start=True, stop=True).then_inc(oss_done, 1)

            def into_resid(m, tile_of, done, ready, first):
                pe.wait_ge(w_in_slot[2 * (m % 3)], 16 * (m // 3 + 1))
                pe.wait_ge(w_in_slot[2 * (m % 3) + 1], 16 * (m // 3 + 1))
                for w in first:
                    pe.wait_ge(*w)
                for g in range(8):
                    t, n = g // 2, g % 2
                    if g >= 4:
                        pe.wait_ge(ready, g - 3)
                    for k in range(KT):
                        last = pe.matmul(ps[:, g % 4], tile_of(k)[:, t * P:(t + 1) * P], slot_w(m, k)[:, n * 512:(n + 1) * 512],
                                         start=(k == 0), stop=(k == KT - 1))
                    last.then_inc(done, 1)

            into_resid(W_OUT, lambda k: chan[:, 12 + k] if k < 4 else chan[:, 16 + k], out_mm, h1_ready,
                       [(dn_done, H), (rg_done, 1)])

            for m in range(MT):
                transposes(NT + m)
            mem_t = chan[:, 4:8, :].rearrange("p a t -> p (a t)").rearrange("p (k m) -> p k m", k=KT)
            pe.wait_ge(tr_evac, 2 * (NT + MT))
            pe.wait_ge(w_in_slot[2 * (W_CK % 3)], 16 * (W_CK // 3 + 1))
            pe.wait_ge(w_in_slot[2 * (W_CK % 3) + 1], 16 * (W_CK // 3 + 1))
            for i in range(8):
                if i >= 4:
                    pe.wait_ge(mk_evac, i - 3)
                else:
                    pe.wait_ge(h1_ready, i + 5)
                for k in range(KT):
                    last = pe.matmul(ps[:, i % 4, 0:M], slot_w(W_CK, k)[:, i * P:(i + 1) * P], mem_t[:, k], start=(k == 0), stop=(k == KT - 1))
                last.then_inc(mk_mm, 1)
            pe.wait_ge(w_in_slot[2 * (W_CV % 3)], 16 * (W_CV // 3 + 1))
            pe.wait_ge(w_in_slot[2 * (W_CV % 3) + 1], 16 * (W_CV // 3 + 1))
            for i in range(4):
                pe.wait_ge(mk_evac, i + 5)
                for k in range(KT):
                    last = pe.matmul(ps[:, i % 4], mem_t[:, k, (i // 2) * P:(i // 2 + 1) * P], slot_w(W_CV, k)[:, (i % 2) * 512:(i % 2 + 1) * 512],
                                     start=(k == 0), stop=(k == KT - 1))
                last.then_inc(mk_mm, 1)

            s = NT + MT
            for t in range(NT):
                transposes(s)
                s += 1
            pe.wait_ge(tr_evac, 2 * s)
            pe.wait_ge(w_in_slot[2 * (W_CQ % 3)], 16 * (W_CQ // 3 + 1))
            pe.wait_ge(w_in_slot[2 * (W_CQ % 3) + 1], 16 * (W_CQ // 3 + 1))
            for i in range(8):
                pe.wait_ge(mk_evac, 9 + i) if i < 4 else pe.wait_ge(q_evac, i - 3)
                for k in range(KT):
                    last = pe.matmul(ps[:, i % 4], slot_w(W_CQ, k)[:, i * P:(i + 1) * P], act_t[:, k], start=(k == 0), stop=(k == KT - 1))
                last.then_inc(q_mm, 1)

            kt_m = extra[:, 0:4, :].rearrange("p a t -> p (a t)").rearrange("p (i m) -> p i m", i=8)
            v_m = extra[:, 4:8, :].rearrange("p a t -> p (a t)").rearrange("p (m d) -> p m d", m=MT)
            pe.wait_ge(q_evac, 8)

            def prob_transposes(t):
                pe.wait_ge(p_ready, t + 1)
                for b in range(2):
                    if t >= 1:
                        pe.wait_ge(pt_evac, 2 * (t - 1) + b + 1)
                    for i in range(4):
                        c = 4 * b + i
                        last = pe.transpose(quarters(4 + b)[:, i], xn[:, t % 2, c * P:(c + 1) * P], ident[:])
                    last.then_inc(pt_mm, 1)

            for t in range(NT):
                if t >= 2:
                    pe.wait_ge(ex_ready, 4 * (t - 1))
                for h in range(XH):
                    o = ps[:, 2 * (t % 2) + h // 2, (h % 2) * M:(h % 2 + 1) * M]
                    for k in range(2):
                        last = pe.matmul(o, chan[:, 2 * h + k, t * P:(t + 1) * P], kt_m[:, 2 * h + k], start=(k == 0), stop=(k == 1))
                last.then_inc(sc_mm, 1)
                if t >= 1:
                    prob_transposes(t - 1)
            prob_transposes(NT - 1)
            pe.wait_ge(pt_evac, 2 * NT)
            for i in range(8):
                if i >= 2:
                    pe.wait_ge(o_evac, i - 1)
                for m in range(2):
                    last = pe.matmul(ps[:, 6 + i % 2], v_m[:, m, i * P:(i + 1) * P], chan[:, 8 + 2 * (i // 2) + m], start=(m == 0), stop=(m == 1))
                last.then_inc(o_mm, 1)
            into_resid(W_CO, lambda k: chan[:, 16 + k], co_mm, h2_ready, [(o_evac, 8)])

            for t in range(NT):
                transposes(s)
                s += 1
                pe.wait_ge(tr_evac, 2 * s)
                pe.wait_ge(h2_ready, 5)
                for k in range(KT):
                    last = pe.matmul(ps[:, 0, t * E:(t + 1) * E], act_t[:, k, t * P:(t + 1) * P], w_rt[:, k], start=(k == 0), stop=(k == KT - 1))
                last.then_inc(lg_mm, 1)
            pe.wait_ge(oh_ready, 1)
            mask = extra[:, 3, 0:NT * E].rearrange("p (t e) -> p t e", t=NT)
            for t in range(NT):
                for u in range(t + 1):
                    lhs = extra[:, 2, 0:P] if u == t else ones[:]
                    pe.matmul(ps[:, 1, t * E:(t + 1) * E], lhs, mask[:, u], start=(u == 0), stop=(u == t))
            for t in range(NT):
                last = pe.matmul(ps[:, 2, 0:E], ones[:], mask[:, t], start=(t == 0), stop=(t == NT - 1))
            last.then_inc(pos_mm, 1)

            def gathered_transposes():
                xgk = xg[:].rearrange("t (h p k) -> t h k p", h=2, k=HALF)
                for b in range(2):
                    for k in range(4):
                        last = pe.transpose(quarters(6 + b)[:, k], xgk[:, b, k], ident[:])
                last.then_inc(xgt_done, 1)

            pe.wait_ge(codes_ready, 1)
            n_blocks = pe.value_load(nblocks[0:1, 0:1], min_val=E, max_val=MAXB - 3)
            pe.wait_ge(tab_step, 1)
            pe.matmul(ps[0:MAXB, 3, 0:1], codes_f, ones[0:1, 0:1], start=True, stop=True).then_inc(tab_mm, 1)
            pe.wait_ge(tab_step, 3)
            pe.transpose(ps[:, 3, 0:MAXB], blk_f, ident[0:MAXB, 0:MAXB]).then_inc(tab_mm, 1)
            pe.wait_ge(xg_in, 16)
            gathered_transposes()
            d0, d1 = 2 * ((GM + 2) % 3), 2 * ((GM + 2) % 3) + 1
            with pe.Fori(0, n_blocks) as n:
                pe.wait_ge(bias3_in, n * 16 + 16)
                pe.wait_ge(xlo_ready, n + 1)
                for j in range(2):
                    for i in range(2):
                        pe.matmul(ps[:, 2 * j + i], ones3[:], bias3[:, j * D + i * 512:j * D + (i + 1) * 512], start=True, stop=False)
                    for k in range(KT):
                        c = KT * j + k
                        pe.wait_ge(lo_ready, n * SPLIT + (c + 1))
                        ks = slice(k * P, (k + 1) * P)
                        for xp, part in ((x_hi, 0), (x_hi, 1), (x_lo, 0)):
                            for i in range(2):
                                last = pe.matmul(ps[:, 2 * j + i], xp[:, ks], wsp[:, c % NSPLIT, part, i * 512:(i + 1) * 512],
                                                 start=False, stop=(k == KT - 1 and xp is x_lo))
                        last.then_inc(split_used, 1)
                pe.wait_ge(xg_in, n * 16 + 32)
                gathered_transposes()
                for i in range(2):
                    last = pe.matmul(ps[:, 4 + i], ones3[:], bias3[:, 2 * D + i * 512:2 * D + (i + 1) * 512], start=True, stop=False)
                last.then_inc(bias3_used, 1)
                hk = hid[:].rearrange("t (h p k) -> t h k p", h=2, k=HALF)
                for b in range(2):
                    pe.wait_ge(hid_ready, n * 2 + (b + 1))
                    for k in range(4):
                        last = pe.transpose(quarters(b)[:, k], hk[:, b, k], ident[:])
                    last.then_inc(hidt_done, 1)
                pe.wait_ge(w_in_slot[d0], n * 16 + (base[d0 // 2] + 16))
                pe.wait_ge(hidt_ready, n + 1)
                for k in range(HALF):
                    for i in range(2):
                        last = pe.matmul(ps[:, 4 + i], hid_t[:, k * P:(k + 1) * P],
                                         ring[:, d0 // 2, k, i * 512:(i + 1) * 512], start=False, stop=False)
                last.then_inc(down_half, 1)
                pe.wait_ge(hidlo_ready, n + 1)
                for k in range(HALF):
                    c = GU + k
                    pe.wait_ge(lo_ready, n * SPLIT + (c + 1))
                    for xp, part in ((hid_hi, 0), (hid_hi, 1), (hid_lo, 0)):
                        for i in range(2):
                            last = pe.matmul(ps[:, 4 + i], xp[:, k * P:(k + 1) * P], wsp[:, c % NSPLIT, part, i * 512:(i + 1) * 512],
                                             start=False, stop=(k == HALF - 1 and xp is hid_lo))
                            if k == HALF - 1 and xp is hid_lo and i == 0:
                                last.then_inc(down_done, 1)
                    last.then_inc(split_used, 1)

        @block.vector
        def _(dve):
            chain = [0]

            def link(ins):
                chain[0] += 1
                ins.then_inc(dve_c, 1)
                dve.wait_ge(dve_c, chain[0])

            dve.memset(par_rows[:], 0.0).then_inc(par_clear, 1)
            dve.memset(eps_t, EPS).then_inc(par_clear, 1)

            def recip_rms(s):
                dve.wait_ge(stat_ready, s + 1)
                dve.reciprocal(rstd[:, s:s + 1], rms[:, s:s + 1]).then_inc(rstd_ready, 1)

            def evac_t(s, gain, dst):
                for b in range(2):
                    dve.wait_ge(tr_done, 2 * s + b + 1)
                    g = par[:, gain + 4 * b:gain + 4 * b + 4].unsqueeze(2).to_broadcast([P, 4, P])
                    dve.tensor_tensor(dst(b), quarters(2 * (s % 2) + 4 + b), g, ALU.mult).then_inc(tr_evac, 1)

            dve.wait_ge(par_t, 1)
            dve.tensor_copy(par[:], ps[:, 7, 0:P]).then_inc(par_ready, 1)
            dve.wait_ge(par_ready, 1)
            dve.wait_ge(places_init, 16)
            for t in range(NT + 1):
                if t < NT:
                    recip_rms(t)
                if t >= 1:
                    evac_t(t - 1, R_MIX, lambda b: act_t[:, 4 * b:4 * b + 4, (t - 1) * P:t * P])

            bt = ps[:, 7, 0:32].rearrange("p (c w) -> p w c", c=4)
            dve.wait_ge(ba_done, 1)
            dve.wait_ge(small_in, 16 * 5)
            v3 = lambda a: a.rearrange("p (h c) -> p h c", h=4)
            dve.tensor_copy(v3(beta), bt[:, 0:4])
            dve.tensor_tensor(v3(sp_in[:, 0:16]), bt[:, 4:8], dtb.unsqueeze(2).to_broadcast([P, 4, 4]), ALU.add)
            link(dve.tensor_scalar(sp_in[:, 16:20], par[:, R_LAM:R_LAM + 4], -1.0, None, ALU.mult))
            dve.scalar_tensor_tensor(out=sp_s, in0=sp_in, scalar=-1.0, in1=sp_in, op0=ALU.mult, op1=ALU.max).then_inc(sp_ready, 1)
            dve.wait_ge(exp_small, 1)
            link(dve.tensor_scalar(sp_s, sp_e, 2.0, None, ALU.add))
            link(dve.reciprocal(sp_s, sp_s))
            link(dve.tensor_tensor(sp_s, sp_s, sp_e, ALU.mult))
            link(dve.tensor_tensor(sp_s2, sp_s, sp_s, ALU.mult))
            link(dve.tensor_scalar(sp_e, sp_s2, 1.0 / 17, None, ALU.mult))
            for d in (15, 13, 11, 9, 7, 5, 3):
                link(dve.scalar_tensor_tensor(out=sp_e, in0=sp_e, scalar=1.0 / d, in1=sp_s2, op0=ALU.add, op1=ALU.mult))
            link(dve.scalar_tensor_tensor(out=sp_e, in0=sp_e, scalar=1.0, in1=sp_s, op0=ALU.add, op1=ALU.mult))
            link(dve.tensor_scalar(sp_e, sp_e, 2.0, None, ALU.mult))
            link(dve.scalar_tensor_tensor(out=sp_e, in0=sp_in, scalar=0.0, in1=sp_e, op0=ALU.max, op1=ALU.add))
            link(dve.tensor_scalar(rate, sp_e[:, 16:20], -8.0, None, ALU.mult))
            link(dve.tensor_scalar(nrate, sp_e[:, 16:20], 8.0, None, ALU.mult))
            dve.wait_ge(exp_small, 2)
            dve.scalar_tensor_tensor(out=v3(g_t), in0=v3(sp_e[:, 0:16]), scalar=-1.0, in1=alog.unsqueeze(2).to_broadcast([P, 4, 4]),
                                     op0=ALU.mult, op1=ALU.mult).then_inc(g_ready, 1)
            dve.memset(sp_in[:, 0:1], P * EPS).then_inc(sp_ready, 1)

            for j in range(24):
                if j < 12 or 16 <= j < 20:
                    nj, r, jj = (12, R_DCONV, j) if j < 12 else (4, R_RCONV, j - 16)
                    dve.wait_ge(tap_ready, (j if j < 12 else j - 4) + 1)
                    for d in (1, 2, 3):
                        w = par[:, r + (3 - d) * nj + jj:][:, 0:1]
                        ins = dve.scalar_tensor_tensor(out=chan[:, j, d:], in0=ps[:, j % 6, 0:T - d], scalar=w,
                                                       in1=chan[:, j, d:], op0=ALU.mult, op1=ALU.add)
                        if d < 3:
                            link(ins)
                        else:
                            ins.then_inc(tile_done, 1)
                elif j < 16:
                    dve.wait_ge(sig_ready, j + 1)
                    dve.wait_ge(bias_out, 16)
                    dve.tensor_tensor(chan[:, j], ps[:, j % 6], extra[:, 4 + j % 2], ALU.mult).then_inc(tile_done, 1)
                else:
                    tb = extra[:, 6 + j % 2]
                    dve.wait_ge(y2_ready, j - 19)
                    link(dve.tensor_scalar(tb, tb, 0.044715, 1.0, ALU.mult, ALU.add))
                    dve.tensor_tensor(tb, tb, ps[:, j % 6], ALU.mult).then_inc(yt_ready, 1)
                    dve.wait_ge(tanh_ready, j - 19)
                    dve.scalar_tensor_tensor(out=chan[:, j], in0=tb, scalar=1.0, in1=ps[:, j % 6], op0=ALU.add, op1=ALU.mult).then_inc(tile_done, 1)
                if j == 2:
                    dve.wait_ge(gp_done, 1)
                    dve.tensor_copy(gp, ps[:, 7, 64:80]).then_inc(gp_ready, 1)
                if j == 15:
                    for i in range(2):
                        dve.wait_ge(norm_ready, i + 1)
                        link(dve.reciprocal(chan[:, 16 + 4 * i:20 + 4 * i], chan[:, 16 + 4 * i:20 + 4 * i]))
                        dve.tensor_tensor(chan[:, 4 * i:4 * i + 4], chan[:, 4 * i:4 * i + 4], chan[:, 16 + 4 * i:20 + 4 * i], ALU.mult).then_inc(qk_ready, 1)

            for h in range(H):
                dve.wait_ge(proj_done, 24)
                if h >= 2:
                    dve.wait_ge(gb_done, h - 1)
                dve.tensor_tensor(quart(as_m[:, h % 2]), tri[:].unsqueeze(1).to_broadcast([P, 4, P]),
                                  g_t[:, 4 * h:4 * h + 4].unsqueeze(2).to_broadcast([P, 4, P]), ALU.mult).then_inc(gu_ready, 1)
            for h in range(H):
                dve.wait_ge(gb_done, h + 1)
                dve.wait_ge(gp_ready, 1)
                g4 = gp[:, 4 * h:4 * h + 4].unsqueeze(2)
                dve.tensor_tensor(quart(a_m[:, h]), quarters(h), g4.to_broadcast([P, 4, P]), ALU.subtract).then_inc(d_ready, 1)
                dve.tensor_tensor(kdf[:, 4 * h:4 * h + 4].unsqueeze(2), quarters(h)[:, :, P - 1:P], g4, ALU.subtract).then_inc(kd_in, 1)

            four = extra[:, 0:4]
            dve.wait_ge(rt_ready, 4)
            link(dve.tensor_scalar(four, act_t[:, 4:8], 1.0, None, ALU.add))
            link(dve.reciprocal(four, four))
            dve.tensor_tensor(act_t[:, 4:8], act_t[:, 4:8], four, ALU.mult).then_inc(mult_in, 1)
            dve.wait_ge(mult_ready, 1)
            link(dve.memset(act_t[:, 4:8, 0:1], 1.0))
            link(dve.tensor_tensor(chan[:, 16:20], chan[:, 16:20], act_t[:, 4:8], ALU.mult))
            dve.wait_ge(rt_ready, 8)
            for n in range(4):
                last = dve.tensor_tensor_scan(four[:, n], act_t[:, n], chan[:, 16 + n], 0.0, ALU.mult, ALU.add)
            link(last)
            dve.scalar_tensor_tensor(out=chan[:, 20:24], in0=four, scalar=0.5, in1=chan[:, 20:24], op0=ALU.mult, op1=ALU.mult).then_inc(rg_done, 1)

            dve.wait_ge(beta_ready, 1)
            dve.wait_ge(kdf_ready, 2)
            link(dve.tensor_tensor(beg, beta, egp, ALU.mult))
            for h in range(H):
                bc = lambda a: a[:, 4 * h:4 * h + 4].unsqueeze(2).to_broadcast([P, 4, P])
                dve.wait_ge(kk_done, 4 * h + 1)
                dve.wait_ge(masked_ready, h + 1)
                dve.tensor_tensor(quart(a_m[:, h]), quarters(4), quart(a_m[:, h]), ALU.mult).then_inc(kk_evac, 1)
                dve.wait_ge(kk_done, 4 * h + 2)
                dve.tensor_tensor(quart(qkt[:, h]), quarters(5), quart(qkt[:, h]), ALU.mult).then_inc(kk_evac, 1)
                dve.wait_ge(kk_done, 4 * h + 3)
                dve.tensor_tensor(quart(chan[:, 4 + h]), quarters(6), bc(beg), ALU.mult)
                dve.tensor_tensor(quart(kdec[:, h]), quarters(6), bc(kdf), ALU.mult).then_inc(kk_evac, 1)
                dve.wait_ge(kk_done, 4 * h + 4)
                dve.tensor_tensor(quart(chan[:, 8 + h]), quarters(7), bc(beta), ALU.mult).then_inc(kk_evac, 1)

            for h in range(H):
                dve.wait_ge(as_ready, h + 1)
                dve.tensor_tensor(quart(x_m[:, h]), ident[:].unsqueeze(1).to_broadcast([P, 4, P]), quart(as_m[:, h % 2]), ALU.subtract).then_inc(x1_ready, 1)
            for i in range(24):
                h = i % 4
                dve.wait_ge(p_done, i + 1)
                dve.wait_ge(y1_ready, 4)
                dve.tensor_tensor(y_m[:, h], y_m[:, h], ps[:, 3 * (i % 2) + 1], ALU.subtract).then_inc(y_lev, 1)
                if i < 20:
                    dve.tensor_tensor(x_m[:, h], x_m[:, h], ps[:, 3 * (i % 2) + 2], ALU.subtract).then_inc(x_lev, 1)

            for c in range(NT - 1):
                for h in range(H):
                    i = 4 * c + h
                    st = state[:, h * P:(h + 1) * P]
                    dve.wait_ge(s_done, i + 1)
                    if c == 0:
                        dve.tensor_copy(st, ps[:, 2 + h % 2, 0:P]).then_inc(s_ready, 1)
                    else:
                        dve.wait_ge(o_done, i + 1)
                        dve.wait_ge(s_ready, i - 3)
                        dve.scalar_tensor_tensor(out=st, in0=st, scalar=elast[:, 4 * h + c:4 * h + c + 1], in1=ps[:, 2 + h % 2, 0:P],
                                                 op0=ALU.mult, op1=ALU.add).then_inc(s_ready, 1)
            for h in range(H):
                dve.wait_ge(orms_ready, h + 1)
                link(dve.reciprocal(q_m[:, h % 2], q_m[:, h % 2]))
                dve.tensor_tensor(q_m[:, h % 2], q_m[:, h % 2], ps[:, 4 + h], ALU.mult).then_inc(onorm_ready, 1)

            def add_resid(g, done, ready):
                dve.wait_ge(done, g + 1)
                r = resid[:, g // 2, (g % 2) * 512:(g % 2 + 1) * 512]
                dve.tensor_tensor(r, r, ps[:, g % 4], ALU.add).then_inc(ready, 1)

            s = NT
            for g in range(8):
                add_resid(g, out_mm, h1_ready)
            mem_t = chan[:, 4:8, :].rearrange("p a t -> p (a t)").rearrange("p (k m) -> p k m", k=KT)
            for m in range(MT + 1):
                if m < MT:
                    recip_rms(s + m)
                if m >= 1:
                    evac_t(s + m - 1, R_MEM, lambda b: mem_t[:, 4 * b:4 * b + 4, (m - 1) * P:m * P])
            s += MT
            for t in range(NT + 1):
                if t < NT:
                    recip_rms(s + t)
                if t >= 1:
                    evac_t(s + t - 1, R_CROSS, lambda b: act_t[:, 4 * b:4 * b + 4, (t - 1) * P:t * P])
            s += NT
            for t in range(NT):
                o = 4 * (t % 2)
                scv = ps[:, 2 * (t % 2):2 * (t % 2) + 2, :].rearrange("p b (g m) -> p (b g) m", g=2)
                dve.wait_ge(sc_mm, t + 1)
                link(dve.tensor_reduce(mx[:, o:o + 4], scv, AX_X, ALU.max))
                dve.tensor_scalar(nmx[:, o:o + 4], mx[:, o:o + 4], -(XD ** -0.5), None, ALU.mult).then_inc(mx_ready, 1)
                dve.wait_ge(ex_ready, 4 * t + 4)
                link(dve.reciprocal(rinv[:, o:o + 4], rsum[:, o:o + 4]))
                pr = xn[:, t % 2].rearrange("p (h m) -> p h m", h=XH)
                dve.tensor_tensor(pr, pr, rinv[:, o:o + 4].unsqueeze(2).to_broadcast([P, 4, M]), ALU.mult).then_inc(p_ready, 1)
            for g in range(8):
                add_resid(g, co_mm, h2_ready)
                if g % 2 == 1:
                    t = g // 2
                    recip_rms(s + t)
                    if t >= 1:
                        evac_t(s + t - 1, R_MOE, lambda b: act_t[:, 4 * b:4 * b + 4, (t - 1) * P:t * P])
            evac_t(s + NT - 1, R_MOE, lambda b: act_t[:, 4 * b:4 * b + 4, (NT - 1) * P:NT * P])
            s += NT

            dve.wait_ge(iota_ready, 1)
            lg = extra[:, 4, 0:NT * E].rearrange("p (t e) -> p t e", t=NT)
            top = extra[:, 5, 0:64]
            topi = extra[:, 5, 64:96].bitcast(U32)
            topf = extra[:, 5, 128:160]
            for t in range(NT):
                dve.wait_ge(lg_mm, NT)
                link(dve.tensor_tensor(lg[:, t], ps[:, 0, t * E:(t + 1) * E], brt[:], ALU.add))
                link(dve.max(top[:, 8 * t:8 * t + 8], lg[:, t]))
                link(dve.max_index(topi[:, 8 * t:8 * t + 8], top[:, 8 * t:8 * t + 8], lg[:, t]))
            link(dve.tensor_copy(topf, topi))
            t4 = top[:, 0:32].rearrange("p (t k) -> p t k", t=NT)
            dve.tensor_tensor(gates[:], t4[:, :, 0:4], t4[:, :, 0:1].to_broadcast([P, NT, TOPK]), ALU.subtract).then_inc(top_ready, 1)
            ef = extra[:, 1, :]
            it_i = extra[:, 0, :].bitcast(I32)
            oh = extra[:, 6, :].rearrange("p (t k e) -> p t k e", t=NT, k=TOPK)
            tf4 = topf.rearrange("p (t k) -> p t k", t=NT)[:, :, 0:4]
            for t in range(NT):
                last = dve.tensor_tensor(oh[:, t], ef[:, 0:E].unsqueeze(1).to_broadcast([P, TOPK, E]),
                                         tf4[:, t].unsqueeze(2).to_broadcast([P, TOPK, E]), ALU.is_equal)
            link(last)
            mask = extra[:, 3, 0:NT * E].rearrange("p (t e) -> p t e", t=NT)
            for t in range(NT):
                last = dve.tensor_reduce(mask[:, t], oh[:, t].rearrange("p k e -> p e k"), AX_X, ALU.add)
            last.then_inc(oh_ready, 1)
            dve.wait_ge(gexp_ready, 1)
            link(dve.tensor_reduce(top[:, 40:44], gates[:], AX_X, ALU.add))
            link(dve.reciprocal(top[:, 40:44], top[:, 40:44]))
            link(dve.tensor_tensor(gates[:], gates[:], top[:, 40:44].unsqueeze(2).to_broadcast([P, NT, TOPK]), ALU.mult))
            dve.wait_ge(pos_mm, 1)
            posp = extra[:, 7, 0:NT * E].rearrange("p (t e) -> p t e", t=NT)
            link(dve.tensor_tensor(posp, ps[:, 1, 0:NT * E].rearrange("p (t e) -> p t e", t=NT),
                                   ef[:, 32:64].unsqueeze(1).to_broadcast([P, NT, E]), ALU.add))
            for t in range(NT):
                last = dve.tensor_tensor(oh[:, t], oh[:, t], posp[:, t:t + 1].to_broadcast([P, TOPK, E]), ALU.mult)
            link(last)
            link(dve.tensor_reduce(topf[:, 0:16], extra[:, 6, :].rearrange("p (a e) -> p a e", e=E), AX_X, ALU.add))
            dve.tensor_copy(it_i[:, 256:272], topf[:, 0:16]).then_inc(slot_ready, 1)
            cnt = extra[0:1, 7, 256:288]
            link(dve.tensor_copy(cnt, ps[0:1, 2, 0:E]))
            flag, rank = extra[0:1, 7, 288:384], extra[0:1, 7, 384:480]
            link(dve.tensor_tensor(flag.rearrange("p (e b) -> p e b", b=3), cnt.unsqueeze(2).to_broadcast([1, E, 3]),
                                   ef[0:1, 96:99].unsqueeze(1).to_broadcast([1, E, 3]), ALU.is_gt))
            link(dve.tensor_tensor_scan(rank, ones[0:1, 0:96], flag, 0.0, ALU.mult, ALU.add))
            link(dve.tensor_scalar(extra[0:1, 7, 480:481], rank[:, 95:96], float(E), None, ALU.add))
            link(dve.tensor_scalar(extra[0:1, 7, 481:482], rank[:, 95:96], float(E - 1), None, ALU.add))
            link(dve.tensor_copy(nblocks[:], extra[0:1, 7, 480:482]))
            link(dve.tensor_tensor(rank, rank, flag, ALU.subtract))
            link(dve.tensor_tensor(flag, flag, ef[0:1, 128:224], ALU.mult))
            sel = act_t[0:1, 0:4, :].rearrange("p a t -> p (a t)")[:, 0:96 * N_MORE].rearrange("p (j f) -> p j f", j=N_MORE)
            dve.wait_ge(lg_mm, NT)
            link(dve.tensor_tensor(sel, rank.unsqueeze(1).to_broadcast([1, N_MORE, 96]), ef[0:1, 224:224 + N_MORE].unsqueeze(2).to_broadcast([1, N_MORE, 96]), ALU.is_equal))
            link(dve.tensor_tensor(sel, sel, flag.unsqueeze(1).to_broadcast([1, N_MORE, 96]), ALU.mult))
            link(dve.tensor_reduce(flag[:, 0:N_MORE], sel, AX_X, ALU.add))
            link(dve.tensor_scalar(flag[:, 0:N_MORE], flag[:, 0:N_MORE], float(E * CAP), None, ALU.add))
            link(dve.tensor_copy(codes[0:1, E:MAXB], flag[:, 0:N_MORE]))
            dve.tensor_copy(codes_f, codes[:]).then_inc(tab_step, 1)
            link(dve.tensor_scalar(experts[:], codes[:], 2, None, ALU.arith_shift_right))
            dve.tensor_scalar(experts[:], experts[:], E - 1, None, ALU.min).then_inc(codes_ready, 1)

            dve.wait_ge(codes_ready, 1)
            n_blocks = dve.value_load(nblocks[0:1, 0:1], min_val=E, max_val=MAXB - 3)

            def evac_xt():
                for b in range(2):
                    g = gain_moe[:, 4 * b:4 * b + 4].unsqueeze(2).to_broadcast([P, 4, P])
                    last = dve.tensor_tensor(quart(gt[:, 512 * b:512 * (b + 1)]), quarters(6 + b), g, ALU.mult)
                return last

            def lo(c, count):
                dve.wait_ge(hi_ready, count)
                k = c % KT if c < GU else HALF + c - GU
                dve.tensor_tensor(wsp[:, c % NSPLIT, 1], ring[:, (GM + c // KT) % 3, k], wsp[:, c % NSPLIT, 0], ALU.subtract).then_inc(lo_ready, 1)

            dve.wait_ge(tab_mm, 1)
            dve.tensor_copy(codes_col, ps[0:MAXB, 3, 0:1]).then_inc(tab_step, 1)
            dve.wait_ge(blk_in, 16)
            dve.tensor_copy(blk_f, blk_i).then_inc(tab_step, 1)
            dve.wait_ge(tab_mm, 2)
            link(dve.tensor_copy(row_tab, ps[:, 3, 0:MAXB]))
            dve.tensor_scalar(tok_tab, row_tab, 2, None, ALU.arith_shift_right).then_inc(tab_step, 1)
            for c in range(NSPLIT):
                lo(c, c + 1)
            dve.wait_ge(xgt_done, 1)
            evac_xt().then_inc(xt_ready, 1)
            dve.wait_ge(xhi_ready, 1)
            dve.tensor_tensor(x_lo[:], gt[:], x_hi[:], ALU.subtract).then_inc(xlo_ready, 1)
            with dve.Fori(0, n_blocks) as n:
                for c in range(NSPLIT, 12):
                    lo(c, n * SPLIT + (c + 1))
                dve.wait_ge(split_used, n * SPLIT + KT)
                dve.tensor_scalar(gt[:], ps[:, 0:2, :].rearrange("p b f -> p (b f)"), 7.0, None, ALU.min).then_inc(gt_ready, 1)
                dve.wait_ge(sg_ready, n + 1)
                dve.tensor_tensor(gt[:], gt[:], sig_e[:], ALU.mult).then_inc(gs_ready, 1)
                for c in range(12, GU + 1):
                    lo(c, n * SPLIT + (c + 1))
                dve.wait_ge(split_used, n * SPLIT + GU)
                dve.wait_ge(gs_ready, n + 1)
                for i in range(2):
                    hs = slice(i * 512, (i + 1) * 512)
                    dve.tensor_scalar(up[:, hs], ps[:, 2 + i], 7.0, -7.0, ALU.min, ALU.max).then_inc(up_ready, 1)
                    dve.wait_ge(up_ready, n * 2 + (i + 1))
                    dve.scalar_tensor_tensor(out=hid[:, hs], in0=up[:, hs], scalar=1.0, in1=gt[:, hs], op0=ALU.add, op1=ALU.mult).then_inc(hid_ready, 1)
                for c in (GU + 1, GU + 2):
                    lo(c, n * SPLIT + (c + 1))
                dve.wait_ge(hidhi_ready, n + 1)
                dve.tensor_tensor(hid_lo[:], ps[:, 1], hid_hi[:], ALU.subtract).then_inc(hidlo_ready, 1)
                lo(GU + 3, n * SPLIT + SPLIT)
                dve.wait_ge(xgt_done, n + 2)
                evac_xt().then_inc(xt_ready, 1)
                for c in range(NSPLIT):
                    if c == 2:
                        dve.wait_ge(xhi_ready, n + 2)
                        dve.tensor_tensor(x_lo[:], gt[:], x_hi[:], ALU.subtract).then_inc(xlo_ready, 1)
                    lo(c, n * SPLIT + (SPLIT + c + 1))

            yv = ring[:, :, :, :].rearrange("p a k d -> p (a k) d")
            for t in range(NT):
                dve.wait_ge(y_in[t], 16)
                for k in range(TOPK):
                    ins = dve.scalar_tensor_tensor(out=resid[:, t], in0=yv[:, 4 * t + k], scalar=gates[:, t, k:k + 1], in1=resid[:, t],
                                                   op0=ALU.mult, op1=ALU.add)
                    ins.then_inc(comb_ready if k == TOPK - 1 else tail_c, 1)
                    if k < TOPK - 1:
                        dve.wait_ge(tail_c, 3 * t + k + 1)
            dve.wait_ge(stat_ready, 14 + NT + 1)
            dve.reciprocal(rstd[:, 0:4], rms[:, 0:4]).then_inc(rstd_ready, 1)
            dve.wait_ge(rstd_ready, 15)
            dve.wait_ge(nf_in, 16)
            for t in range(NT):
                dve.scalar_tensor_tensor(out=resid[:, t], in0=resid[:, t], scalar=rstd[:, t:t + 1], in1=up[:], op0=ALU.mult, op1=ALU.mult).then_inc(fin_ready, 1)


_INS = ["x", "mem", "norm_mix", "w_in", "dn_conv", "dn_a_log", "dn_dt_bias", "dn_norm", "rg_conv", "rg_conv_b",
        "rg_w_a", "rg_b_a", "rg_w_x", "rg_b_x", "rg_lambda", "w_out", "norm_cross", "norm_mem", "w_cq", "w_ckv",
        "w_co", "norm_moe", "w_router", "b_router", "w_gate", "b_gate", "w_up", "b_up", "w_down", "b_down",
        "norm_final"]


def kernel(**inputs):
    import numpy as _np
    import concourse.bacc as _bacc
    from concourse import mybir as _mybir
    from concourse.bass_utils import run_bass_kernel_spmd as _run

    nc = _bacc.Bacc("TRN2", target_bir_lowering=False, num_devices=1)
    arrays, args = {}, []
    for name in _INS:
        a = _np.ascontiguousarray(inputs[name])
        arrays[f"in_{name}_dram"] = a
        args.append(nc.dram_tensor(f"in_{name}_dram", a.shape, _mybir.dt.from_np(a.dtype), kind="ExternalInput").ap())
    shape = inputs["x"].shape
    args.append(nc.dram_tensor("out_0_dram", shape, _mybir.dt.float32, kind="ExternalOutput").ap())
    build_layer(nc, *args)
    r = _run(nc, [arrays], core_ids=[0])
    return r.results[0]["out_0_dram"]
```

```python
from contextlib import ExitStack

import concourse.bass as bass
from concourse import mybir

ALU = mybir.AluOpType
ACT = mybir.ActivationFunctionType
AX_X = mybir.AxisListType.X
F32 = mybir.dt.float32
BF16 = mybir.dt.bfloat16
F32R = mybir.dt.float32r
I32 = mybir.dt.int32
U32 = mybir.dt.uint32

P = 128
EPS = 1e-6
GELU_C = 0.7978845608028654


def build_layer(nc, x, mem, norm_mix, w_in, dn_conv, dn_a_log, dn_dt_bias, dn_norm, rg_conv, rg_conv_b,
                rg_w_a, rg_b_a, rg_w_x, rg_b_x, rg_lambda, w_out, norm_cross, norm_mem, w_cq, w_ckv,
                w_co, norm_moe, w_router, b_router, w_gate, b_gate, w_up, b_up, w_down, b_down,
                norm_final, out):
    T, D = x.shape[1], x.shape[2]
    NT = T // P
    KT = D // P
    HALF = KT // 2
    H = dn_a_log.shape[1]
    M = mem.shape[1]
    MT = M // P
    XH = 4
    XD = D // XH
    E = w_router.shape[2]
    TOPK = 4
    N_ROW = T * TOPK
    CAP = NT
    NSPLIT = 4
    MAXB = 50
    N_MORE = MAXB - E
    GU = 2 * KT
    N_POOL = 10
    SPLIT = GU + HALF
    NOBODY = 1 << 20
    LEVELS = [1, 2, 4, 8, 16, 32, 64]
    assert D == 1024 and T == 512 and H == 4 and M == 256 and E == 32

    hn_rows = nc.dram_tensor("hn_rows", [T, D], F32, kind="Internal").ap()
    y_rows = nc.dram_tensor("y_rows", [N_ROW, D], F32, kind="Internal").ap()
    bias_parts = nc.dram_tensor("bias_parts", [E, 3, 3 * D], BF16, kind="Internal").ap()

    with ExitStack() as ctx:
        def sb(name, shape, dt=F32):
            return ctx.enter_context(nc.sbuf_tensor(name, shape, dt))

        def sem(name):
            return ctx.enter_context(nc.semaphore(name))

        ps = ctx.enter_context(nc.psum_tensor("ps", [P, 8, 512], F32))

        def quarters(bank):
            return ps[:, bank, :].rearrange("p (c f) -> p c f", c=4)

        resid = sb("resid", [P, NT, D])
        with ExitStack() as early:
            early.enter_context(nc.sbuf_tensor("ring_first", [P, 2, KT, D], F32))
            wf = early.enter_context(nc.sbuf_tensor("wf", [P, 2, 2, D], F32R))
            act_lo = early.enter_context(nc.sbuf_tensor("act_lo", [P, KT, T], F32R))
        ring = sb("ring", [P, 3, KT, D])
        ident = sb("ident", [P, P])
        ones = sb("ones", [P, P])
        tri = sb("tri", [P, P])
        par_rows = sb("par_rows", [P, P])
        par = sb("par", [P, P])
        w_ba = sb("w_ba", [P, KT, 2 * H])
        w_rt = sb("w_rt", [P, KT, E])
        brt = sb("brt", [P, E])
        small = sb("small", [P, 320])
        ones3 = sb("ones3", [3, P], BF16)
        codes = sb("codes", [1, MAXB], I32)
        experts = sb("experts", [1, MAXB], I32)
        nblocks = sb("nblocks", [1, 2], I32)
        gates = sb("gates", [P, NT, TOPK])
        guard = sb("guard", [1, 8])
        gain_moe = sb("gain_moe", [P, KT])

        idx = sb("idx", [P, 2], I32)
        xn = sb("xn", [P, 2, D])
        extra = sb("extra", [P, 8, T])
        with ExitStack() as dense:
            act_t = dense.enter_context(nc.sbuf_tensor("act_t", [P, KT, T], F32))
            chan = dense.enter_context(nc.sbuf_tensor("chan", [P, 24, T], F32))
        with ExitStack() as attention:
            act_hi = attention.enter_context(nc.sbuf_tensor("act_hi", [P, KT, T], F32R))
        wsp = sb("wsp", [P, NSPLIT, 2, D], F32R)
        x_hi, x_lo = sb("x_hi", [P, D], F32R), sb("x_lo", [P, D], F32R)
        hid_hi, hid_lo = sb("hid_hi", [P, HALF * P], F32R), sb("hid_lo", [P, HALF * P], F32R)
        hid_t = sb("hid_t", [P, HALF * P])
        y_sb, xg, gt, up = (sb(n, [P, D]) for n in ("y_sb", "xg", "gt", "up"))
        row_tab, tok_tab = extra[:, 3, P:P + E * CAP + 1].bitcast(I32), extra[:, 3, 264:264 + E * CAP + 1].bitcast(I32)
        zero_i = extra[:, 3, 500:501].bitcast(I32)
        oh_pos = chan[:, 8:12, :].rearrange("p a t -> p (a t)").rearrange("p (j f) -> p j f", f=P)
        oh_blk = chan[:, 12:16, :].rearrange("p a t -> p (a t)").rearrange("p (j f) -> p j f", f=E * CAP)
        bias3 = extra[0:3, 4:7, :].rearrange("p a t -> p (a t)").bitcast(BF16)
        sig_e = up
        hid = up

        at = [0]

        def cols(n):
            at[0] += n
            assert at[0] <= 320
            return small[:, at[0] - n:at[0]]

        eps_t = cols(1)
        ss = cols(14)
        rms = cols(14)
        rstd = cols(14)
        dtb = cols(H)
        alog = cols(H)
        sp_in = cols(20)
        sp_e = cols(20)
        sp_s = cols(20)
        sp_s2 = cols(20)
        g_t = cols(16)
        beta = cols(16)
        gp = cols(16)
        egp = cols(16)
        kdf = cols(16)
        beg = cols(16)
        elast = cols(16)
        rate = cols(4)
        nrate = cols(4)
        mx = cols(8)
        nmx = cols(8)
        rsum = cols(8)
        rinv = cols(8)

        R_DCONV, R_RCONV, R_RCB, R_BA, R_BX, R_LAM, R_DN = 0, 48, 64, 68, 72, 76, 80
        R_MIX, R_CROSS, R_MEM, R_MOE = 81, 89, 97, 105

        xn_flat = xn[:, :, :].rearrange("p a d -> p (a d)")
        rgw = xn_flat[:, 0:1024].rearrange("p (g n o) -> p g n o", g=2, n=4)
        lmask = xn_flat[:, 1024:1024 + 7 * P].rearrange("p (l s) -> p l s", l=7)

        tmp = ring[:, 2, :, :].rearrange("p k d -> p (k d)").rearrange("p (a f) -> p a f", f=T)
        a_m, x_m, kdec = tmp[:, 0:4], tmp[:, 4:8], tmp[:, 8:12]
        as_m, q_m = tmp[:, 12:14], tmp[:, 14:16]
        vnew, state = tmp[:, 12, :], tmp[:, 13, :]
        y_m, qkt = extra[:, 0:4], extra[:, 4:8]

        def onrm(h):
            return tmp[:, (14, 15, 12, 13)[h]]

        b_f = extra[0:3 * E, 0:2, :].rearrange("p a t -> p (a t)")
        b_part = [extra[0:3 * E, u, :].bitcast(BF16) for u in (2, 3, 6)]

        def quart(ap):
            return ap.rearrange("p (c f) -> p c f", c=4)

        x_in = [sem(f"x_in{t}") for t in range(NT)]
        w_in_slot = [sem(f"w_in_slot{i}") for i in range(6)]
        par_in, ba_in, rgw_in, small_in, bias_in = (sem(n) for n in ("par_in", "ba_in", "rgw_in", "small_in", "bias_in"))
        consts_ready, par_clear = sem("consts_ready"), sem("par_clear")
        par_t, par_ready = sem("par_t"), sem("par_ready")
        xn_ready, tr_done, tr_evac = sem("xn_ready"), sem("tr_done"), sem("tr_evac")
        stat_ready, rstd_ready = sem("stat_ready"), sem("rstd_ready")
        dve_c, act_c, pool_c = sem("dve_chain"), sem("act_chain"), sem("pool_chain")
        ba_done, g_ready, gp_done, gp_ready = sem("ba_done"), sem("g_ready"), sem("gp_done"), sem("gp_ready")
        exp_small, beta_ready, sp_ready = sem("exp_small"), sem("beta_ready"), sem("sp_ready")
        proj_done, tap_ready, tile_done, sig_ready, silu_done = (sem(n) for n in ("proj_done", "tap_ready", "tile_done", "sig_ready", "silu_done"))
        sq_ready, l2_done, l2_evac, norm_ready, qk_ready = (sem(n) for n in ("sq_ready", "l2_done", "l2_evac", "norm_ready", "qk_ready"))
        y2_ready, yt_ready, tanh_ready = sem("y2_ready"), sem("yt_ready"), sem("tanh_ready")
        gate_mm, ri_ready, bx_ready, rt_ready, mult_in, mult_ready, rg_done = (sem(n) for n in ("gate_mm", "ri_ready", "bx_ready", "rt_ready", "mult_in", "mult_ready", "rg_done"))
        gu_ready, gb_done, split_ready, decay_ready, masked_ready = (sem(n) for n in ("gu_ready", "gb_done", "split_ready", "decay_ready", "masked_ready"))
        kk_done, kk_evac, qexp_ready, kd_in, kdf_ready = (sem(n) for n in ("kk_done", "kk_evac", "qexp_ready", "kd_in", "kdf_ready"))
        x1_ready, x1t_done, y1_ready = sem("x1_ready"), sem("x1t_done"), sem("y1_ready")
        as_ready, qm_done, qm_ready, p_done, y_lev, x_lev = (sem(n) for n in ("as_ready", "qm_done", "qm_ready", "p_done", "y_lev", "x_lev"))
        wt_done, wt_ready = sem("wt_done"), sem("wt_ready")
        vn_done, vn_ready, s_done, s_ready, o_done = (sem(n) for n in ("vn_done", "vn_ready", "s_done", "s_ready", "o_done"))
        osq_ready, oss_done, orms_ready, onorm_ready, dn_done = (sem(n) for n in ("osq_ready", "oss_done", "orms_ready", "onorm_ready", "dn_done"))
        out_mm, h1_ready = sem("out_mm"), sem("h1_ready")
        mem_in, mk_mm, mk_evac = sem("mem_in"), sem("mk_mm"), sem("mk_evac")
        q_evac = sem("q_evac")
        sc_mm, mx_ready, ex_ready, p_ready, pt_mm, pt_evac = (sem(n) for n in ("sc_mm", "mx_ready", "ex_ready", "p_ready", "pt_mm", "pt_evac"))
        o_mm, co_mm, h2_ready = sem("o_mm"), sem("co_mm"), sem("h2_ready")
        hn_out = [sem(f"hn_out{i}") for i in range(2)]
        lg_mm, top_ready, gexp_ready, oh_ready, pos_mm = (sem(n) for n in ("lg_mm", "top_ready", "gexp_ready", "oh_ready", "pos_mm"))
        codes_ready, ohp_ready, ohb_ready, iota_ready = (sem(n) for n in ("codes_ready", "ohp_ready", "ohb_ready", "iota_ready"))
        bias_split, bias_out = sem("bias_split"), sem("bias_out")
        xg_clear, xg_in, xgt_done, xt_ready = (sem(n) for n in ("xg_clear", "xg_in", "xgt_done", "xt_ready"))
        bias3_in = sem("bias3_in")
        tab_step, tab_mm, row_ready = (sem(n) for n in ("tab_step", "tab_mm", "row_ready"))
        hidhi_ready, hidlo_ready = sem("hidhi_ready"), sem("hidlo_ready")
        wfh_ready, wfl_ready, wf_used, ah_ready, al_ready = (sem(n) for n in ("wfh_ready", "wfl_ready", "wf_used", "ah_ready", "al_ready"))
        gt_ready, sg_ready, hid_ready, hidt_done, hidt_ready = (sem(n) for n in ("gt_ready", "sg_ready", "hid_ready", "hidt_done", "hidt_ready"))
        down_done, y_ready, y_out = sem("down_done"), sem("y_ready"), sem("y_out")
        y_in = [sem(f"y_in{t}") for t in range(NT)]
        comb_ready, nf_in, fin_ready, out_sent = sem("comb_ready"), sem("nf_in"), sem("fin_ready"), sem("out_sent")
        stood, hi_ready, lo_ready, split_used, xhi_ready, xlo_ready, bias3_used, down_half, gs_ready, up_ready, tail_c = (sem(n) for n in ("stood", "hi_ready", "lo_ready", "split_used", "xhi_ready", "xlo_ready", "bias3_used", "down_half", "gs_ready", "up_ready", "tail_c"))

        block = ctx.enter_context(nc.Block())

        def front(w, c0):
            v = w[0].rearrange("(h k p) n -> h p k n", h=2, p=P)
            return [v[h, :, :, c0:c0 + D] for h in range(2)]

        C_BA = 4 * H * P
        FRONT = [front(w_in, 0), front(w_in, D), front(w_in, C_BA + 2 * H),
                 front(w_out, 0), front(w_ckv, 0), front(w_ckv, D), front(w_cq, 0), front(w_co, 0)]
        NF = len(FRONT)
        W_QK, W_VZ, W_RXY, W_OUT, W_CK, W_CV, W_CQ, W_CO = range(NF)
        SLOT = [m % 2 for m in range(NF)]
        FILL = [SLOT[:m + 1].count(SLOT[m]) for m in range(NF)]
        F_OUT = 3 * KT
        F_CQ = F_OUT + 4 * HALF
        F_CO = F_CQ + KT
        N_CO = 4 * HALF
        F_END = F_CO + N_CO
        OUT_ORDER = ([(0, 0, 2), (0, 0, 3), (0, 1, 2), (0, 1, 3), (0, 0, 0), (0, 0, 1), (0, 1, 0), (0, 1, 1)]
                     + [(1, n, kp) for n in range(2) for kp in (2, 3, 0, 1)])
        CO_ORDER = [(tp, n, kp) for tp in range(2) for n in range(2) for kp in range(4)]
        FREE = {W_RXY: (wfl_ready, KT), W_OUT: (wfl_ready, 2 * KT), W_CK: (wfl_ready, F_OUT), W_CV: (wfl_ready, F_CQ),
                W_CQ: (mk_mm, 8), W_CO: (mk_mm, 12)}

        def matrix_of(f):
            return f // KT if f < F_OUT else W_OUT if f < F_CQ else W_CQ if f < F_CO else W_CO

        def pair_of(f):
            order, i = (OUT_ORDER, f - F_OUT) if f < F_CQ else (CO_ORDER, f - F_CO)
            return (*order[i], all(o[:2] != order[i][:2] for o in order[i + 1:]))

        def by_rows(f):
            return F_OUT <= f < F_CQ or f >= F_CO

        def piece(f):
            w = ring[:, SLOT[matrix_of(f)]]
            if not by_rows(f):
                return w[:, :, f % KT * P:(f % KT + 1) * P]
            _, n, kp, _ = pair_of(f)
            return w[:, 2 * kp:2 * kp + 2, n * 512:(n + 1) * 512]

        def parts_of(f, part):
            return wf[:, f % 2, part].rearrange("p (k c) -> p k c", k=2 if by_rows(f) else KT)

        def used(f):
            if f < F_OUT:
                return proj_done, f + 1
            if by_rows(f) and pair_of(f)[3]:
                first, done = (F_OUT, out_mm) if f < F_CQ else (F_CO, co_mm)
                return done, 2 * len([g for g in range(first, f + 1) if pair_of(g)[3]])
            return wf_used, len([g for g in range(F_OUT, f + 1) if not (by_rows(g) and pair_of(g)[3])])

        OUT_BANKS = {(0, 0): (2, 3), (0, 1): (0, 1), (1, 0): (4, 5), (1, 1): (6, 7)}
        A_X = NT
        A_RG = A_X + H
        A_DN = A_RG + H
        A_H1 = A_DN + NT

        F_POOL = KT

        def slot_w(m, k):
            return ring[:, SLOT[m], k, :]

        expert_w = [w[0].rearrange("e (h p k) n -> e h p k n", h=2, p=P) for w in (w_gate, w_up, w_down)]

        GM = 2
        base = [16 * SLOT.count(s) for s in range(3)]

        @block.sync
        def _(sp):
            for t in range(NT):
                sp.dma_start(resid[:, t, :], x[0, t * P:(t + 1) * P, :]).then_inc(x_in[t], 16)
            sp.dma_start(w_ba[:], w_in[0].rearrange("(k p) n -> p k n", p=P)[:, :, C_BA:C_BA + 2 * H]).then_inc(ba_in, 16)
            sp.wait_ge(par_in, 16 * 11)
            for m in range(NF):
                if m == W_CV:
                    sp.wait_ge(dn_done, H)
                    sp.dma_start(chan[:, 0:4, :].rearrange("p a t -> p (a t)").rearrange("p (m d) -> p m d", m=MT),
                                 mem[0].rearrange("(m p) d -> p m d", p=P)).then_inc(mem_in, 16)
                if m in FREE:
                    sp.wait_ge(*FREE[m])
                for h in range(2):
                    s = 2 * SLOT[m] + h
                    sp.dma_start(ring[:, SLOT[m], HALF * h:HALF * (h + 1), :], FRONT[m][h]).then_inc(w_in_slot[s], 16)
                if m == W_QK:
                    sp.dma_start(dtb, dn_dt_bias.to_broadcast([P, H])).then_inc(small_in, 16)
                    sp.dma_start(alog, dn_a_log.to_broadcast([P, H])).then_inc(small_in, 16)
                    sp.dma_start(brt[:], b_router.to_broadcast([P, E])).then_inc(small_in, 16)
                    sp.dma_start(w_rt[:], w_router[0].rearrange("(k p) n -> p k n", p=P)).then_inc(small_in, 16)
                    sp.dma_start(gain_moe[:].rearrange("p (h k) -> p h k", h=2),
                                 norm_moe[0].rearrange("(h p k) -> p h k", h=2, p=P)).then_inc(small_in, 16)
                    for i, b in enumerate((b_gate, b_up, b_down)):
                        sp.dma_start(extra[E * i:E * (i + 1), 0:2, :].rearrange("p a t -> p (a t)"), b[0]).then_inc(bias_in, 16)
                if m == W_RXY:
                    sp.wait_ge(tr_evac, 2 * NT)
                    sp.dma_start(rgw[:, 0], rg_w_a[0].rearrange("n i o -> i n o")).then_inc(rgw_in, 16)
                    sp.dma_start(rgw[:, 1], rg_w_x[0].rearrange("n i o -> i n o")).then_inc(rgw_in, 16)
                    sp.wait_ge(bias_split, 1)
                    for i in range(3):
                        for part in range(3):
                            sp.dma_start(bias_parts[:, part, i * D:(i + 1) * D], b_part[part][E * i:E * (i + 1)]).then_inc(bias_out, 16)

            for j, free in ((1, (wfl_ready, F_CO)), (2, (wfl_ready, F_END)), (0, (co_mm, 8))):
                sp.wait_ge(*free)
                for h in range(2):
                    sp.dma_start(ring[:, (GM + j) % 3, HALF * h:HALF * (h + 1), :],
                                 expert_w[j][0, h]).then_inc(w_in_slot[2 * ((GM + j) % 3) + h], 16)
            sp.wait_ge(codes_ready, 1)
            sp.dma_start(bias3, bias_parts[0]).then_inc(bias3_in, 16)
            sp.wait_ge(hn_out[0], 16 * (NT // 2))
            sp.wait_ge(hn_out[1], 16 * (NT // 2))
            sp.dma_start(xn[:, 0], norm_final.rearrange("(o d) -> o d", o=1).to_broadcast([P, D])).then_inc(nf_in, 16)
            n_blocks = sp.value_load(nblocks[0:1, 0:1], min_val=E, max_val=MAXB - 3)
            n_more = sp.value_load(nblocks[0:1, 1:2], min_val=E - 1, max_val=MAXB - 4)
            with sp.Fori(0, n_more) as n:
                e = sp.value_load(experts[0:1, bass.ds(n + 1, 1)], min_val=0, max_val=E - 1)
                for j in range(3):
                    if j == 2:
                        sp.wait_ge(bias3_used, n + 1)
                        sp.dma_start(bias3, bias_parts[bass.ds(e, 1)].rearrange("o a b -> (o a) b")).then_inc(bias3_in, 16)
                    for h in range(2):
                        if j == 2 and h == 0:
                            sp.wait_ge(down_half, n + 1)
                        else:
                            sp.wait_ge(lo_ready, n * SPLIT + min(KT * j + HALF * (h + 1), SPLIT))
                        sp.dma_start(ring[:, (GM + j) % 3, HALF * h:HALF * (h + 1), :],
                                     expert_w[j][bass.ds(e, 1), h].rearrange("o p k n -> (o p) k n"))\
                            .then_inc(w_in_slot[2 * ((GM + j) % 3) + h], 16)
            sp.wait_ge(lo_ready, n_more * SPLIT + HALF)
            sp.dma_start(ring[:, GM, 0:HALF, :], expert_w[0][0, 0]).then_inc(w_in_slot[2 * GM], 16)
            sp.wait_ge(y_out, n_blocks * 16)
            y_tok = y_rows.rearrange("(t p k) d -> t p k d", p=P, k=TOPK)
            for t in range(NT):
                sp.dma_start(ring[:, :, :, :].rearrange("p a k d -> p (a k) d")[:, 4 * t:4 * t + 4, :], y_tok[t]).then_inc(y_in[t], 16)
            for t in range(NT):
                sp.wait_ge(fin_ready, t + 1)
                sp.dma_start(out[0, t * P:(t + 1) * P, :], resid[:, t, :]).then_inc(out_sent, 16)
            sp.wait_ge(out_sent, 16 * NT)

        @block.gpsimd
        def _(pool):
            chain = [0]

            def link(ins):
                chain[0] += 1
                ins.then_inc(pool_c, 1)
                pool.wait_ge(pool_c, chain[0])

            link(pool.memset(ones[:], 1.0))
            link(pool.memset(ident[:], 0.0))
            pool.affine_select(out=ident[:], in_=ident[:], compare_op=ALU.not_equal, fill=1.0, base=0,
                               pattern=[[-1, P]], channel_multiplier=1).then_inc(consts_ready, 1)
            pool.affine_select(out=tri[:], in_=ones[:], compare_op=ALU.is_ge, fill=0.0, base=0,
                               pattern=[[1, P]], channel_multiplier=-1).then_inc(consts_ready, 1)
            pool.memset(ones3[:], 1.0).then_inc(consts_ready, 1)
            pool.memset(guard[:], 0.0).then_inc(stood, 1)
            pool.wait_ge(tr_evac, 2 * NT)
            for l, w in enumerate(LEVELS):
                nb = P // (2 * w)
                v = lmask[:, l, :].rearrange("p (b j) -> p b j", b=nb)
                src = ones[:, :].rearrange("p (b j) -> p b j", b=nb)
                link(pool.affine_select(out=v, in_=src, compare_op=ALU.is_ge, fill=0.0, base=-w,
                                        pattern=[[-2 * w, nb], [0, 2 * w]], channel_multiplier=1))
                link(pool.affine_select(out=v, in_=v, compare_op=ALU.is_ge, fill=0.0, base=2 * w - 1,
                                        pattern=[[2 * w, nb], [0, 2 * w]], channel_multiplier=-1))
                link(pool.affine_select(out=v, in_=v, compare_op=ALU.is_ge, fill=0.0, base=w - 1,
                                        pattern=[[0, nb], [-1, 2 * w]], channel_multiplier=0))

            for j in range(22):
                if j + 2 >= F_POOL:
                    pool.wait_ge(wfl_ready, j + 2)
                    pool.wait_ge(wfh_ready, j + 3)
                    pool.tensor_tensor(parts_of(j + 2, 1), piece(j + 2), parts_of(j + 2, 0), ALU.subtract).then_inc(wfl_ready, 1)
                if j < 12:
                    pool.wait_ge(sig_ready, j + 1)
                    pool.tensor_tensor(chan[:, j], chan[:, j], extra[:, 4 + j % 2], ALU.mult).then_inc(silu_done, 1)
                if j == 0:
                    pool.wait_ge(bias_in, 48)
                if j < 4:
                    if j % 2 == 0:
                        link(pool.tensor_copy(b_part[j // 2], b_f))
                    else:
                        link(pool.tensor_tensor(b_f, b_f, b_part[j // 2], ALU.subtract))
                if j == 4:
                    pool.tensor_copy(b_part[2], b_f).then_inc(bias_split, 1)

            for n in range(4):
                pool.wait_ge(ri_ready, 2 * n + 2)
                pool.tensor_tensor(chan[:, 16 + n], chan[:, 16 + n], act_t[:, 4 + n], ALU.mult).then_inc(bx_ready, 1)

            for h in range(H):
                pool.wait_ge(decay_ready, 3 * h + 2)
                pool.affine_select(out=quart(a_m[:, h]), in_=quart(a_m[:, h]), compare_op=ALU.is_ge, fill=0.0,
                                   base=-1, pattern=[[0, 4], [-1, P]], channel_multiplier=1).then_inc(masked_ready, 1)
                pool.affine_select(out=quart(qkt[:, h]), in_=quart(qkt[:, h]), compare_op=ALU.is_ge, fill=0.0,
                                   base=0, pattern=[[0, 4], [1, P]], channel_multiplier=-1).then_inc(masked_ready, 1)
                pool.wait_ge(decay_ready, 3 * h + 3)
                pool.wait_ge(kk_done, 4 * h + 2)
                link(pool.tensor_tensor(chan[:, h], chan[:, h], q_m[:, h % 2], ALU.mult))
                pool.tensor_copy(elast[:, 4 * h:4 * h + 4].unsqueeze(2), quart(q_m[:, h % 2])[:, :, P - 1:P]).then_inc(qexp_ready, 1)

            pool.wait_ge(kk_evac, 4 * H)
            for l in range(7):
                for h in range(H):
                    i = 4 * l + h
                    if l == 0 and h >= 2:
                        pool.wait_ge(x1_ready, h - 1)
                    if l > 0:
                        if i - 4 >= 2:
                            pool.wait_ge(qm_done, i - 5)
                        else:
                            pool.wait_ge(x1_ready, H)
                    pool.tensor_tensor(quart(as_m[:, i % 2]), quart(a_m[:, h]),
                                       lmask[:, l:l + 1, :].to_broadcast([P, 4, P]), ALU.mult).then_inc(as_ready, 1)

            for h in range(H):
                pool.wait_ge(onorm_ready, h + 1)
                link(pool.tensor_scalar(onrm(h), onrm(h), par[:, R_DN:R_DN + 1], None, ALU.mult))
                pool.tensor_tensor(chan[:, 12 + h], chan[:, 12 + h], onrm(h), ALU.mult).then_inc(dn_done, 1)

            pool.wait_ge(co_mm, 1)
            it_i = extra[:, 0, :].bitcast(I32)
            ef = extra[:, 1, :]
            link(pool.iota(it_i[:, 0:E], pattern=[[1, E]], base=0, channel_multiplier=0))
            link(pool.iota(it_i[:, 64:80], pattern=[[4 * P, 4], [1, 4]], base=1, channel_multiplier=4))
            link(pool.iota(it_i[:, 96:99], pattern=[[P, 3]], base=P, channel_multiplier=0))
            link(pool.iota(it_i[:, 128:224], pattern=[[4, E], [1, 3]], base=1 - E * CAP, channel_multiplier=0))
            link(pool.iota(it_i[:, 288:288 + P], pattern=[[1, P]], base=0, channel_multiplier=0))
            link(pool.iota(it_i[:, 416:417], pattern=[[0, 1]], base=0, channel_multiplier=1))
            link(pool.tensor_copy(ef[:, 64:80], it_i[:, 64:80]))
            link(pool.tensor_copy(ef[:, 288:417], it_i[:, 288:417]))
            link(pool.tensor_copy(ef[:, 0:E], it_i[:, 0:E]))
            link(pool.tensor_scalar(ef[:, 32:64], ef[:, 0:E], float(CAP * P), None, ALU.mult))
            link(pool.tensor_copy(ef[:, 96:99], it_i[:, 96:99]))
            link(pool.tensor_copy(ef[:, 128:224], it_i[:, 128:224]))
            link(pool.affine_select(out=extra[:, 2, 0:P], in_=ones[:], compare_op=ALU.is_ge, fill=0.0, base=-1,
                                    pattern=[[1, P]], channel_multiplier=-1))
            link(pool.memset(extra[:, 3, 500:501], 0.0))
            pool.iota(codes[0:1, 0:E], pattern=[[CAP, E]], base=0, channel_multiplier=0).then_inc(iota_ready, 1)
            pool.wait_ge(co_mm, 8)
            pool.memset(xg[:], 0.0).then_inc(xg_clear, 1)

            pool.wait_ge(tab_step, 1)
            pos_f = extra[:, 5, 176:192]
            for j in range(N_POOL):
                pool.tensor_scalar(oh_pos[:, j], ef[:, 288:416], pos_f[:, j:j + 1], None, ALU.is_equal).then_inc(ohp_ready, 1)
            pool.wait_ge(xg_clear, 1)
            pool.wait_ge(hn_out[0], 16 * (NT // 2))
            pool.wait_ge(hn_out[1], 16 * (NT // 2))

            def stand(i):
                return pool.tensor_tensor(guard[:, i:i + 1], guard[:, 0:1], guard[:, 0:1], ALU.mult)

            def gather():
                pool.indirect_dma_start(out=xg[:], out_offset=None, in_=hn_rows,
                                        in_offset=bass.IndirectOffsetOnAxis(ap=idx[:, 0:1], axis=0),
                                        bounds_check=T - 1, oob_is_err=False).then_inc(xg_in, 16)

            pool.wait_ge(tab_step, 3)

            def take(col, table, at):
                return pool.tensor_tensor(idx[:, col:col + 1], table[:, at], zero_i, ALU.add)

            for c in range(2):
                if c > 0:
                    pool.wait_ge(xgt_done, c)
                link(take(0, tok_tab, slice(CAP * c, CAP * c + 1)))
                gather()
            take(1, row_tab, slice(0, 1)).then_inc(row_ready, 1)
            pool.wait_ge(codes_ready, 1)
            n_blocks = pool.value_load(nblocks[0:1, 0:1], min_val=E, max_val=MAXB - 3)
            with pool.Fori(0, n_blocks) as n:
                code1 = pool.value_load(codes[0:1, bass.ds(n + 1, 1)], min_val=0, max_val=E * CAP)
                code2 = pool.value_load(codes[0:1, bass.ds(n + 2, 1)], min_val=0, max_val=E * CAP)
                pool.wait_ge(xgt_done, n + 2)
                stand(4)
                take(0, tok_tab, bass.ds(code2, 1)).then_inc(stood, 1)
                pool.wait_ge(stood, n + 2)
                stand(1)
                gather()
                pool.wait_ge(y_ready, n * 2 + 2)
                stand(2)
                pool.wait_ge(row_ready, n + 1)
                stand(3)
                pool.indirect_dma_start(out=y_rows, out_offset=bass.IndirectOffsetOnAxis(ap=idx[:, 1:2], axis=0),
                                        in_=y_sb[:], in_offset=None, bounds_check=N_ROW - 1,
                                        oob_is_err=False).then_inc(y_out, 16)
                pool.wait_ge(y_out, n * 16 + 16)
                stand(5)
                take(1, row_tab, bass.ds(code1, 1)).then_inc(row_ready, 1)

        @block.scalar
        def _(act):
            chain = [0]

            def link(ins):
                chain[0] += 1
                ins.then_inc(act_c, 1)
                act.wait_ge(act_c, chain[0])

            act.wait_ge(par_clear, 1)

            def row(dst, src):
                act.dma_start(par_rows[dst:dst + src.shape[0], :], src).then_inc(par_in, 16)

            row(R_DCONV, dn_conv[0].rearrange("k (j p) -> (k j) p", p=P))
            row(R_RCONV, rg_conv[0].rearrange("k (j p) -> (k j) p", p=P))
            row(R_RCB, rg_conv_b[0].rearrange("(j p) -> j p", p=P))
            row(R_BA, rg_b_a[0])
            row(R_BX, rg_b_x[0])
            row(R_LAM, rg_lambda[0].rearrange("(j p) -> j p", p=P))
            row(R_DN, dn_norm)
            row(R_MIX, norm_mix[0].rearrange("(j p) -> j p", p=P))
            row(R_CROSS, norm_cross[0].rearrange("(j p) -> j p", p=P))
            row(R_MEM, norm_mem[0].rearrange("(j p) -> j p", p=P))
            row(R_MOE, norm_moe[0].rearrange("(j p) -> j p", p=P))
            def norm_rows(src, s, waits=()):
                for w in waits:
                    act.wait_ge(*w)
                if s >= 2:
                    act.wait_ge(tr_done, 2 * (s - 1))
                link(act.activation(xn[:, s % 2], src, ACT.Square, accum_out=ss[:, s:s + 1]))
                act.activation(rms[:, s:s + 1], ss[:, s:s + 1], ACT.Sqrt, scale=1.0 / D, bias=eps_t).then_inc(stat_ready, 1)
                act.wait_ge(rstd_ready, s + 1)
                act.activation(xn[:, s % 2], src, ACT.Copy, scale=rstd[:, s:s + 1]).then_inc(xn_ready, 1)

            def piece_hi(f):
                m = matrix_of(f)
                if f in (0, KT, 2 * KT, F_OUT, F_CQ, F_CO):
                    act.wait_ge(w_in_slot[2 * SLOT[m]], 16 * FILL[m])
                    act.wait_ge(w_in_slot[2 * SLOT[m] + 1], 16 * FILL[m])
                if f >= 2:
                    act.wait_ge(*used(f - 2))
                act.activation(parts_of(f, 0), piece(f), ACT.Copy).then_inc(wfh_ready, 1)

            def normed_hi(s, src):
                t = (s if s < NT else s - MT) % NT
                act.wait_ge(tr_evac, 2 * (s + 1))
                act.activation(act_hi[:, :, t * P:(t + 1) * P], src[:, :, t * P:(t + 1) * P], ACT.Copy).then_inc(ah_ready, 1)

            act.wait_ge(par_clear, 2)
            for t in range(NT):
                norm_rows(resid[:, t], t, [(x_in[t], 16)])
                if t >= 2:
                    normed_hi(t - 2, chan[:, 0:8])
            for t in (2, 3):
                normed_hi(t, chan[:, 0:8])
            piece_hi(0)
            piece_hi(1)

            act.wait_ge(sp_ready, 1)
            act.activation(sp_e, sp_s, ACT.Exp, scale=-1.0).then_inc(exp_small, 1)
            act.wait_ge(small_in, 16 * 5)
            act.activation(alog, alog, ACT.Exp).then_inc(exp_small, 1)
            act.wait_ge(sp_ready, 2)
            act.activation(beta, beta, ACT.Sigmoid).then_inc(beta_ready, 1)

            def tap(j, r, nj, bias):
                act.wait_ge(proj_done, j + 1)
                c = r + 3 * nj + (j if nj == 12 else j - 16)
                w3 = par[:, c:c + 1]
                if bias is None:
                    act.activation(chan[:, j], ps[:, j % 6], ACT.Copy, scale=w3).then_inc(tap_ready, 1)
                else:
                    act.activation(chan[:, j], ps[:, j % 6], ACT.Identity, scale=w3, bias=bias).then_inc(tap_ready, 1)

            def sigmoid_of(j):
                act.wait_ge(tile_done, j + 1)
                if j >= 2:
                    act.wait_ge(silu_done, j - 1)
                act.activation(extra[:, 4 + j % 2], chan[:, j], ACT.Sigmoid).then_inc(sig_ready, 1)

            def square_of(j):
                act.wait_ge(silu_done, j + 1)
                act.activation(chan[:, 16 + j], chan[:, j], ACT.Square).then_inc(sq_ready, 1)

            def sums_of(j):
                act.wait_ge(l2_done, j + 1)
                act.activation(chan[:, 16 + j], ps[:, 6 + j % 2], ACT.Copy).then_inc(l2_evac, 1)

            for j in range(24):
                if j < 22:
                    piece_hi(j + 2)
                if j < 12:
                    if j == 0:
                        act.wait_ge(par_ready, 1)
                    tap(j, R_DCONV, 12, None)
                if 1 <= j <= 12:
                    sigmoid_of(j - 1)
                if 12 <= j < 16:
                    act.wait_ge(proj_done, j + 1)
                    act.wait_ge(silu_done, min(j - 1, 12))
                    if j - 2 >= 12:
                        act.wait_ge(tile_done, j - 1)
                    act.activation(extra[:, 4 + j % 2], ps[:, j % 6], ACT.Sigmoid).then_inc(sig_ready, 1)
                if j in (11, 14):
                    i = (11, 14).index(j)
                    act.wait_ge(l2_evac, 4 * i + 4)
                    act.activation(chan[:, 16 + 4 * i:20 + 4 * i], chan[:, 16 + 4 * i:20 + 4 * i], ACT.Sqrt, scale=float(P) if i == 0 else 1.0,
                                   bias=sp_in[:, 0:1] if i == 0 else eps_t).then_inc(norm_ready, 1)
                if 16 <= j < 20:
                    act.wait_ge(qk_ready, H)
                    tap(j, R_RCONV, 4, par[:, R_RCB + j - 16:R_RCB + j - 15])
                if j >= 20:
                    act.wait_ge(proj_done, j + 1)
                    if j == 20:
                        act.wait_ge(bias_out, 16 * 9)
                    if j >= 22:
                        act.wait_ge(tile_done, j - 1)
                    act.activation(extra[:, 6 + j % 2], ps[:, j % 6], ACT.Square).then_inc(y2_ready, 1)
                    act.wait_ge(yt_ready, j - 19)
                    act.activation(extra[:, 6 + j % 2], extra[:, 6 + j % 2], ACT.Tanh, scale=GELU_C).then_inc(tanh_ready, 1)
                if 2 <= j < 10:
                    square_of(j - 2)
                if 6 <= j < 14:
                    sums_of(j - 6)

            act.wait_ge(proj_done, 24)
            for n in range(4):
                for g in range(2):
                    act.wait_ge(gate_mm, 2 * n + g + 1)
                    r = (R_BA if g == 0 else R_BX) + n
                    act.activation(act_t[:, 4 * g + n], ps[:, 6 + g], ACT.Sigmoid, bias=par[:, r:r + 1]).then_inc(ri_ready, 1)
            act.wait_ge(ri_ready, 8)
            for n in range(4):
                act.wait_ge(bx_ready, n + 1)
                act.activation(act_t[:, 4 + n], act_t[:, n], ACT.Tanh, scale=nrate[:, n:n + 1]).then_inc(rt_ready, 1)
            act.wait_ge(rt_ready, 4)
            for n in range(4):
                act.activation(act_t[:, n], act_t[:, n], ACT.Exp, scale=rate[:, n:n + 1]).then_inc(rt_ready, 1)

            act.wait_ge(gp_ready, 1)
            act.activation(egp, gp, ACT.Exp).then_inc(kdf_ready, 1)
            for h in range(H):
                act.wait_ge(split_ready, h + 1)
                act.activation(a_m[:, h], a_m[:, h], ACT.Exp, scale=-1.0).then_inc(decay_ready, 1)
                act.activation(qkt[:, h], qkt[:, h], ACT.Exp).then_inc(decay_ready, 1)
                act.wait_ge(kd_in, h + 1)
                if h >= 2:
                    act.wait_ge(qexp_ready, h - 1)
                act.activation(q_m[:, h % 2], ps[:, h], ACT.Exp).then_inc(decay_ready, 1)
                if h == 1:
                    act.wait_ge(kd_in, H)
                    act.activation(kdf, kdf, ACT.Exp).then_inc(kdf_ready, 1)

            def rg_hi(n):
                act.wait_ge(rg_done, n + 1)
                act.activation(act_hi[:, n], chan[:, 20 + n], ACT.Copy).then_inc(ah_ready, 1)

            for h in range(H):
                act.wait_ge(x1t_done, h + 1)
                act.activation(y_m[:, h], ps[:, h], ACT.Copy).then_inc(y1_ready, 1)
            for i in range(24):
                act.wait_ge(qm_done, i + 1)
                if i >= 2:
                    act.wait_ge(p_done, i - 1)
                else:
                    act.wait_ge(qexp_ready, H)
                act.activation(q_m[:, i % 2], ps[:, 3 * (i % 2)], ACT.Copy).then_inc(qm_ready, 1)
                if i in (4, 7, 10, 13):
                    n = i // 3 - 1
                    act.wait_ge(mult_in, n + 1)
                    act.activation(act_t[:, 4 + n], act_t[:, 4 + n], ACT.Sqrt, scale=2.0).then_inc(mult_ready, 1)
                if i in (16, 19, 22):
                    rg_hi(i // 3 - 5)
            for h in range(H):
                act.wait_ge(wt_done, h + 1)
                act.activation(chan[:, 4 + h], ps[:, 6 + h % 2], ACT.Copy, scale=-1.0).then_inc(wt_ready, 1)
            for c in range(NT):
                for h in range(H):
                    act.wait_ge(vn_done, 4 * c + h + 1)
                    if c > 0:
                        act.wait_ge(o_done, 4 * (c - 1) + h + 1)
                    act.activation(vnew[:, h * P:(h + 1) * P], ps[:, h % 2, 0:P], ACT.Copy).then_inc(vn_ready, 1)
                if c == 0:
                    rg_hi(3)
                elif c < 3:
                    piece_hi(F_OUT + c - 1)
            for h in range(H):
                act.wait_ge(o_done, 4 * (NT - 1) + (h + 1 if h < 2 else H))
                act.activation(onrm(h), ps[:, 4 + h], ACT.Square).then_inc(osq_ready, 1)
                act.wait_ge(oss_done, h + 1)
                act.activation(onrm(h), ps[:, h % 2], ACT.Sqrt, scale=1.0 / P, bias=eps_t).then_inc(orms_ready, 1)
            piece_hi(F_OUT + 2)
            piece_hi(F_OUT + 3)
            for h in range(H):
                act.wait_ge(dn_done, h + 1)
                act.activation(act_hi[:, (6, 7, 4, 5)[h]], chan[:, 12 + h], ACT.Copy).then_inc(ah_ready, 1)
                if h == 2:
                    piece_hi(F_OUT + 4)
            piece_hi(F_OUT + 5)

            s = NT
            memf = chan[:, 0:4, :].rearrange("p a t -> p (a t)").rearrange("p (m d) -> p m d", m=MT)
            for i in range(6, 4 * HALF):
                piece_hi(F_OUT + i)
                if i in (10, 12):
                    norm_rows(memf[:, s - NT], s, [(mem_in, 16)])
                    s += 1
            def norm_h1(t):
                norm_rows(resid[:, t], NT + MT + t, [(h1_ready, (3, 4, 7, 8)[t])])

            def h1_hi(t):
                normed_hi(NT + MT + t, chan[:, 16:24])

            def v_copy(i):
                act.wait_ge(mk_mm, 9 + i)
                act.activation(extra[:, 4 + i], ps[:, i % 4], ACT.Copy).then_inc(mk_evac, 1)

            norm_h1(0)
            norm_h1(1)
            for i in range(8):
                act.wait_ge(mk_mm, i + 1)
                act.activation(extra[:, 0:4, :].rearrange("p a t -> p (a t)")[:, i * M:(i + 1) * M], ps[:, i % 4, 0:M], ACT.Copy).then_inc(mk_evac, 1)
            h1_hi(0)
            h1_hi(1)
            norm_h1(2)
            norm_h1(3)
            v_copy(0)
            v_copy(1)
            piece_hi(F_CQ)
            piece_hi(F_CQ + 1)
            h1_hi(2)
            h1_hi(3)
            v_copy(2)
            v_copy(3)
            for i in range(8):
                act.wait_ge(*used(F_CQ + i))
                act.activation(chan[:, i], ps[:, i % 4], ACT.Copy).then_inc(q_evac, 1)
                piece_hi(F_CQ + i + 2)
            def pt_copies(t):
                for b in range(2):
                    act.wait_ge(pt_mm, 2 * t + b + 1)
                    act.activation(chan[:, 8 + 4 * b:12 + 4 * b, t * P:(t + 1) * P], quarters(4 + b), ACT.Copy).then_inc(pt_evac, 1)

            for t in range(NT):
                act.wait_ge(mx_ready, t + 1)
                if t >= 2:
                    act.wait_ge(pt_mm, 2 * (t - 1))
                pr = xn[:, t % 2].rearrange("p (h m) -> p h m", h=XH)
                scv = ps[:, 2 * (t % 2):2 * (t % 2) + 2, :].rearrange("p b (g m) -> p (b g) m", g=2)
                for h in range(XH):
                    c = 4 * (t % 2) + h
                    act.activation(pr[:, h], scv[:, h], ACT.Exp, scale=XD ** -0.5, bias=nmx[:, c:c + 1],
                                   accum_out=rsum[:, c:c + 1]).then_inc(ex_ready, 1)
                if t >= 1:
                    pt_copies(t - 1)
            pt_copies(NT - 1)
            for i in range(8):
                act.wait_ge(o_mm, i + 1)
                act.activation(act_hi[:, i], ps[:, 6 + i % 2], ACT.Copy).then_inc(ah_ready, 1)

            def norm_h2(t):
                s = 2 * NT + MT + t
                norm_rows(resid[:, t], s, [(h2_ready, (3, 4, 7, 8)[t])] + ([(hn_out[s % 2], 16 * (t // 2))] if t >= 2 else []))
                act.wait_ge(xn_ready, s + 1)
                act.dma_start(hn_rows[t * P:(t + 1) * P, :], xn[:, s % 2]).then_inc(hn_out[s % 2], 16)

            for c in range(N_CO):
                if c < N_CO - 2:
                    piece_hi(F_CO + c + 2)
                if c in (8, 10):
                    norm_h2(c // 2 - 4)
            norm_h2(2)
            norm_h2(3)
            act.wait_ge(top_ready, 1)
            act.activation(gates[:], gates[:], ACT.Exp).then_inc(gexp_ready, 1)

            def hi(c, block=None):
                k = c % KT if c < GU else HALF + c - GU
                m = (GM + c // KT) % 3
                s = 2 * m + k // HALF
                if c % HALF == 0:
                    act.wait_ge(w_in_slot[s], base[m] + 16 if block is None else block * 16 + (base[m] + 16))
                if block is not None:
                    act.wait_ge(split_used, block * SPLIT + (c - NSPLIT + 1))
                act.activation(wsp[:, c % NSPLIT, 0], ring[:, m, k], ACT.Copy).then_inc(hi_ready, 1)

            act.wait_ge(lg_mm, NT)
            for c in range(NSPLIT):
                hi(c)
            act.wait_ge(codes_ready, 1)
            n_blocks = act.value_load(nblocks[0:1, 0:1], min_val=E, max_val=MAXB - 3)
            act.wait_ge(xt_ready, 1)
            act.activation(x_hi[:], gt[:], ACT.Copy).then_inc(xhi_ready, 1)
            with act.Fori(0, n_blocks) as n:
                for c in range(NSPLIT, 12):
                    hi(c, n)
                act.wait_ge(gt_ready, n + 1)
                act.activation(sig_e[:], gt[:], ACT.Sigmoid, scale=1.702).then_inc(sg_ready, 1)
                for c in range(12, SPLIT):
                    hi(c, n)
                act.wait_ge(hidt_done, n * 2 + 1)
                act.activation(hid_t[:], ps[:, 0], ACT.Copy).then_inc(hidt_ready, 1)
                act.wait_ge(hidt_done, n * 2 + 2)
                act.activation(hid_hi[:], ps[:, 1], ACT.Copy).then_inc(hidhi_ready, 1)
                act.wait_ge(xt_ready, n + 2)
                act.activation(x_hi[:], gt[:], ACT.Copy).then_inc(xhi_ready, 1)
                for c in range(NSPLIT):
                    if c == 0:
                        act.wait_ge(w_in_slot[2 * GM], n * 16 + (base[GM] + 32))
                    act.wait_ge(split_used, n * SPLIT + (SPLIT + c - NSPLIT + 1))
                    act.activation(wsp[:, c, 0], ring[:, GM, c], ACT.Copy).then_inc(hi_ready, 1)
                act.wait_ge(row_ready, n + 1)
                for i in range(2):
                    act.wait_ge(*((down_done, n + 1) if i == 0 else (split_used, n * SPLIT + SPLIT)))
                    act.activation(y_sb[:, i * 512:(i + 1) * 512], ps[:, 4 + i], ACT.Copy).then_inc(y_ready, 1)
            for t in range(NT):
                act.wait_ge(comb_ready, t + 1)
                if t >= 1:
                    act.wait_ge(stat_ready, 14 + t)
                link(act.activation(xn[:, 1], resid[:, t], ACT.Square, accum_out=ss[:, t:t + 1]))
                act.activation(rms[:, t:t + 1], ss[:, t:t + 1], ACT.Sqrt, scale=1.0 / D, bias=eps_t).then_inc(stat_ready, 1)

        @block.tensor
        def _(pe):
            pe.wait_ge(consts_ready, 3)
            pe.wait_ge(par_in, 16 * 11)
            pe.transpose(ps[:, 7, 0:P], par_rows[:], ident[:]).then_inc(par_t, 1)

            def transposes(s):
                pe.wait_ge(xn_ready, s + 1)
                for b in range(2):
                    bank = 2 * (s % 2) + 4 + b
                    if s >= 2:
                        pe.wait_ge(tr_evac, 2 * (s - 2) + b + 1)
                    elif s == 1:
                        pe.wait_ge(par_ready, 1)
                    for k in range(4):
                        last = pe.transpose(quarters(bank)[:, k], xn[:, s % 2, (4 * b + k) * P:(4 * b + k + 1) * P], ident[:])
                    last.then_inc(tr_done, 1)

            for t in range(NT):
                transposes(t)
            pe.wait_ge(tr_evac, 2 * NT)
            pe.wait_ge(ba_in, 16)
            for t in range(NT):
                for k in range(KT):
                    last = pe.matmul(ps[:, 7, 8 * t:8 * t + 8], chan[:, k, t * P:(t + 1) * P], w_ba[:, k], start=(k == 0), stop=(k == KT - 1))
            last.then_inc(ba_done, 1)

            def by_channels(f, o):
                for k in range(KT):
                    for w, a in ((0, act_hi), (1, act_hi), (0, act_lo)):
                        last = pe.matmul(o, parts_of(f, w)[:, k], a[:, k], start=(k == 0 and w == 0 and a is act_hi),
                                         stop=(k == KT - 1 and a is act_lo))
                return last

            for j in range(24):
                pe.wait_ge(al_ready, NT)
                pe.wait_ge(wfl_ready, j + 1)
                if j >= 6:
                    pe.wait_ge(tile_done, j - 5)
                last = by_channels(j, ps[:, j % 6])
                last.then_inc(proj_done, 1)
                if j == 2:
                    pe.wait_ge(g_ready, 1)
                    pe.matmul(ps[:, 7, 64:80], tri[:], g_t, start=True, stop=True).then_inc(gp_done, 1)
                if 5 <= j < 13:
                    i = j - 5
                    pe.wait_ge(sq_ready, i + 1)
                    if i >= 2:
                        pe.wait_ge(l2_evac, i - 1)
                    elif i == 1:
                        pe.wait_ge(gp_ready, 1)
                    pe.matmul(ps[:, 6 + i % 2], ones[:], chan[:, 16 + i], start=True, stop=True).then_inc(l2_done, 1)

            pe.wait_ge(rgw_in, 32)
            pe.wait_ge(tile_done, 20)
            for n in range(4):
                for g in range(2):
                    if n > 0:
                        pe.wait_ge(ri_ready, 2 * (n - 1) + g + 1)
                    pe.matmul(ps[:, 6 + g], rgw[:, g, n], chan[:, 16 + n], start=True, stop=True).then_inc(gate_mm, 1)

            pe.wait_ge(tile_done, 24)
            for h in range(H):
                pe.wait_ge(gu_ready, h + 1)
                pe.matmul(ps[:, h], ones[:], as_m[:, h % 2], start=True, stop=True).then_inc(gb_done, 1)

            pe.wait_ge(qk_ready, 2 * H)
            for h in range(H):
                for w in range(4):
                    if h > 0:
                        pe.wait_ge(kk_evac, 4 * (h - 1) + w + 1)
                    elif w == 2:
                        pe.wait_ge(ri_ready, 8)
                    for c in range(4):
                        kc = chan[:, 4 + h, c * P:(c + 1) * P]
                        o = quarters(4 + w)[:, c]
                        if w == 0:
                            last = pe.matmul(o, kc, kc, start=True, stop=True)
                        elif w == 1:
                            last = pe.matmul(o, kc, chan[:, h, c * P:(c + 1) * P], start=True, stop=True)
                        elif w == 2:
                            last = pe.transpose(o, kc, ident[:])
                        else:
                            last = pe.transpose(o, chan[:, 8 + h, c * P:(c + 1) * P], ident[:])
                    last.then_inc(kk_done, 1)

            pe.wait_ge(decay_ready, 3 * H)
            for h in range(H):
                pe.wait_ge(x1_ready, h + 1)
                for c in range(4):
                    last = pe.transpose(quarters(h)[:, c], quart(x_m[:, h])[:, c], ident[:])
                last.then_inc(x1t_done, 1)

            def level_q(i):
                h = i % 4
                pe.wait_ge(as_ready, 4 + i + 1)
                if i < 4:
                    pe.wait_ge(y1_ready, 4)
                else:
                    pe.wait_ge(y_lev, i - 3)
                for c in range(4):
                    last = pe.matmul(quarters(3 * (i % 2))[:, c], quart(as_m[:, i % 2])[:, c], quart(y_m[:, h])[:, c], start=True, stop=True)
                last.then_inc(qm_done, 1)

            def level_p(i):
                h = i % 4
                pe.wait_ge(qm_ready, i + 1)
                if i >= 2:
                    pe.wait_ge(y_lev, i - 1)
                    pe.wait_ge(x_lev, min(i - 1, 20))
                for c in range(4):
                    qc, xc = quart(q_m[:, i % 2])[:, c], quart(x_m[:, h])[:, c]
                    last = pe.matmul(quarters(3 * (i % 2) + 1)[:, c], xc, qc, start=True, stop=True)
                    if i < 20:
                        last = pe.matmul(quarters(3 * (i % 2) + 2)[:, c], qc, xc, start=True, stop=True)
                last.then_inc(p_done, 1)

            for i in range(25):
                if i < 24:
                    level_q(i)
                if i >= 1:
                    level_p(i - 1)

            for h in range(H):
                pe.wait_ge(y_lev, 20 + h + 1)
                if h >= 2:
                    pe.wait_ge(wt_ready, h - 1)
                for c in range(4):
                    last = pe.matmul(quarters(6 + h % 2)[:, c], quart(chan[:, 4 + h])[:, c], quart(y_m[:, h])[:, c], start=True, stop=True)
                last.then_inc(wt_done, 1)
            pe.wait_ge(wt_ready, 4)

            for c in range(NT):
                for h in range(H):
                    i = 4 * c + h
                    if i >= 2:
                        pe.wait_ge(vn_ready, i - 1)
                    if c > 0:
                        pe.wait_ge(s_ready, 4 * (c - 1) + h + 1)
                    o = ps[:, h % 2, 0:P]
                    last = pe.matmul(o, quart(y_m[:, h])[:, c], quart(chan[:, 8 + h])[:, c], start=True, stop=(c == 0))
                    if c > 0:
                        last = pe.matmul(o, quart(chan[:, 4 + h])[:, c], state[:, h * P:(h + 1) * P], start=False, stop=True)
                    last.then_inc(vn_done, 1)
                for h in range(H):
                    i = 4 * c + h
                    vn = vnew[:, h * P:(h + 1) * P]
                    pe.wait_ge(vn_ready, i + 1)
                    o = quarters(4 + h)[:, c]
                    if c > 0:
                        pe.matmul(o, state[:, h * P:(h + 1) * P], quart(chan[:, h])[:, c], start=True, stop=False)
                    pe.matmul(o, vn, quart(qkt[:, h])[:, c], start=(c == 0), stop=True).then_inc(o_done, 1)
                    if c < NT - 1:
                        if i >= 2:
                            pe.wait_ge(s_ready, i - 1)
                        pe.matmul(ps[:, 2 + h % 2, 0:P], quart(kdec[:, h])[:, c], vn, start=True, stop=True).then_inc(s_done, 1)
            def by_tokens(f, banks, done):
                tp, n, kp, final = pair_of(f)
                order = OUT_ORDER if f < F_CQ else CO_ORDER
                first = order.index((tp, n, kp)) == min(i for i, o in enumerate(order) if o[:2] == (tp, n))
                rows = (6, 4, 0, 2)[kp] if f < F_CQ else 2 * kp
                pe.wait_ge(wfl_ready, f + 1)
                for b in range(2):
                    ts = slice((2 * tp + b) * P, (2 * tp + b + 1) * P)
                    for kk in range(2):
                        for a, w in ((act_hi, 0), (act_hi, 1), (act_lo, 0)):
                            last = pe.matmul(ps[:, banks[b]], a[:, rows + kk, ts], parts_of(f, w)[:, kk],
                                             start=(first and kk == 0 and a is act_hi and w == 0),
                                             stop=(final and kk == 1 and a is act_lo))
                    if final:
                        last.then_inc(done, 1)
                if not final:
                    last.then_inc(wf_used, 1)

            def mixer_out(i):
                tp, n = OUT_ORDER[i][:2]
                by_tokens(F_OUT + i, OUT_BANKS[tp, n], out_mm)

            for h in range(H):
                pe.wait_ge(osq_ready, h + 1)
                if h >= 2:
                    pe.wait_ge(orms_ready, h - 1)
                pe.matmul(ps[:, h % 2], ones[:], onrm(h), start=True, stop=True).then_inc(oss_done, 1)
                if h == 1:
                    pe.wait_ge(s_ready, 4 * (NT - 1))
                    pe.wait_ge(al_ready, A_RG)
                    mixer_out(0)
                if h == 2:
                    mixer_out(1)
            pe.wait_ge(orms_ready, H)
            for i in range(2, 4 * HALF):
                if i == 4:
                    pe.wait_ge(al_ready, A_DN)
                    pe.wait_ge(onorm_ready, H)
                mixer_out(i)

            pe.wait_ge(h1_ready, 8)
            for m in range(MT):
                transposes(NT + m)
            mem_t = chan[:, 4:8, :].rearrange("p a t -> p (a t)").rearrange("p (k m) -> p k m", k=KT)
            pe.wait_ge(tr_evac, 2 * (NT + MT))
            pe.wait_ge(w_in_slot[2 * SLOT[W_CK]], 16 * FILL[W_CK])
            pe.wait_ge(w_in_slot[2 * SLOT[W_CK] + 1], 16 * FILL[W_CK])
            for i in range(8):
                if i >= 4:
                    pe.wait_ge(mk_evac, i - 3)
                for k in range(KT):
                    last = pe.matmul(ps[:, i % 4, 0:M], slot_w(W_CK, k)[:, i * P:(i + 1) * P], mem_t[:, k], start=(k == 0), stop=(k == KT - 1))
                last.then_inc(mk_mm, 1)
            pe.wait_ge(w_in_slot[2 * SLOT[W_CV]], 16 * FILL[W_CV])
            pe.wait_ge(w_in_slot[2 * SLOT[W_CV] + 1], 16 * FILL[W_CV])
            for i in range(4):
                if i in (0, 2):
                    transposes(NT + MT + i)
                    transposes(NT + MT + i + 1)
                pe.wait_ge(mk_evac, i + 5)
                for k in range(KT):
                    last = pe.matmul(ps[:, i % 4], mem_t[:, k, (i // 2) * P:(i // 2 + 1) * P], slot_w(W_CV, k)[:, (i % 2) * 512:(i % 2 + 1) * 512],
                                     start=(k == 0), stop=(k == KT - 1))
                last.then_inc(mk_mm, 1)

            s = 2 * NT + MT
            pe.wait_ge(al_ready, A_H1)
            for i in range(8):
                pe.wait_ge(mk_evac, 9 + i) if i < 4 else pe.wait_ge(q_evac, i - 3)
                pe.wait_ge(wfl_ready, F_CQ + i + 1)
                by_channels(F_CQ + i, ps[:, i % 4]).then_inc(wf_used, 1)

            kt_m = extra[:, 0:4, :].rearrange("p a t -> p (a t)").rearrange("p (i m) -> p i m", i=8)
            v_m = extra[:, 4:8, :].rearrange("p a t -> p (a t)").rearrange("p (m d) -> p m d", m=MT)
            pe.wait_ge(q_evac, 8)

            def prob_transposes(t):
                pe.wait_ge(p_ready, t + 1)
                for b in range(2):
                    if t >= 1:
                        pe.wait_ge(pt_evac, 2 * (t - 1) + b + 1)
                    for i in range(4):
                        c = 4 * b + i
                        last = pe.transpose(quarters(4 + b)[:, i], xn[:, t % 2, c * P:(c + 1) * P], ident[:])
                    last.then_inc(pt_mm, 1)

            for t in range(NT):
                if t >= 2:
                    pe.wait_ge(ex_ready, 4 * (t - 1))
                for h in range(XH):
                    o = ps[:, 2 * (t % 2) + h // 2, (h % 2) * M:(h % 2 + 1) * M]
                    for k in range(2):
                        last = pe.matmul(o, chan[:, 2 * h + k, t * P:(t + 1) * P], kt_m[:, 2 * h + k], start=(k == 0), stop=(k == 1))
                last.then_inc(sc_mm, 1)
                if t >= 1:
                    prob_transposes(t - 1)
            prob_transposes(NT - 1)
            pe.wait_ge(pt_evac, 2 * NT)
            for i in range(8):
                if i >= 2:
                    pe.wait_ge(al_ready, A_H1 + i - 1)
                for m in range(2):
                    last = pe.matmul(ps[:, 6 + i % 2], v_m[:, m, i * P:(i + 1) * P], chan[:, 8 + 2 * (i // 2) + m], start=(m == 0), stop=(m == 1))
                last.then_inc(o_mm, 1)
            pe.wait_ge(al_ready, A_H1 + KT)
            for g in range(0, 8, 2):
                if g >= 4:
                    pe.wait_ge(h2_ready, g - 2)
                for kp in range(HALF):
                    by_tokens(F_CO + HALF * (g // 2) + kp, (g % 4, g % 4 + 1), co_mm)
                if g == 4:
                    transposes(s)
                    transposes(s + 1)

            for t in range(NT):
                if t < 2:
                    transposes(s + 2)
                s += 1
                pe.wait_ge(tr_evac, 2 * s)
                pe.wait_ge(h2_ready, 5)
                for k in range(KT):
                    last = pe.matmul(ps[:, 0, t * E:(t + 1) * E], chan[:, k, t * P:(t + 1) * P], w_rt[:, k], start=(k == 0), stop=(k == KT - 1))
                last.then_inc(lg_mm, 1)
            pe.wait_ge(oh_ready, 1)
            mask = extra[:, 3, 0:NT * E].rearrange("p (t e) -> p t e", t=NT)
            pe.matmul(ps[:, 1, 0:NT * E], extra[:, 2, 0:P], extra[:, 3, 0:NT * E], start=True, stop=False)
            for u in range(1, NT):
                pe.matmul(ps[:, 1, u * E:NT * E], ones[:], extra[:, 3, 0:(NT - u) * E], start=False, stop=(u == NT - 1))
            for t in range(NT):
                last = pe.matmul(ps[:, 2, 0:E], ones[:], mask[:, t], start=(t == 0), stop=(t == NT - 1))
            last.then_inc(pos_mm, 1)

            def gathered_transposes():
                xgk = xg[:].rearrange("t (h p k) -> t h k p", h=2, k=HALF)
                for b in range(2):
                    for k in range(4):
                        last = pe.transpose(quarters(6 + b)[:, k], xgk[:, b, k], ident[:])
                last.then_inc(xgt_done, 1)

            for j in range(NT * TOPK):
                if j < N_POOL:
                    pe.wait_ge(ohp_ready, j + 1)
                pe.wait_ge(ohb_ready, j + 1)
                last = pe.matmul(ps[:, 3, 0:E * CAP], oh_pos[:, j], oh_blk[:, j], start=(j == 0), stop=(j == NT * TOPK - 1))
            last.then_inc(tab_mm, 1)
            pe.wait_ge(tab_step, 2)
            pe.matmul(ps[0:1, 4, 0:N_MORE], extra[:, 7, 484:485], ident[:, 0:N_MORE], start=True, stop=True).then_inc(tab_mm, 1)
            pe.wait_ge(xg_in, 16)
            gathered_transposes()
            pe.wait_ge(codes_ready, 1)
            n_blocks = pe.value_load(nblocks[0:1, 0:1], min_val=E, max_val=MAXB - 3)
            d0, d1 = 2 * ((GM + 2) % 3), 2 * ((GM + 2) % 3) + 1
            with pe.Fori(0, n_blocks) as n:
                pe.wait_ge(bias3_in, n * 16 + 16)
                pe.wait_ge(xlo_ready, n + 1)
                for j in range(2):
                    for i in range(2):
                        pe.matmul(ps[:, 2 * j + i], ones3[:], bias3[:, j * D + i * 512:j * D + (i + 1) * 512], start=True, stop=False)
                    for k in range(KT):
                        c = KT * j + k
                        pe.wait_ge(lo_ready, n * SPLIT + (c + 1))
                        ks = slice(k * P, (k + 1) * P)
                        for xp, part in ((x_hi, 0), (x_hi, 1), (x_lo, 0)):
                            for i in range(2):
                                last = pe.matmul(ps[:, 2 * j + i], xp[:, ks], wsp[:, c % NSPLIT, part, i * 512:(i + 1) * 512],
                                                 start=False, stop=(k == KT - 1 and xp is x_lo))
                        last.then_inc(split_used, 1)
                pe.wait_ge(xg_in, n * 16 + 32)
                gathered_transposes()
                for i in range(2):
                    last = pe.matmul(ps[:, 4 + i], ones3[:], bias3[:, 2 * D + i * 512:2 * D + (i + 1) * 512], start=True, stop=False)
                last.then_inc(bias3_used, 1)
                hk = hid[:].rearrange("t (h p k) -> t h k p", h=2, k=HALF)
                for b in range(2):
                    pe.wait_ge(hid_ready, n * 2 + (b + 1))
                    for k in range(4):
                        last = pe.transpose(quarters(b)[:, k], hk[:, b, k], ident[:])
                    last.then_inc(hidt_done, 1)
                pe.wait_ge(w_in_slot[d0], n * 16 + (base[d0 // 2] + 16))
                pe.wait_ge(hidt_ready, n + 1)
                for k in range(HALF):
                    for i in range(2):
                        last = pe.matmul(ps[:, 4 + i], hid_t[:, k * P:(k + 1) * P],
                                         ring[:, d0 // 2, k, i * 512:(i + 1) * 512], start=False, stop=False)
                last.then_inc(down_half, 1)
                pe.wait_ge(hidlo_ready, n + 1)
                for k in range(HALF):
                    c = GU + k
                    pe.wait_ge(lo_ready, n * SPLIT + (c + 1))
                    for xp, part in ((hid_hi, 0), (hid_hi, 1), (hid_lo, 0)):
                        for i in range(2):
                            last = pe.matmul(ps[:, 4 + i], xp[:, k * P:(k + 1) * P], wsp[:, c % NSPLIT, part, i * 512:(i + 1) * 512],
                                             start=False, stop=(k == HALF - 1 and xp is hid_lo))
                            if k == HALF - 1 and xp is hid_lo and i == 0:
                                last.then_inc(down_done, 1)
                    last.then_inc(split_used, 1)

        @block.vector
        def _(dve):
            chain = [0]

            def link(ins):
                chain[0] += 1
                ins.then_inc(dve_c, 1)
                dve.wait_ge(dve_c, chain[0])

            dve.memset(par_rows[:], 0.0).then_inc(par_clear, 1)
            dve.memset(eps_t, EPS).then_inc(par_clear, 1)

            def recip_rms(s):
                dve.wait_ge(stat_ready, s + 1)
                dve.reciprocal(rstd[:, s:s + 1], rms[:, s:s + 1]).then_inc(rstd_ready, 1)

            def evac_t(s, gain, dst):
                for b in range(2):
                    dve.wait_ge(tr_done, 2 * s + b + 1)
                    g = par[:, gain + 4 * b:gain + 4 * b + 4].unsqueeze(2).to_broadcast([P, 4, P])
                    dve.tensor_tensor(dst(b), quarters(2 * (s % 2) + 4 + b), g, ALU.mult).then_inc(tr_evac, 1)

            dve.wait_ge(par_t, 1)
            dve.tensor_copy(par[:], ps[:, 7, 0:P]).then_inc(par_ready, 1)
            dve.wait_ge(par_ready, 1)
            def piece_lo(f):
                dve.wait_ge(wfh_ready, f + 1)
                dve.tensor_tensor(parts_of(f, 1), piece(f), parts_of(f, 0), ALU.subtract).then_inc(wfl_ready, 1)

            def normed_lo(t, count, src):
                dve.wait_ge(ah_ready, count)
                ts = slice(t * P, (t + 1) * P)
                dve.tensor_tensor(act_lo[:, :, ts], src[:, :, ts], act_hi[:, :, ts], ALU.subtract).then_inc(al_ready, 1)

            for t in range(NT + 1):
                if t < NT:
                    recip_rms(t)
                if t >= 1:
                    evac_t(t - 1, R_MIX, lambda b: chan[:, 4 * b:4 * b + 4, (t - 1) * P:t * P])
                if t >= 2:
                    normed_lo(t - 2, t - 1, chan[:, 0:8])
            normed_lo(3, NT, chan[:, 0:8])
            piece_lo(0)
            piece_lo(1)

            bt = ps[:, 7, 0:32].rearrange("p (c w) -> p w c", c=4)
            dve.wait_ge(ba_done, 1)
            dve.wait_ge(small_in, 16 * 5)
            v3 = lambda a: a.rearrange("p (h c) -> p h c", h=4)
            dve.tensor_copy(v3(beta), bt[:, 0:4])
            dve.tensor_tensor(v3(sp_in[:, 0:16]), bt[:, 4:8], dtb.unsqueeze(2).to_broadcast([P, 4, 4]), ALU.add)
            link(dve.tensor_scalar(sp_in[:, 16:20], par[:, R_LAM:R_LAM + 4], -1.0, None, ALU.mult))
            dve.scalar_tensor_tensor(out=sp_s, in0=sp_in, scalar=-1.0, in1=sp_in, op0=ALU.mult, op1=ALU.max).then_inc(sp_ready, 1)
            dve.wait_ge(exp_small, 1)
            link(dve.tensor_scalar(sp_s, sp_e, 2.0, None, ALU.add))
            link(dve.reciprocal(sp_s, sp_s))
            link(dve.tensor_tensor(sp_s, sp_s, sp_e, ALU.mult))
            link(dve.tensor_tensor(sp_s2, sp_s, sp_s, ALU.mult))
            link(dve.tensor_scalar(sp_e, sp_s2, 1.0 / 17, None, ALU.mult))
            for d in (15, 13, 11, 9, 7, 5, 3):
                link(dve.scalar_tensor_tensor(out=sp_e, in0=sp_e, scalar=1.0 / d, in1=sp_s2, op0=ALU.add, op1=ALU.mult))
            link(dve.scalar_tensor_tensor(out=sp_e, in0=sp_e, scalar=1.0, in1=sp_s, op0=ALU.add, op1=ALU.mult))
            link(dve.tensor_scalar(sp_e, sp_e, 2.0, None, ALU.mult))
            link(dve.scalar_tensor_tensor(out=sp_e, in0=sp_in, scalar=0.0, in1=sp_e, op0=ALU.max, op1=ALU.add))
            link(dve.tensor_scalar(rate, sp_e[:, 16:20], -8.0, None, ALU.mult))
            link(dve.tensor_scalar(nrate, sp_e[:, 16:20], 8.0, None, ALU.mult))
            dve.wait_ge(exp_small, 2)
            dve.scalar_tensor_tensor(out=v3(g_t), in0=v3(sp_e[:, 0:16]), scalar=-1.0, in1=alog.unsqueeze(2).to_broadcast([P, 4, 4]),
                                     op0=ALU.mult, op1=ALU.mult).then_inc(g_ready, 1)
            dve.memset(sp_in[:, 0:1], P * EPS).then_inc(sp_ready, 1)

            for j in range(24):
                if j + 2 < F_POOL:
                    piece_lo(j + 2)
                if j < 12 or 16 <= j < 20:
                    nj, r, jj = (12, R_DCONV, j) if j < 12 else (4, R_RCONV, j - 16)
                    dve.wait_ge(tap_ready, (j if j < 12 else j - 4) + 1)
                    for d in (1, 2, 3):
                        w = par[:, r + (3 - d) * nj + jj:][:, 0:1]
                        ins = dve.scalar_tensor_tensor(out=chan[:, j, d:], in0=ps[:, j % 6, 0:T - d], scalar=w,
                                                       in1=chan[:, j, d:], op0=ALU.mult, op1=ALU.add)
                        if d < 3:
                            link(ins)
                        else:
                            ins.then_inc(tile_done, 1)
                elif j < 16:
                    dve.wait_ge(sig_ready, j + 1)
                    dve.tensor_tensor(chan[:, j], ps[:, j % 6], extra[:, 4 + j % 2], ALU.mult).then_inc(tile_done, 1)
                else:
                    tb = extra[:, 6 + j % 2]
                    dve.wait_ge(y2_ready, j - 19)
                    link(dve.tensor_scalar(tb, tb, 0.044715, 1.0, ALU.mult, ALU.add))
                    dve.tensor_tensor(tb, tb, ps[:, j % 6], ALU.mult).then_inc(yt_ready, 1)
                    dve.wait_ge(tanh_ready, j - 19)
                    dve.scalar_tensor_tensor(out=chan[:, j], in0=tb, scalar=1.0, in1=ps[:, j % 6], op0=ALU.add, op1=ALU.mult).then_inc(tile_done, 1)
                if j == 2:
                    dve.wait_ge(gp_done, 1)
                    dve.tensor_copy(gp, ps[:, 7, 64:80]).then_inc(gp_ready, 1)
                if 11 <= j < 19:
                    i = j - 11
                    dve.wait_ge(norm_ready, i // 4 + 1)
                    link(dve.reciprocal(chan[:, 16 + i], chan[:, 16 + i]))
                    dve.tensor_tensor(chan[:, i], chan[:, i], chan[:, 16 + i], ALU.mult).then_inc(qk_ready, 1)

            for h in range(H):
                dve.wait_ge(proj_done, 24)
                if h >= 2:
                    dve.wait_ge(gb_done, h - 1)
                dve.tensor_tensor(quart(as_m[:, h % 2]), tri[:].unsqueeze(1).to_broadcast([P, 4, P]),
                                  g_t[:, 4 * h:4 * h + 4].unsqueeze(2).to_broadcast([P, 4, P]), ALU.mult).then_inc(gu_ready, 1)
            for h in range(H):
                dve.wait_ge(gb_done, h + 1)
                dve.wait_ge(gp_ready, 1)
                g4 = gp[:, 4 * h:4 * h + 4].unsqueeze(2)
                link(dve.tensor_tensor(quart(a_m[:, h]), quarters(h), g4.to_broadcast([P, 4, P]), ALU.subtract))
                dve.tensor_tensor(kdf[:, 4 * h:4 * h + 4].unsqueeze(2), quarters(h)[:, :, P - 1:P], g4, ALU.subtract).then_inc(kd_in, 1)
                dve.tensor_scalar(qkt[:, h], a_m[:, h], 0.0, None, ALU.min)
                dve.tensor_scalar(a_m[:, h], a_m[:, h], 0.0, None, ALU.max).then_inc(split_ready, 1)

            dve.wait_ge(beta_ready, 1)
            dve.wait_ge(kdf_ready, 2)
            link(dve.tensor_tensor(beg, beta, egp, ALU.mult))
            for h in range(H):
                bc = lambda a: a[:, 4 * h:4 * h + 4].unsqueeze(2).to_broadcast([P, 4, P])
                dve.wait_ge(kk_done, 4 * h + 1)
                dve.wait_ge(masked_ready, 2 * h + 1)
                for c in range(4):
                    ins = dve.scalar_tensor_tensor(out=quart(a_m[:, h])[:, c], in0=quarters(4)[:, c], scalar=beta[:, 4 * h + c:4 * h + c + 1],
                                                   in1=quart(a_m[:, h])[:, c], op0=ALU.mult, op1=ALU.mult)
                ins.then_inc(kk_evac, 1)
                dve.wait_ge(kk_done, 4 * h + 2)
                dve.wait_ge(masked_ready, 2 * h + 2)
                dve.tensor_tensor(quart(qkt[:, h]), quarters(5), quart(qkt[:, h]), ALU.mult).then_inc(kk_evac, 1)
                dve.wait_ge(kk_done, 4 * h + 3)
                dve.tensor_tensor(quart(chan[:, 4 + h]), quarters(6), bc(beg), ALU.mult)
                dve.tensor_tensor(quart(kdec[:, h]), quarters(6), bc(kdf), ALU.mult).then_inc(kk_evac, 1)
                dve.wait_ge(kk_done, 4 * h + 4)
                dve.tensor_tensor(quart(chan[:, 8 + h]), quarters(7), bc(beta), ALU.mult).then_inc(kk_evac, 1)

            for h in range(H):
                dve.wait_ge(as_ready, h + 1)
                dve.tensor_tensor(quart(x_m[:, h]), ident[:].unsqueeze(1).to_broadcast([P, 4, P]), quart(as_m[:, h % 2]), ALU.subtract).then_inc(x1_ready, 1)
            for i in range(24):
                h = i % 4
                dve.wait_ge(p_done, i + 1)
                dve.wait_ge(y1_ready, 4)
                dve.tensor_tensor(y_m[:, h], y_m[:, h], ps[:, 3 * (i % 2) + 1], ALU.subtract).then_inc(y_lev, 1)
                if i < 20:
                    dve.tensor_tensor(x_m[:, h], x_m[:, h], ps[:, 3 * (i % 2) + 2], ALU.subtract).then_inc(x_lev, 1)
                if i < 12:
                    n = i // 3
                    den = xn_flat[:, n % 2 * 512:(n % 2 + 1) * 512]
                    if i % 3 == 0:
                        dve.wait_ge(rt_ready, 8)
                        dve.wait_ge(gate_mm, 8)
                        link(dve.tensor_scalar(den, act_t[:, 4 + n], 1.0, None, ALU.add))
                    if i % 3 < 2:
                        half = slice(i % 3 * 256, (i % 3 + 1) * 256)
                        link(dve.reciprocal(den[:, half], den[:, half]))
                    else:
                        dve.tensor_tensor(act_t[:, 4 + n], act_t[:, 4 + n], den, ALU.mult).then_inc(mult_in, 1)
                else:
                    n = i // 3 - 4
                    if i % 3 == 0:
                        dve.wait_ge(mult_ready, n + 1)
                        link(dve.memset(act_t[:, 4 + n, 0:1], 1.0))
                        link(dve.tensor_tensor(chan[:, 16 + n], chan[:, 16 + n], act_t[:, 4 + n], ALU.mult))
                    elif i % 3 == 1:
                        link(dve.tensor_tensor_scan(act_t[:, 4 + n], act_t[:, n], chan[:, 16 + n], 0.0, ALU.mult, ALU.add))
                    else:
                        dve.scalar_tensor_tensor(out=chan[:, 20 + n], in0=act_t[:, 4 + n], scalar=0.5, in1=chan[:, 20 + n], op0=ALU.mult, op1=ALU.mult).then_inc(rg_done, 1)

            for c in range(NT - 1):
                for h in range(H):
                    i = 4 * c + h
                    st = state[:, h * P:(h + 1) * P]
                    dve.wait_ge(s_done, i + 1)
                    if c == 0:
                        dve.tensor_copy(st, ps[:, 2 + h % 2, 0:P]).then_inc(s_ready, 1)
                    else:
                        dve.wait_ge(o_done, i + 1)
                        dve.wait_ge(s_ready, i - 3)
                        dve.scalar_tensor_tensor(out=st, in0=st, scalar=elast[:, 4 * h + c:4 * h + c + 1], in1=ps[:, 2 + h % 2, 0:P],
                                                 op0=ALU.mult, op1=ALU.add).then_inc(s_ready, 1)
                if c > 0:
                    piece_lo(F_OUT + c - 1)
            dve.wait_ge(s_done, 4 * (NT - 1))
            dve.wait_ge(ah_ready, A_RG)
            dve.tensor_tensor(act_lo[:, 0:4], chan[:, 20:24], act_hi[:, 0:4], ALU.subtract).then_inc(al_ready, 4)
            for h in range(H):
                dve.wait_ge(orms_ready, h + 1)
                link(dve.reciprocal(onrm(h), onrm(h)))
                dve.tensor_tensor(onrm(h), onrm(h), ps[:, 4 + h], ALU.mult).then_inc(onorm_ready, 1)
                if h == 2:
                    piece_lo(F_OUT + 2)
                    piece_lo(F_OUT + 3)
            for h in range(H):
                dve.wait_ge(ah_ready, A_RG + h + 1)
                k = (6, 7, 4, 5)[h]
                dve.tensor_tensor(act_lo[:, k], chan[:, 12 + h], act_hi[:, k], ALU.subtract).then_inc(al_ready, 1)
                if h == 2:
                    piece_lo(F_OUT + 4)
            piece_lo(F_OUT + 5)

            def add_resid(g, done, ready, t, n, bank):
                dve.wait_ge(done, g + 1)
                r = resid[:, t, n * 512:(n + 1) * 512]
                dve.tensor_tensor(r, r, ps[:, bank], ALU.add).then_inc(ready, 1)

            s = NT
            g = 0
            for i in range(4, 4 * HALF):
                if 6 <= i:
                    piece_lo(F_OUT + i)
                if i in (10, 12):
                    recip_rms(s + i // 2 - 5)
                tp, n, kp, final = pair_of(F_OUT + i - 1)
                if i > 4 and final:
                    for b in range(2):
                        add_resid(g, out_mm, h1_ready, 2 * tp + b, n, OUT_BANKS[tp, n][b])
                        g += 1
            for b in range(2):
                add_resid(g + b, out_mm, h1_ready, 2 + b, 1, OUT_BANKS[1, 1][b])
            mem_t = chan[:, 4:8, :].rearrange("p a t -> p (a t)").rearrange("p (k m) -> p k m", k=KT)
            for m in range(MT):
                evac_t(s + m, R_MEM, lambda b: mem_t[:, 4 * b:4 * b + 4, m * P:(m + 1) * P])
            s += MT

            for t0 in (0, 2):
                for t in (t0, t0 + 1):
                    recip_rms(s + t)
                for t in (t0, t0 + 1):
                    evac_t(s + t, R_CROSS, lambda b: chan[:, 16 + 4 * b:20 + 4 * b, t * P:(t + 1) * P])
                if t0 == 2:
                    piece_lo(F_CQ)
                    piece_lo(F_CQ + 1)
                for t in (t0, t0 + 1):
                    normed_lo(t, A_DN + t + 1, chan[:, 16:24])
            for i in range(8):
                piece_lo(F_CQ + i + 2)
            s += NT
            for t in range(NT):
                o = 4 * (t % 2)
                scv = ps[:, 2 * (t % 2):2 * (t % 2) + 2, :].rearrange("p b (g m) -> p (b g) m", g=2)
                dve.wait_ge(sc_mm, t + 1)
                link(dve.tensor_reduce(mx[:, o:o + 4], scv, AX_X, ALU.max))
                dve.tensor_scalar(nmx[:, o:o + 4], mx[:, o:o + 4], -(XD ** -0.5), None, ALU.mult).then_inc(mx_ready, 1)
                dve.wait_ge(ex_ready, 4 * t + 4)
                link(dve.reciprocal(rinv[:, o:o + 4], rsum[:, o:o + 4]))
                pr = xn[:, t % 2].rearrange("p (h m) -> p h m", h=XH)
                dve.tensor_tensor(pr, pr, rinv[:, o:o + 4].unsqueeze(2).to_broadcast([P, 4, M]), ALU.mult).then_inc(p_ready, 1)
            for i in range(8):
                dve.wait_ge(ah_ready, A_H1 + i + 1)
                dve.tensor_tensor(act_lo[:, i], ps[:, 6 + i % 2], act_hi[:, i], ALU.subtract).then_inc(al_ready, 1)

            def evac_h2(t):
                evac_t(s + t, R_MOE, lambda b: chan[:, 4 * b:4 * b + 4, t * P:(t + 1) * P])

            for c in range(N_CO):
                if c < N_CO - 2:
                    piece_lo(F_CO + c + 2)
                if c % HALF == HALF - 1:
                    q = c // HALF
                    for b in range(2):
                        add_resid(2 * q + b, co_mm, h2_ready, 2 * (q // 2) + b, q % 2, (2 * q + b) % 4)
                if c in (8, 10):
                    recip_rms(s + c // 2 - 4)
                if c in (13, 14):
                    evac_h2(c - 13)
            for t in (2, 3):
                recip_rms(s + t)
            for t in (2, 3):
                evac_h2(t)
            s += NT

            def lo(c, count):
                dve.wait_ge(hi_ready, count)
                k = c % KT if c < GU else HALF + c - GU
                dve.tensor_tensor(wsp[:, c % NSPLIT, 1], ring[:, (GM + c // KT) % 3, k], wsp[:, c % NSPLIT, 0], ALU.subtract).then_inc(lo_ready, 1)

            dve.wait_ge(iota_ready, 1)
            lg = extra[:, 4, 0:NT * E].rearrange("p (t e) -> p t e", t=NT)
            top = extra[:, 5, 0:64]
            topi = extra[:, 5, 64:96].bitcast(U32)
            topf = extra[:, 5, 128:160]
            for t in range(NT):
                dve.wait_ge(lg_mm, NT)
                link(dve.tensor_tensor(lg[:, t], ps[:, 0, t * E:(t + 1) * E], brt[:], ALU.add))
                link(dve.max(top[:, 8 * t:8 * t + 8], lg[:, t]))
                link(dve.max_index(topi[:, 8 * t:8 * t + 8], top[:, 8 * t:8 * t + 8], lg[:, t]))
            link(dve.tensor_copy(topf, topi))
            t4 = top[:, 0:32].rearrange("p (t k) -> p t k", t=NT)
            dve.tensor_tensor(gates[:], t4[:, :, 0:4], t4[:, :, 0:1].to_broadcast([P, NT, TOPK]), ALU.subtract).then_inc(top_ready, 1)
            ef = extra[:, 1, :]
            it_i = extra[:, 0, :].bitcast(I32)
            oh = extra[:, 6, :].rearrange("p (t k e) -> p t k e", t=NT, k=TOPK)
            tf4 = topf.rearrange("p (t k) -> p t k", t=NT)[:, :, 0:4]
            for t in range(NT):
                last = dve.tensor_tensor(oh[:, t], ef[:, 0:E].unsqueeze(1).to_broadcast([P, TOPK, E]),
                                         tf4[:, t].unsqueeze(2).to_broadcast([P, TOPK, E]), ALU.is_equal)
            link(last)
            mask = extra[:, 3, 0:NT * E].rearrange("p (t e) -> p t e", t=NT)
            for t in range(NT):
                last = dve.tensor_reduce(mask[:, t], oh[:, t].rearrange("p k e -> p e k"), AX_X, ALU.add)
            last.then_inc(oh_ready, 1)
            dve.wait_ge(gexp_ready, 1)
            link(dve.tensor_reduce(top[:, 40:44], gates[:], AX_X, ALU.add))
            link(dve.reciprocal(top[:, 40:44], top[:, 40:44]))
            link(dve.tensor_tensor(gates[:], gates[:], top[:, 40:44].unsqueeze(2).to_broadcast([P, NT, TOPK]), ALU.mult))
            for c in range(2):
                lo(c, c + 1)
            dve.wait_ge(pos_mm, 1)
            posp = extra[:, 7, 0:NT * E].rearrange("p (t e) -> p t e", t=NT)
            link(dve.tensor_tensor(posp, ps[:, 1, 0:NT * E].rearrange("p (t e) -> p t e", t=NT),
                                   ef[:, 32:64].unsqueeze(1).to_broadcast([P, NT, E]), ALU.add))
            for t in range(NT):
                last = dve.tensor_tensor(oh[:, t], oh[:, t], posp[:, t:t + 1].to_broadcast([P, TOPK, E]), ALU.mult)
            link(last)
            link(dve.tensor_reduce(topf[:, 0:16], extra[:, 6, :].rearrange("p (a e) -> p a e", e=E), AX_X, ALU.add))
            link(dve.tensor_copy(it_i[:, 256:272], topf[:, 0:16]))
            blk_f, pos_f = extra[:, 5, 160:176], extra[:, 5, 176:192]
            dve.tensor_scalar(it_i[:, 224:240], it_i[:, 256:272], 7, None, ALU.arith_shift_right)
            link(dve.tensor_scalar(it_i[:, 240:256], it_i[:, 256:272], P - 1, None, ALU.bitwise_and))
            dve.tensor_copy(extra[:, 5, 160:192], it_i[:, 224:256]).then_inc(tab_step, 1)
            dve.wait_ge(tab_step, 1)
            for j in range(NT * TOPK):
                if j >= N_POOL:
                    dve.tensor_scalar(oh_pos[:, j], ef[:, 288:416], pos_f[:, j:j + 1], None, ALU.is_equal)
                dve.tensor_scalar(oh_blk[:, j], ef[:, 288:288 + E * CAP], blk_f[:, j:j + 1], ef[:, 64 + j:65 + j], ALU.is_equal, ALU.mult).then_inc(ohb_ready, 1)
            cnt = extra[:, 7, 256:288]
            link(dve.tensor_copy(cnt, ps[:, 2, 0:E]))
            flag, rank = extra[:, 7, 288:384], extra[:, 7, 384:480]
            link(dve.tensor_tensor(flag.rearrange("p (e b) -> p e b", b=3), cnt.unsqueeze(2).to_broadcast([P, E, 3]),
                                   ef[:, 96:99].unsqueeze(1).to_broadcast([P, E, 3]), ALU.is_gt))
            link(dve.tensor_tensor_scan(rank, ones[:, 0:96], flag, 0.0, ALU.mult, ALU.add))
            dve.tensor_scalar(extra[0:1, 7, 480:481], rank[0:1, 95:96], float(E), None, ALU.add)
            link(dve.tensor_scalar(extra[0:1, 7, 481:482], rank[0:1, 95:96], float(E - 1), None, ALU.add))
            dve.tensor_copy(nblocks[:], extra[0:1, 7, 480:482])
            link(dve.tensor_tensor(rank, rank, flag, ALU.subtract))
            link(dve.tensor_tensor(flag, flag, ef[:, 128:224], ALU.mult))
            link(dve.scalar_tensor_tensor(out=rank, in0=rank, scalar=ef[:, 416:417], in1=flag, op0=ALU.is_equal, op1=ALU.mult))
            dve.tensor_reduce(extra[:, 7, 484:485], rank, AX_X, ALU.add).then_inc(tab_step, 1)
            dve.wait_ge(tab_mm, 1)
            free = extra[:, 2, P:P + E * CAP + 1]
            link(dve.tensor_scalar(free[:, 0:E * CAP], ps[:, 3, 0:E * CAP], 0.0, float(NOBODY), ALU.is_equal, ALU.mult))
            dve.memset(free[:, E * CAP:E * CAP + 1], float(NOBODY))
            link(dve.scalar_tensor_tensor(out=free[:, 0:E * CAP], in0=ps[:, 3, 0:E * CAP], scalar=-1.0, in1=free[:, 0:E * CAP], op0=ALU.add, op1=ALU.add))
            link(dve.tensor_copy(row_tab, free))
            dve.tensor_scalar(tok_tab, row_tab, 2, None, ALU.arith_shift_right).then_inc(tab_step, 1)
            dve.wait_ge(tab_mm, 2)
            dve.wait_ge(iota_ready, 1)
            link(dve.tensor_scalar(extra[0:1, 7, 486:486 + N_MORE], ps[0:1, 4, 0:N_MORE], float(E * CAP), None, ALU.add))
            link(dve.tensor_copy(codes[0:1, E:MAXB], extra[0:1, 7, 486:486 + N_MORE]))
            link(dve.tensor_scalar(experts[:], codes[:], 2, None, ALU.arith_shift_right))
            dve.tensor_scalar(experts[:], experts[:], E - 1, None, ALU.min).then_inc(codes_ready, 1)
            for c in range(2, NSPLIT):
                lo(c, c + 1)

            dve.wait_ge(codes_ready, 1)
            n_blocks = dve.value_load(nblocks[0:1, 0:1], min_val=E, max_val=MAXB - 3)

            def evac_xt():
                for b in range(2):
                    g = gain_moe[:, 4 * b:4 * b + 4].unsqueeze(2).to_broadcast([P, 4, P])
                    last = dve.tensor_tensor(quart(gt[:, 512 * b:512 * (b + 1)]), quarters(6 + b), g, ALU.mult)
                return last

            dve.wait_ge(xgt_done, 1)
            evac_xt().then_inc(xt_ready, 1)
            dve.wait_ge(xhi_ready, 1)
            dve.tensor_tensor(x_lo[:], gt[:], x_hi[:], ALU.subtract).then_inc(xlo_ready, 1)
            with dve.Fori(0, n_blocks) as n:
                for c in range(NSPLIT, 11):
                    lo(c, n * SPLIT + (c + 1))
                dve.wait_ge(split_used, n * SPLIT + KT)
                dve.tensor_scalar(gt[:], ps[:, 0:2, :].rearrange("p b f -> p (b f)"), 7.0, None, ALU.min).then_inc(gt_ready, 1)
                lo(11, n * SPLIT + 12)
                dve.wait_ge(sg_ready, n + 1)
                dve.tensor_tensor(gt[:], gt[:], sig_e[:], ALU.mult).then_inc(gs_ready, 1)
                for c in range(12, GU + 1):
                    lo(c, n * SPLIT + (c + 1))
                dve.wait_ge(split_used, n * SPLIT + GU)
                dve.wait_ge(gs_ready, n + 1)
                for i in range(2):
                    hs = slice(i * 512, (i + 1) * 512)
                    dve.tensor_scalar(up[:, hs], ps[:, 2 + i], 7.0, -7.0, ALU.min, ALU.max).then_inc(up_ready, 1)
                    dve.wait_ge(up_ready, n * 2 + (i + 1))
                    dve.scalar_tensor_tensor(out=hid[:, hs], in0=up[:, hs], scalar=1.0, in1=gt[:, hs], op0=ALU.add, op1=ALU.mult).then_inc(hid_ready, 1)
                for c in (GU + 1, GU + 2):
                    lo(c, n * SPLIT + (c + 1))
                dve.wait_ge(hidhi_ready, n + 1)
                dve.tensor_tensor(hid_lo[:], ps[:, 1], hid_hi[:], ALU.subtract).then_inc(hidlo_ready, 1)
                lo(GU + 3, n * SPLIT + SPLIT)
                dve.wait_ge(xgt_done, n + 2)
                evac_xt().then_inc(xt_ready, 1)
                dve.wait_ge(xhi_ready, n + 2)
                dve.tensor_tensor(x_lo[:], gt[:], x_hi[:], ALU.subtract).then_inc(xlo_ready, 1)
                for c in range(NSPLIT):
                    lo(c, n * SPLIT + (SPLIT + c + 1))

            yv = ring[:, :, :, :].rearrange("p a k d -> p (a k) d")
            for t in range(NT + 1):
                if t < NT:
                    dve.wait_ge(y_in[t], 16)
                    for k in range(TOPK):
                        ins = dve.scalar_tensor_tensor(out=resid[:, t], in0=yv[:, 4 * t + k], scalar=gates[:, t, k:k + 1], in1=resid[:, t],
                                                       op0=ALU.mult, op1=ALU.add)
                        ins.then_inc(comb_ready if k == TOPK - 1 else tail_c, 1)
                        if k < TOPK - 1:
                            dve.wait_ge(tail_c, 3 * t + k + 1)
                if t >= 1:
                    dve.wait_ge(stat_ready, 14 + t)
                    dve.reciprocal(rstd[:, t - 1:t], rms[:, t - 1:t]).then_inc(rstd_ready, 1)
                    dve.wait_ge(rstd_ready, 14 + t)
                    if t == 1:
                        dve.wait_ge(nf_in, 16)
                    dve.scalar_tensor_tensor(out=resid[:, t - 1], in0=resid[:, t - 1], scalar=rstd[:, t - 1:t], in1=xn[:, 0], op0=ALU.mult, op1=ALU.mult).then_inc(fin_ready, 1)


_INS = ["x", "mem", "norm_mix", "w_in", "dn_conv", "dn_a_log", "dn_dt_bias", "dn_norm", "rg_conv", "rg_conv_b",
        "rg_w_a", "rg_b_a", "rg_w_x", "rg_b_x", "rg_lambda", "w_out", "norm_cross", "norm_mem", "w_cq", "w_ckv",
        "w_co", "norm_moe", "w_router", "b_router", "w_gate", "b_gate", "w_up", "b_up", "w_down", "b_down",
        "norm_final"]


def kernel(**inputs):
    import numpy as _np
    import concourse.bacc as _bacc
    from concourse import mybir as _mybir
    from concourse.bass_utils import run_bass_kernel_spmd as _run

    nc = _bacc.Bacc("TRN2", target_bir_lowering=False, num_devices=1)
    arrays, args = {}, []
    for name in _INS:
        a = _np.ascontiguousarray(inputs[name])
        arrays[f"in_{name}_dram"] = a
        args.append(nc.dram_tensor(f"in_{name}_dram", a.shape, _mybir.dt.from_np(a.dtype), kind="ExternalInput").ap())
    shape = inputs["x"].shape
    args.append(nc.dram_tensor("out_0_dram", shape, _mybir.dt.float32, kind="ExternalOutput").ap())
    build_layer(nc, *args)
    r = _run(nc, [arrays], core_ids=[0])
    return r.results[0]["out_0_dram"]
```
